# Optimizing a Trainium2 kernel written in Bass

```python
import jax, jax.numpy as jnp
from jax import lax
import numpy as np

D_MODEL = 1024
BATCH = 1
SEQ = 256
DEPTH = 1

CHUNK = 64
SSM_INNER = 1024
SSM_HEAD_DIM = 64
SSM_HEADS = SSM_INNER // SSM_HEAD_DIM
SSM_GROUPS = 2
SSM_STATE = 128
SSM_CONV = 4
SSM_CONV_DIM = SSM_INNER + 2 * SSM_GROUPS * SSM_STATE
LRU_WIDTH = 1024
LRU_BLOCKS = 16
LRU_BLOCK = LRU_WIDTH // LRU_BLOCKS
LRU_CONV = 4
LRU_C = 8.0
FFN_DIM = 3072
FFN_CONV = 3
N_BRANCHES = 2
RMS_EPS = 1e-6
IN_SPLITS = (
    SSM_INNER,
    SSM_INNER + SSM_CONV_DIM,
    SSM_INNER + SSM_CONV_DIM + SSM_HEADS,
    SSM_INNER + SSM_CONV_DIM + SSM_HEADS + LRU_WIDTH,
    SSM_INNER + SSM_CONV_DIM + SSM_HEADS + 2 * LRU_WIDTH,
)
N_IN = SSM_INNER + SSM_CONV_DIM + SSM_HEADS + 2 * LRU_WIDTH + N_BRANCHES * D_MODEL


def rmsnorm(x, w):
    xf = x.astype(jnp.float32)
    y = xf * lax.rsqrt(jnp.mean(xf * xf, axis=-1, keepdims=True) + RMS_EPS)
    return (y * w.astype(jnp.float32)).astype(x.dtype)

def causal_dwconv(x, w, b):
    k = w.shape[0]
    out = lax.conv_general_dilated(
        x, w[:, None, :].astype(x.dtype), window_strides=(1,), padding=[(k - 1, 0)],
        dimension_numbers=("NWC", "WIO", "NWC"), feature_group_count=x.shape[-1])
    return out + b

def ssd_chunked(xh, dt, a, bm, cm):
    b, s = xh.shape[:2]
    c = s // CHUNK
    e = SSM_HEADS // SSM_GROUPS
    x = xh.reshape(b, c, CHUNK, SSM_GROUPS, e, SSM_HEAD_DIM)
    dtc = dt.reshape(b, c, CHUNK, SSM_GROUPS, e)
    bc = bm.reshape(b, c, CHUNK, SSM_GROUPS, SSM_STATE)
    cc = cm.reshape(b, c, CHUNK, SSM_GROUPS, SSM_STATE)
    a_dt = (dtc * a.reshape(SSM_GROUPS, e)).transpose(0, 3, 4, 1, 2)
    a_cs = jnp.cumsum(a_dt, axis=-1)
    xdt = x * dtc[..., None]
    causal = jnp.tril(jnp.ones((CHUNK, CHUNK), dtype=bool))
    seg = a_cs[..., :, None] - a_cs[..., None, :]
    decay = jnp.exp(jnp.where(causal, seg, -jnp.inf))
    cb = jnp.einsum("bclgn,bcsgn->bgcls", cc, bc)
    y_diag = jnp.einsum("bgcls,bgecls,bcsgep->bclgep", cb, decay, xdt)
    decay_states = jnp.exp(a_cs[..., -1:] - a_cs)
    states = jnp.einsum("bclgn,bgecl,bclgep->cbgepn", bc, decay_states, xdt)
    chunk_decay = jnp.exp(a_cs[..., -1]).transpose(3, 0, 1, 2)

    def step(h, inp):
        st, dec = inp
        return h * dec[..., None, None] + st, h

    h0 = jnp.zeros(states.shape[1:], states.dtype)
    _, prev = lax.scan(step, h0, (states, chunk_decay))
    y_off = jnp.einsum("bclgn,cbgepn,bgecl->bclgep", cc, prev, jnp.exp(a_cs))
    return (y_diag + y_off).reshape(b, s, SSM_HEADS, SSM_HEAD_DIM)

def ssd_mixer(u_z, u_xbc, u_dt, conv_w, conv_b, dt_bias, a_log, d_skip, norm_w):
    b, s = u_z.shape[:2]
    xbc = jax.nn.silu(causal_dwconv(u_xbc, conv_w, conv_b)).astype(jnp.float32)
    xs, bm, cm = jnp.split(xbc, [SSM_INNER, SSM_INNER + SSM_GROUPS * SSM_STATE], axis=-1)
    dt = jax.nn.softplus(u_dt.astype(jnp.float32) + dt_bias.astype(jnp.float32))
    a = -jnp.exp(a_log.astype(jnp.float32))
    xh = xs.reshape(b, s, SSM_HEADS, SSM_HEAD_DIM)
    y = ssd_chunked(xh, dt, a,
                    bm.reshape(b, s, SSM_GROUPS, SSM_STATE),
                    cm.reshape(b, s, SSM_GROUPS, SSM_STATE))
    y = y + d_skip.astype(jnp.float32)[:, None] * xh
    yg = (y.reshape(b, s, SSM_INNER) * jax.nn.silu(u_z.astype(jnp.float32)))
    yg = yg.reshape(b, s, SSM_GROUPS, SSM_INNER // SSM_GROUPS)
    yg = yg * lax.rsqrt(jnp.mean(yg * yg, axis=-1, keepdims=True) + RMS_EPS)
    yg = yg.reshape(b, s, SSM_INNER) * norm_w.astype(jnp.float32)
    return yg.astype(u_z.dtype)

def rglru_mixer(u_y, u_x, conv_w, conv_b, wr, br, wi, bi, lam):
    b, s = u_x.shape[:2]
    gate = jax.nn.gelu(u_y, approximate=True)
    xc = causal_dwconv(u_x, conv_w, conv_b)
    xb = xc.reshape(b, s, LRU_BLOCKS, LRU_BLOCK)
    r = jax.nn.sigmoid(jnp.einsum("bshi,hij->bshj", xb, wr) + br).reshape(b, s, LRU_WIDTH)
    i = jax.nn.sigmoid(jnp.einsum("bshi,hij->bshj", xb, wi) + bi).reshape(b, s, LRU_WIDTH)
    log_a = -LRU_C * r.astype(jnp.float32) * jax.nn.softplus(-lam.astype(jnp.float32))
    a = jnp.exp(log_a)
    mult = jnp.sqrt(-jnp.expm1(2.0 * log_a))
    bx = mult * i.astype(jnp.float32) * xc.astype(jnp.float32)

    def combine(lhs, rhs):
        a1, b1 = lhs
        a2, b2 = rhs
        return a1 * a2, a2 * b1 + b2

    _, h = lax.associative_scan(combine, (a, bx), axis=1)
    return (h.astype(u_x.dtype) * gate)

def first_inputs(seed: int = 0) -> dict:
    key = jax.random.key(seed)
    ks = jax.random.split(key, 32)
    L = DEPTH
    f32 = jnp.float32

    def nrm(k, shape, scale):
        return jax.random.normal(k, shape, f32) * scale

    def gain(k, shape):
        return 1.0 + 0.05 * jax.random.normal(k, shape, f32)

    dt0 = jnp.exp(jax.random.uniform(ks[8], (L, SSM_HEADS), f32, np.log(1e-3), np.log(1e-1)))
    a_c = jax.random.uniform(ks[16], (L, LRU_WIDTH), f32, 0.9, 0.999)
    a0 = a_c ** (1.0 / LRU_C)
    return {
        "x": nrm(ks[0], (BATCH, SEQ, D_MODEL), 1.0),
        "mix_pre_norm": gain(ks[1], (L, D_MODEL)),
        "mix_post_norm": gain(ks[2], (L, D_MODEL)),
        "w_in": nrm(ks[3], (L, D_MODEL, N_IN), D_MODEL ** -0.5),
        "ssm_conv_w": nrm(ks[4], (L, SSM_CONV, SSM_CONV_DIM), SSM_CONV ** -0.5),
        "ssm_conv_b": nrm(ks[5], (L, SSM_CONV_DIM), 0.02),
        "ssm_dt_bias": dt0 + jnp.log(-jnp.expm1(-dt0)),
        "ssm_a_log": jnp.log(jax.random.uniform(ks[6], (L, SSM_HEADS), f32, 1.0, 16.0)),
        "ssm_d": 1.0 + 0.1 * jax.random.normal(ks[7], (L, SSM_HEADS), f32),
        "ssm_norm": gain(ks[9], (L, SSM_INNER)),
        "w_proj_ssm": nrm(ks[10], (L, SSM_INNER, D_MODEL), SSM_INNER ** -0.5),
        "lru_conv_w": nrm(ks[11], (L, LRU_CONV, LRU_WIDTH), LRU_CONV ** -0.5),
        "lru_conv_b": nrm(ks[12], (L, LRU_WIDTH), 0.02),
        "lru_wr": nrm(ks[13], (L, LRU_BLOCKS, LRU_BLOCK, LRU_BLOCK), LRU_BLOCK ** -0.5),
        "lru_br": nrm(ks[14], (L, LRU_BLOCKS, LRU_BLOCK), 0.02),
        "lru_wi": nrm(ks[15], (L, LRU_BLOCKS, LRU_BLOCK, LRU_BLOCK), LRU_BLOCK ** -0.5),
        "lru_bi": nrm(ks[17], (L, LRU_BLOCKS, LRU_BLOCK), 0.02),
        "lru_lambda": jnp.log(a0) - jnp.log1p(-a0),
        "w_proj_lru": nrm(ks[18], (L, LRU_WIDTH, D_MODEL), LRU_WIDTH ** -0.5),
        "gate_b": nrm(ks[19], (L, N_BRANCHES, D_MODEL), 0.02),
        "w_out": nrm(ks[20], (L, D_MODEL, D_MODEL), D_MODEL ** -0.5),
        "ffn_pre_norm": gain(ks[21], (L, D_MODEL)),
        "ffn_post_norm": gain(ks[22], (L, D_MODEL)),
        "w_ffn_up": nrm(ks[23], (L, D_MODEL, 2 * FFN_DIM), D_MODEL ** -0.5),
        "ffn_conv_w": nrm(ks[24], (L, FFN_CONV, 2 * FFN_DIM), FFN_CONV ** -0.5),
        "ffn_conv_b": nrm(ks[25], (L, 2 * FFN_DIM), 0.02),
        "w_ffn_down": nrm(ks[26], (L, FFN_DIM, D_MODEL), FFN_DIM ** -0.5),
    }

def first_block(x, mix_pre_norm, mix_post_norm, w_in, ssm_conv_w, ssm_conv_b, ssm_dt_bias,
              ssm_a_log, ssm_d, ssm_norm, w_proj_ssm, lru_conv_w, lru_conv_b, lru_wr, lru_br,
              lru_wi, lru_bi, lru_lambda, w_proj_lru, gate_b, w_out, ffn_pre_norm,
              ffn_post_norm, w_ffn_up, ffn_conv_w, ffn_conv_b, w_ffn_down):
    b, s, _ = x.shape
    for l in range(DEPTH):
        h = rmsnorm(x, mix_pre_norm[l])
        u = h @ w_in[l]
        u_z, u_xbc, u_dt, u_ly, u_lx, u_g = jnp.split(u, list(IN_SPLITS), axis=-1)
        y_a = ssd_mixer(u_z, u_xbc, u_dt, ssm_conv_w[l], ssm_conv_b[l], ssm_dt_bias[l],
                        ssm_a_log[l], ssm_d[l], ssm_norm[l])
        y_b = rglru_mixer(u_ly, u_lx, lru_conv_w[l], lru_conv_b[l], lru_wr[l], lru_br[l],
                          lru_wi[l], lru_bi[l], lru_lambda[l])
        g = jax.nn.sigmoid(u_g.reshape(b, s, N_BRANCHES, D_MODEL) + gate_b[l])
        merged = g[:, :, 0, :] * (y_a @ w_proj_ssm[l]) + g[:, :, 1, :] * (y_b @ w_proj_lru[l])
        x = x + rmsnorm(merged @ w_out[l], mix_post_norm[l])
        h = rmsnorm(x, ffn_pre_norm[l])
        up = causal_dwconv(h @ w_ffn_up[l], ffn_conv_w[l], ffn_conv_b[l])
        f_gate, f_val = jnp.split(up, 2, axis=-1)
        f = (jax.nn.gelu(f_gate, approximate=True) * f_val) @ w_ffn_down[l]
        x = x + rmsnorm(f, ffn_post_norm[l])
    return x


DEPTH_2 = 2

QBLOCK = 128
HEAD_DIM = 64
EPS = 1e-6
H_FOX = 8
H_CHK = 8
N_LEFT_CHUNKS = 8
BAND = (N_LEFT_CHUNKS + 1) * CHUNK
REL_CLIP = 256
N_REL = CHUNK - 1 + REL_CLIP + 1
FORGET_BIAS = 3.0
H_SB = 8
H_MLA = 8
Q_LORA = 384
KV_LORA = 256
NOPE_DIM = 64
ROPE_DIM = 32
V_DIM = 64
ROPE_THETA = 10000.0
D_FF = 4 * D_MODEL
N_EVEN = (DEPTH_2 + 1) // 2
N_ODD = DEPTH_2 // 2

W_FOX = H_FOX * HEAD_DIM
W_CHK = H_CHK * HEAD_DIM
W_SB = H_SB * HEAD_DIM
W_MLA = H_MLA * V_DIM
SPLIT_AB = [W_FOX, W_FOX, W_FOX, H_FOX, W_CHK, W_CHK, W_CHK]
SPLIT_CD = [W_SB, W_SB, W_SB, Q_LORA, KV_LORA, ROPE_DIM]
IN_AB = sum(SPLIT_AB)
IN_CD = sum(SPLIT_CD)
MIX_AB = W_FOX + W_CHK
MIX_CD = W_SB + W_MLA


def _split(h, sizes):
    return jnp.split(h, np.cumsum(sizes)[:-1].tolist(), axis=-1)

def rmsnorm_2(x, g):
    xf = x.astype(jnp.float32)
    y = xf * lax.rsqrt(jnp.mean(xf * xf, axis=-1, keepdims=True) + EPS)
    return (y * g.astype(jnp.float32)).astype(x.dtype)

def rope(x, positions):
    half = ROPE_DIM // 2
    inv_freq = ROPE_THETA ** (-jnp.arange(half, dtype=jnp.float32) / half)
    ang = positions.astype(jnp.float32)[..., None] * inv_freq
    cos = jnp.cos(ang)[:, :, None, :]
    sin = jnp.sin(ang)[:, :, None, :]
    x1 = x[..., :half].astype(jnp.float32)
    x2 = x[..., half:].astype(jnp.float32)
    out = jnp.concatenate([x1 * cos - x2 * sin, x2 * cos + x1 * sin], axis=-1)
    return out.astype(x.dtype)

def _sweep_query_blocks(block_fn, seq):
    out = lax.map(block_fn, jnp.arange(seq // QBLOCK))
    nb, b, qb, h, dv = out.shape
    return jnp.moveaxis(out, 0, 1).reshape(b, nb * qb, h, dv)

def fox_attention(q, k, v, log_f):
    seq = q.shape[1]
    scale = HEAD_DIM ** -0.5
    cum = jnp.transpose(jnp.cumsum(log_f, axis=1), (0, 2, 1))
    k_pos = jnp.arange(seq)

    def block(i):
        start = i * QBLOCK
        qb = lax.dynamic_slice_in_dim(q, start, QBLOCK, axis=1)
        cq = lax.dynamic_slice_in_dim(cum, start, QBLOCK, axis=2)
        q_pos = start + jnp.arange(QBLOCK)
        s = jnp.einsum('bqhd,bkhd->bhqk', qb, k).astype(jnp.float32) * scale
        s = s + cq[..., :, None] - cum[..., None, :]
        mask = k_pos[None, :] <= q_pos[:, None]
        p = jax.nn.softmax(jnp.where(mask, s, -jnp.inf), axis=-1)
        return jnp.einsum('bhqk,bkhd->bqhd', p.astype(v.dtype), v)

    return _sweep_query_blocks(block, seq)

def chunked_relpos_attention(q, k, v, rel_bias):
    b, seq, h, d = q.shape
    nc = seq // CHUNK
    left = N_LEFT_CHUNKS * CHUNK
    scale = HEAD_DIM ** -0.5

    def band(t):
        tp = jnp.pad(t, ((0, 0), (left, 0), (0, 0), (0, 0)))
        tp = tp.reshape(b, nc + N_LEFT_CHUNKS, CHUNK, h, d)
        return jnp.concatenate([tp[:, i:i + nc] for i in range(N_LEFT_CHUNKS + 1)], axis=2)

    kb, vb = band(k), band(v)
    qc = q.reshape(b, nc, CHUNK, h, d)
    rel = np.arange(CHUNK)[:, None] + left - np.arange(BAND)[None, :]
    rel_idx = np.clip(rel, -(CHUNK - 1), REL_CLIP) + (CHUNK - 1)
    bias = rel_bias[:, rel_idx].astype(jnp.float32)
    s = jnp.einsum('bcqhd,bckhd->bhcqk', qc, kb).astype(jnp.float32) * scale
    s = s + bias[None, :, None]
    key_abs = jnp.arange(nc)[:, None] * CHUNK - left + jnp.arange(BAND)[None, :]
    valid = (key_abs >= 0)[None, None, :, None, :]
    p = jax.nn.softmax(jnp.where(valid, s, -jnp.inf), axis=-1)
    out = jnp.einsum('bhcqk,bckhd->bcqhd', p.astype(v.dtype), vb)
    return out.reshape(b, seq, h, d)

def stick_breaking_attention(q, k, v):
    seq = q.shape[1]
    scale = HEAD_DIM ** -0.5
    k_pos = jnp.arange(seq)

    def block(i):
        start = i * QBLOCK
        qb = lax.dynamic_slice_in_dim(q, start, QBLOCK, axis=1)
        q_pos = start + jnp.arange(QBLOCK)
        z = jnp.einsum('bqhd,bkhd->bhqk', qb, k).astype(jnp.float32) * scale
        mask = k_pos[None, :] < q_pos[:, None]
        log_beta = jax.nn.log_sigmoid(z)
        log_keep = jnp.where(mask, jax.nn.log_sigmoid(-z), 0.0)
        suffix = lax.cumsum(log_keep, axis=3, reverse=True) - log_keep
        a = jnp.where(mask, jnp.exp(log_beta + suffix), 0.0)
        return jnp.einsum('bhqk,bkhd->bqhd', a.astype(v.dtype), v)

    return _sweep_query_blocks(block, seq)

def mla_attention(q_nope, q_rope, k_nope, k_rope, v):
    seq = q_nope.shape[1]
    scale = (NOPE_DIM + ROPE_DIM) ** -0.5
    k_chunk = jnp.arange(seq) // CHUNK

    def block(i):
        start = i * QBLOCK
        qn = lax.dynamic_slice_in_dim(q_nope, start, QBLOCK, axis=1)
        qr = lax.dynamic_slice_in_dim(q_rope, start, QBLOCK, axis=1)
        q_chunk = (start + jnp.arange(QBLOCK)) // CHUNK
        s = (jnp.einsum('bqhd,bkhd->bhqk', qn, k_nope)
             + jnp.einsum('bqhr,bkr->bhqk', qr, k_rope)).astype(jnp.float32) * scale
        mask = k_chunk[None, :] <= q_chunk[:, None]
        p = jax.nn.softmax(jnp.where(mask, s, -jnp.inf), axis=-1)
        return jnp.einsum('bhqk,bkhd->bqhd', p.astype(v.dtype), v)

    return _sweep_query_blocks(block, seq)

def even_mixer(h, w_in, b_forget, rel_bias, w_out):
    b, s, _ = h.shape
    qa, ka, va, fa, qb, kb, vb = _split(h @ w_in, SPLIT_AB)
    heads = lambda t, n: t.reshape(b, s, n, HEAD_DIM)
    log_f = jax.nn.log_sigmoid((fa + b_forget).astype(jnp.float32))
    o_a = fox_attention(heads(qa, H_FOX), heads(ka, H_FOX), heads(va, H_FOX), log_f)
    o_b = chunked_relpos_attention(heads(qb, H_CHK), heads(kb, H_CHK), heads(vb, H_CHK), rel_bias)
    o = jnp.concatenate([o_a.reshape(b, s, W_FOX), o_b.reshape(b, s, W_CHK)], axis=-1)
    return o @ w_out

def odd_mixer(h, positions, w_in, q_norm, kv_norm, w_uq, w_ukv, w_out):
    b, s, _ = h.shape
    qc, kc, vc, c_q, c_kv, k_r = _split(h @ w_in, SPLIT_CD)
    heads = lambda t, n, d: t.reshape(b, s, n, d)
    o_c = stick_breaking_attention(heads(qc, H_SB, HEAD_DIM), heads(kc, H_SB, HEAD_DIM), heads(vc, H_SB, HEAD_DIM))
    q_full = heads(rmsnorm_2(c_q, q_norm) @ w_uq, H_MLA, NOPE_DIM + ROPE_DIM)
    q_nope, q_rope = q_full[..., :NOPE_DIM], rope(q_full[..., NOPE_DIM:], positions)
    kv_full = heads(rmsnorm_2(c_kv, kv_norm) @ w_ukv, H_MLA, NOPE_DIM + V_DIM)
    k_nope, v_d = kv_full[..., :NOPE_DIM], kv_full[..., NOPE_DIM:]
    k_rope = rope(k_r[:, :, None, :], positions)[:, :, 0, :]
    o_d = mla_attention(q_nope, q_rope, k_nope, k_rope, v_d)
    o = jnp.concatenate([o_c.reshape(b, s, W_SB), o_d.reshape(b, s, W_MLA)], axis=-1)
    return o @ w_out

def squared_relu_mlp(h, w_up, w_down):
    return jnp.square(jax.nn.relu(h @ w_up)) @ w_down

def second_inputs(seed: int = 0) -> dict:
    key = jax.random.key(seed)
    ks = jax.random.split(key, 20)
    nrm = lambda k, shape, fan_in: jax.random.normal(k, shape, jnp.float32) * fan_in ** -0.5
    gain = lambda k, shape: 1.0 + 0.05 * jax.random.normal(k, shape, jnp.float32)
    x = jax.random.normal(ks[0], (BATCH, SEQ, D_MODEL), jnp.float32)
    offset = jax.random.randint(ks[1], (BATCH, 1), 0, 100000, dtype=jnp.int32)
    positions = offset + jnp.arange(SEQ, dtype=jnp.int32)[None, :]
    return {
        "x": x,
        "positions": positions,
        "norm_mix": gain(ks[2], (DEPTH_2, D_MODEL)),
        "norm_mlp": gain(ks[3], (DEPTH_2, D_MODEL)),
        "norm_final": gain(ks[4], (D_MODEL,)),
        "w_in_ab": nrm(ks[5], (N_EVEN, D_MODEL, IN_AB), D_MODEL),
        "b_forget": FORGET_BIAS + 0.5 * jax.random.normal(ks[6], (N_EVEN, H_FOX), jnp.float32),
        "rel_bias": 0.2 * jax.random.normal(ks[7], (N_EVEN, H_CHK, N_REL), jnp.float32),
        "w_out_ab": nrm(ks[8], (N_EVEN, MIX_AB, D_MODEL), MIX_AB),
        "w_in_cd": nrm(ks[9], (N_ODD, D_MODEL, IN_CD), D_MODEL),
        "q_norm": gain(ks[10], (N_ODD, Q_LORA)),
        "kv_norm": gain(ks[11], (N_ODD, KV_LORA)),
        "w_uq": nrm(ks[12], (N_ODD, Q_LORA, H_MLA * (NOPE_DIM + ROPE_DIM)), Q_LORA),
        "w_ukv": nrm(ks[13], (N_ODD, KV_LORA, H_MLA * (NOPE_DIM + V_DIM)), KV_LORA),
        "w_out_cd": nrm(ks[14], (N_ODD, MIX_CD, D_MODEL), MIX_CD),
        "w_up": nrm(ks[15], (DEPTH_2, D_MODEL, D_FF), D_MODEL),
        "w_down": nrm(ks[16], (DEPTH_2, D_FF, D_MODEL), D_FF),
    }

def second_block(x, positions, norm_mix, norm_mlp, norm_final, w_in_ab, b_forget, rel_bias, w_out_ab,
              w_in_cd, q_norm, kv_norm, w_uq, w_ukv, w_out_cd, w_up, w_down):
    for layer in range(DEPTH_2):
        h = rmsnorm_2(x, norm_mix[layer])
        if layer % 2 == 0:
            e = layer // 2
            x = x + even_mixer(h, w_in_ab[e], b_forget[e], rel_bias[e], w_out_ab[e])
        else:
            o = layer // 2
            x = x + odd_mixer(h, positions, w_in_cd[o], q_norm[o], kv_norm[o], w_uq[o], w_ukv[o], w_out_cd[o])
        x = x + squared_relu_mlp(rmsnorm_2(x, norm_mlp[layer]), w_up[layer], w_down[layer])
    return rmsnorm_2(x, norm_final)


def setup_inputs(seed=0):
    out = dict(first_inputs(seed))
    for name, value in second_inputs(seed + 1).items():
        if name != "x":
            out[name + "_2"] = value
    return out


def reference(
    x, mix_pre_norm, mix_post_norm, w_in, ssm_conv_w, ssm_conv_b, ssm_dt_bias, ssm_a_log, ssm_d,
    ssm_norm, w_proj_ssm, lru_conv_w, lru_conv_b, lru_wr, lru_br, lru_wi, lru_bi, lru_lambda,
    w_proj_lru, gate_b, w_out, ffn_pre_norm, ffn_post_norm, w_ffn_up, ffn_conv_w, ffn_conv_b,
    w_ffn_down, positions_2, norm_mix_2, norm_mlp_2, norm_final_2, w_in_ab_2, b_forget_2,
    rel_bias_2, w_out_ab_2, w_in_cd_2, q_norm_2, kv_norm_2, w_uq_2, w_ukv_2, w_out_cd_2, w_up_2,
    w_down_2,
):
    x = first_block(
        x, mix_pre_norm, mix_post_norm, w_in, ssm_conv_w, ssm_conv_b, ssm_dt_bias, ssm_a_log,
        ssm_d, ssm_norm, w_proj_ssm, lru_conv_w, lru_conv_b, lru_wr, lru_br, lru_wi, lru_bi,
        lru_lambda, w_proj_lru, gate_b, w_out, ffn_pre_norm, ffn_post_norm, w_ffn_up,
        ffn_conv_w, ffn_conv_b, w_ffn_down,
    )
    return second_block(
        x, positions_2, norm_mix_2, norm_mlp_2, norm_final_2, w_in_ab_2, b_forget_2, rel_bias_2,
        w_out_ab_2, w_in_cd_2, q_norm_2, kv_norm_2, w_uq_2, w_ukv_2, w_out_cd_2, w_up_2,
        w_down_2,
    )


_drawn_inputs = setup_inputs


def setup_inputs(seed=0):
    import zlib

    import numpy as np

    out = dict(_drawn_inputs(seed))
    spreads = {}
    factors = {'lru_br': 8.0,
     'lru_bi': 8.0,
     'gate_b': 7.972,
     'ffn_conv_b': 2.901,
     'norm_mix_2': 2.996,
     'rel_bias_2': 4.567,
     'q_norm_2': 8.0,
     'kv_norm_2': 8.0}
    for name, (base, spread) in spreads.items():
        noise = np.random.default_rng([zlib.crc32(name.encode()), seed]).standard_normal(out[name].shape)
        drawn = base * np.exp(spread * noise) if base else spread * noise
        out[name] = __import__('jax').numpy.asarray(drawn.astype(out[name].dtype))
    for name, factor in factors.items():
        out[name] = (out[name] * factor).astype(out[name].dtype)
    return out
```

```python
import concourse.bass as bass
import numpy as np
from concourse import mybir

P = 128
T = 256
TB = T // P
D = 1024
KD = D // P
EPS = 1e-6
NEG = -1.0e30
CHUNK = 64

SSM_TILES = 8
XBC_TILES = 12
SSM_HEADS = 16
FFN_PAIRS = 24
MLP_TILES = 32
F_TILES = 16
HEADS = 8
N_REL = 320
Q_KT, KV_KT = 3, 2

R = 4
BLOCKS = 8
BANKS = 4
S3 = 3 * P


LAYERS = [
    ("dt", 1, KD), ("xbc", XBC_TILES, KD), ("ly", KD, KD), ("lx", KD, KD), ("z", KD, KD), ("g0", KD, KD),
    ("proj_ssm", KD, KD), ("g1", KD, KD), ("proj_lru", KD, KD), ("mix_out", KD, KD),
    ("ffn_up_a", 2 * F_TILES, KD), ("ffn_down_a", KD, F_TILES),
    ("ffn_up_b", 2 * (FFN_PAIRS - F_TILES), KD), ("ffn_down_b", KD, FFN_PAIRS - F_TILES),
    ("fa", 1, KD), ("q_fox", 4, KD), ("k_fox", 4, KD), ("v_fox", 4, KD),
    ("q_chk", 4, KD), ("k_chk", 4, KD), ("v_chk", 4, KD), ("ab_out", KD, KD),
    ("mlp_up0a", F_TILES, KD), ("mlp_down0a", KD, F_TILES), ("mlp_up0b", F_TILES, KD), ("mlp_down0b", KD, F_TILES),
    ("q_sb", 4, KD), ("k_sb", 4, KD), ("v_sb", 4, KD), ("c_q", Q_KT, KD), ("c_kv", KV_KT, KD), ("k_rope", 2, KD),
    ("q_mla", HEADS, Q_KT), ("k_mla", HEADS, KV_KT), ("v_mla", 4, KV_KT), ("cd_out", KD, KD),
    ("mlp_up1a", F_TILES, KD), ("mlp_down1a", KD, F_TILES), ("mlp_up1b", F_TILES, KD), ("mlp_down1b", KD, F_TILES),
]


def plan():
    first, tiles, block, units, last_unit = {}, [], 0, 0, {}
    for name, count, depth in LAYERS:
        first[name] = len(tiles)
        for _ in range(count):
            pieces = []
            for k in range(depth):
                slab = block // BLOCKS
                if not pieces or pieces[-1][0] != slab:
                    pieces.append((slab, []))
                pieces[-1][1].append((block % BLOCKS, k))
                block += 1
            units += len(pieces)
            for n, (slab, _) in enumerate(pieces):
                last_unit[slab] = units - len(pieces) + n + 1
            tiles.append((pieces, units, depth))
    return first, tiles, -(-block // BLOCKS), last_unit


FIRST, TILES, SLABS, LAST_UNIT = plan()
COUNT = {name: count for name, count, _ in LAYERS}


def columns():
    at, n = {}, 0
    for name, width in [
        ("mix_pre", 8), ("mix_post", 8), ("xbc_w", 48), ("xbc_b", 12), ("skip", 8), ("ssm_norm", 8), ("lx_w", 32),
        ("lx_b", 8), ("br", 8), ("bi", 8), ("lam", 8), ("gate_b", 16), ("ffn_pre", 8), ("ffn_post", 8),
        ("ffn_w", 3 * 48), ("ffn_b", 48), ("mix2", 16), ("mlp2", 16), ("final", 8), ("q_norm", 3), ("kv_norm", 2),
        ("dt_bias", 1), ("a_log", 1), ("b_forget", 1), ("inv_freq", 1), ("rope_sign", 1),
    ]:
        at[name] = n
        n += width
    return at, n


COL, NCOL = columns()

TWO_PI = 6.283185307179586
TWO_PI_PARTS = (6.28125, 0.0019340515136718750, TWO_PI - 6.28125 - 0.0019340515136718750)
PI_DOWN = 3.1415925
ROUND = 12582912.0

NORMS = [
    ("mix_pre", 8, 1 / D), ("ssm0", 4, 2 / D), ("ssm1", 4, 2 / D), ("mix_post", 8, 1 / D), ("ffn_pre", 8, 1 / D),
    ("ffn_post", 8, 1 / D), ("mix2_0", 8, 1 / D), ("mlp2_0", 8, 1 / D), ("mix2_1", 8, 1 / D),
    ("q_norm", Q_KT, 1 / (Q_KT * P)), ("kv_norm", KV_KT, 1 / (KV_KT * P)), ("mlp2_1", 8, 1 / D), ("final", 8, 1 / D),
]
NORM = {name: i for i, (name, _, _) in enumerate(NORMS)}
DIRECT = ("mix_pre", "ffn_pre", "mix2_0")
ADDS = [sum(n - 1 for name, n, _ in NORMS[:i] if name not in DIRECT) for i in range(len(NORMS) + 1)]
PARTS = [sum(n - 1 for name, n, _ in NORMS[:i] if name in DIRECT) for i in range(len(NORMS) + 1)]
SQ_SLOTS = 4
SQUARES = [sum(n for _, n, _ in NORMS[:i]) for i in range(len(NORMS) + 1)]


def build(nc, x_t, consts, positions, stream, lru_r, lru_i, rel, out_t):
    fp32, fp32r, bf16, i32 = mybir.dt.float32, mybir.dt.float32r, mybir.dt.bfloat16, mybir.dt.int32
    ALU, ACT = mybir.AluOpType, mybir.ActivationFunctionType
    sb = lambda name, *shape, dt=fp32: nc.alloc_sbuf_tensor(name, list(shape), dt)

    RAW = sb("weights_raw", P, R, BLOCKS * P)
    WH = sb("weights_hi", P, R, BLOCKS * P, dt=fp32r)
    WL = sb("weights_lo", P, R, BLOCKS * P, dt=fp32r)
    C = sb("consts", P, NCOL)
    X = sb("residual", P, KD, T)
    HH, HL = (sb(f"hidden_{part}", P, KD, T, dt=fp32r) for part in ("hi", "lo"))
    FH, FL = (sb(f"inner_{part}", P, F_TILES, T, dt=fp32r) for part in ("hi", "lo"))
    SQ = sb("squares", P, SQ_SLOTS, T)
    ACC = sb("square_sum", P, T)
    RS = sb("rstd", P, 3, T)
    A = sb("arena", P, 72, T)
    ident = sb("ident", P, P)
    ones = sb("ones", P, T)
    keep_incl = sb("keep_incl", P, S3, dt=bf16)
    keep_strict = sb("keep_strict", P, S3, dt=bf16)
    neg_strict = sb("neg_strict", P, S3, dt=bf16)
    neg_causal = sb("neg_causal", P, S3, dt=bf16)
    neg_chunk = sb("neg_chunk", P, S3, dt=bf16)
    neg_tri = sb("neg_tri", P, P)
    neg_one = sb("neg_one", P, P)
    S = sb("scores", P, 2, S3)
    M = sb("weights", P, 2, S3)
    PT = sb("weights_turned", P, 2, S3)
    ST = sb("stats", P, 2, 8)
    POS = sb("positions_sb", P, T, dt=i32)
    EPSC = sb("eps_column", P, 1)
    a = lambda lo, n: A[:, lo:lo + n, :]
    flat = lambda lo, n: A[:, lo:lo + n, :].rearrange("p a t -> p (a t)")
    XS, BC, XC, GATE, ZS, G = a(0, 8), a(8, 4), a(12, 8), a(20, 8), a(28, 8), a(36, 8)
    CBM = flat(8, 3).rearrange("p (g n) -> p g n", g=2)
    XDT = flat(44, 8).rearrange("p (b h d) -> p b h d", b=TB, d=64)
    YS, IG = a(52, 8), a(60, 8)
    TH, AG = XS, a(44, 8)
    MG = ZS
    Y = XC
    HT = a(68, 4)
    BLKR, BLKI = IG[:, :, 0:P], IG[:, :, P:T]
    CV = a(28, 4)
    SP = a(51, 5)
    Q, K = a(0, 8), a(8, 8)
    V = flat(16, 4).rearrange("p (b n) -> p b n", b=TB)
    Q2, K2 = a(20, 4), a(24, 4)
    V2 = flat(28, 4).rearrange("p (b n) -> p b n", b=TB)
    AQ, BK = a(32, 4), a(36, 4)
    CUM, NCUM = A[0:HEADS, 40, :], A[0:HEADS, 41, :]
    LAT = a(42, 5)
    KF, TQ, COS, SIN, KR, ANG = A[:, 47, :], A[:, 48, :], A[:, 49, :], A[:, 50, :], a(51, 2), a(20, 6)
    BIAS = flat(56, 12).rearrange("p (h n) -> p h n", n=S3)
    RT = a(0, 4)
    DT, ACS = sb("dt_steps", 16, T), sb("a_cumsum", 16, T)
    NEGA = sb("neg_a", 16, 1)
    COLS = sb("dt_columns", P, TB, 2, SSM_HEADS)
    LSP = sb("lru_softplus", P, 6, KD)
    HB = sb("half_biases", P, 32)
    NB = sb("neg_b_forget", HEADS, 1)

    bank = [nc.alloc_psum_tensor(f"bank{i}", [P, 512], fp32) for i in range(8)]
    N4, N5, N6, N7 = bank[4:]

    def sems(names):
        return [nc.alloc_semaphore(name) for name in names.split()]

    slab_in = [nc.alloc_semaphore(f"slab_in{s}") for s in range(R)]
    consts_in, x_in, blk_in, bias_in, pos_in = sems("consts_in x_in blk_in bias_in pos_in")
    tables, blk_zero, bias_ready = sems("tables blk_zero bias_ready")
    unit, = sems("unit_done")
    hi_ready, lo_ready = sems("weights_hi_ready weights_lo_ready")
    squared, added, ms_part, ms_ready = sems("squared squares_added ms_part ms_ready")
    std_ready, rstd_ready = sems("std_ready rstd_ready")
    h32, h_hi, h_ready, x_ready, step = sems("h_float32 h_hi h_ready x_ready dve_step")
    evac, conv, conv0, act_in, dve_take, y_evac = sems("evac conv_done conv_started act_in_place dve_take y_evac")
    tap_done, u_taken, y_sum = sems("tap_done u_taken y_sum")
    sp_in, sp_exp, dt_ready, nega, acs_ready = sems("softplus_in softplus_exp dt_ready neg_a acs_ready")
    colt, cols_ready, xst, xdt_ready, cbt, cbm_ready = sems("colt cols_ready xs_turned xdt_ready cb_done cbm_ready")
    bcast, seg_ready, decay_ready, m_ready, y_mm = sems("acs_broadcast seg_ready decay_ready m_ready y_mm")
    ys_ready, yg_ready, yn_ready, ya_hi, ya_ready = sems("ys_ready yg_ready yn_ready ya_hi ya_ready")
    lam_ready, half_bias, rg_mm, rg_ready, ag_ready, th_ready = sems("lam_ready half_bias rg_mm rg_ready ag_ready th_ready")
    m2_ready, ix_ready, mult_ready, g_ready = sems("m2_ready ix_ready mult_ready g_ready")
    yb32, yb_hi, yb_ready, mg32, mg_hi, mg_ready = sems("yb_float32 yb_hi yb_ready merged_float32 merged_hi merged_ready")
    gelu_done, f32_ready, f_hi, f_ready = sems("gelu_done f_float32 f_hi f_ready")
    relu_done, zs_ready = sems("relu_done zs_ready")
    cum_ready, dtile_zero, dtile_in = sems("cum_ready dtile_zero dtile_in")
    s_mm, s_max, s_bias, p_exp, p_norm, pt_mm = sems("scores_done scores_max exp_bias weights_exp weights_normed turned")
    pt_ready, pv_mm, o_hi, o_ready = sems("turned_out pv_done heads_hi heads_out")
    z_abs, z_exp, z_ln, lm_ready, arg_mm, arg_ready, a_exp = sems("z_abs z_exp z_ln lm_ready arg_mm arg_ready a_exp")
    ang_ready, sin_ready, trig_ready, kcopy = sems("ang_ready sin_ready trig_ready kcopy")
    out_ready, stored = sems("out_ready stored")

    FREE, counts = {}, {x_ready: 2 * KD}

    def frees(layer, s):
        for n in range(COUNT[layer]):
            counts[s] = counts.get(s, 0) + 1
            FREE[FIRST[layer] + n] = (s, counts[s])

    def taken(layer, n=0):
        return FREE[FIRST[layer] + n][1]

    for names, s in [("dt", u_taken), ("xbc", conv), ("ly", evac), ("lx", conv), ("z", dve_take), ("g0", evac),
                     ("proj_ssm", dve_take), ("g1", evac), ("proj_lru", dve_take), ("ffn_up_a", conv),
                     ("ffn_down_a", evac), ("ffn_up_b", conv), ("ffn_down_b", y_sum), ("fa", u_taken),
                     ("q_fox k_fox v_fox q_chk k_chk v_chk", evac), ("ab_out", x_ready), ("mlp_up0a", evac),
                     ("mlp_down0a", x_ready), ("mlp_up0b", evac), ("mlp_down0b", x_ready),
                     ("q_sb k_sb v_sb c_q c_kv k_rope", evac), ("q_mla", dve_take), ("k_mla v_mla", evac),
                     ("cd_out", x_ready), ("mlp_up1a", evac), ("mlp_down1a", x_ready), ("mlp_up1b", evac),
                     ("mlp_down1b", x_ready)]:
        for name in names.split():
            frees(name, s)
    for n in range(KD):
        FREE[FIRST["mix_out"] + n] = (squared, SQUARES[NORM["mix_post"]] + n + 1)

    def col(name, n=0, rows=slice(0, P)):
        return C[rows, COL[name] + n:COL[name] + n + 1]

    def col_n(name, n):
        return C[:, COL[name]:COL[name] + n]

    def dyn(i):
        return slice(i, i + 1) if isinstance(i, int) else bass.ds(i, 1)

    def tile_bank(layer, n):
        return bank[(FIRST[layer] + n) % BANKS]

    def unit_of(layer, n):
        return TILES[FIRST[layer] + n][1]

    def slab_of(layer, n):
        return TILES[FIRST[layer] + n][0][-1][0]

    def square_used(q):
        i = max(i for i in range(len(NORMS)) if SQUARES[i] <= q)
        name, n, _ = NORMS[i]
        k = q - SQUARES[i]
        if name not in DIRECT:
            return added, ADDS[i] + max(k, 1)
        return (ms_ready, i + 1) if k == n - 1 else (ms_part, PARTS[i] + k + 1)

    ALL_TABLES = 22

    block = nc.Block()
    with block:
        @block.sync
        def _(sp):
            for half in range(2):
                sp.dma_start(X[:, 4 * half:4 * half + 4, :], x_t[:, 4 * half:4 * half + 4, :]).then_inc(x_in, 16)
            sp.dma_start(C[:, :], consts).then_inc(consts_in, 16)
            for s in range(R):
                sp.dma_start(RAW[:, s, :], stream[s]).then_inc(slab_in[s], 16)
            turns = SLABS // R
            with sp.Fori(1, turns) as it:
                for s in range(R):
                    sp.wait_ge(lo_ready, it * R + (s - R + 1))
                    sp.dma_start(RAW[:, s, :], stream[it * R + s]).then_inc(slab_in[s], 16)
            for i in range(R * turns, SLABS):
                sp.wait_ge(lo_ready, i - R + 1)
                sp.dma_start(RAW[:, i % R, :], stream[i]).then_inc(slab_in[i % R], 16)
            for k in range(KD):
                sp.wait_ge(out_ready, k + 1)
                sp.dma_start(out_t[:, k, :], Y[:, k, :]).then_inc(stored, 16)
            sp.wait_ge(stored, 16 * KD)

        @block.gpsimd
        def _(pool):
            pool.dma_start(POS[:, :], positions.to_broadcast([P, T])).then_inc(pos_in, 16)
            pool.memset(BLKR, 0.0).then_inc(blk_zero, 1)
            pool.memset(BLKI, 0.0).then_inc(blk_zero, 1)
            pool.wait_ge(blk_zero, 2)
            for dst, src in ((BLKR, lru_r), (BLKI, lru_i)):
                for half in range(2):
                    rows = slice(64 * half, 64 * half + 64)
                    pool.dma_start(dst[rows, :, rows], src[half]).then_inc(blk_in, 16)
            fills = [(ident, 0.0), (ones, 1.0), (keep_incl, 1.0), (keep_strict, 1.0), (neg_strict, 0.0),
                     (neg_causal, 0.0), (neg_chunk, 0.0), (neg_tri, -1.0), (neg_one, -1.0), (EPSC, EPS)]
            for tile, value in fills:
                pool.memset(tile[:, :], value).then_inc(tables, 1)
            n = len(fills)
            pool.wait_ge(tables, n)
            pool.affine_select(out=ident[:, :], in_=ident[:, :], compare_op=ALU.not_equal, fill=1.0, base=0,
                               pattern=[[-1, P]], channel_multiplier=1).then_inc(tables, 1)
            for tile, fill, base, row, colm in [(keep_incl, 0.0, 0, -1, 1), (keep_strict, 0.0, -1, -1, 1),
                                                (neg_strict, NEG, -1, -1, 1), (neg_causal, NEG, 0, 1, -1)]:
                for d in (0, 2):
                    part = tile[:, d * P:d * P + P]
                    pool.affine_select(out=part, in_=part, compare_op=ALU.is_ge, fill=fill, base=base,
                                       pattern=[[colm, P]], channel_multiplier=row).then_inc(tables, 1)
            for d in (0, 2):
                part = neg_chunk[:, d * P + CHUNK:d * P + P]
                pool.affine_select(out=part, in_=part, compare_op=ALU.is_ge, fill=NEG, base=-CHUNK,
                                   pattern=[[0, CHUNK]], channel_multiplier=1).then_inc(tables, 1)
            pool.affine_select(out=neg_tri[:, :], in_=neg_tri[:, :], compare_op=ALU.is_ge, fill=0.0, base=0,
                               pattern=[[-1, P]], channel_multiplier=1).then_inc(tables, 1)
            pool.wait_ge(unit, unit_of("mix_out", 0))
            pool.wait_ge(tables, ALL_TABLES)
            pool.dma_start(BIAS, rel).then_inc(bias_in, 16)
            pool.wait_ge(bias_in, 16)
            for h in range(HEADS):
                pool.tensor_tensor(BIAS[:, h, :], BIAS[:, h, :], neg_chunk[:, :], ALU.add).then_inc(bias_ready, 1)
            pool.memset(AQ, 0.0).then_inc(dtile_zero, 1)
            pool.memset(BK, 0.0).then_inc(dtile_zero, 1)
            pool.wait_ge(dtile_zero, 2)
            for base in (0, 64):
                pool.memset(AQ[base:base + 2], 1.0).then_inc(dtile_zero, 1)
                pool.memset(BK[base:base + 2], 1.0).then_inc(dtile_zero, 1)
            pool.wait_ge(dtile_zero, 6)
            pool.wait_ge(cum_ready, 4)
            for h in range(HEADS):
                row = 64 * (h % 2)
                pool.dma_start(AQ[row + 1:row + 2, h // 2, :], CUM[h:h + 1, :]).then_inc(dtile_in, 16)
                pool.dma_start(BK[row:row + 1, h // 2, :], NCUM[h:h + 1, :]).then_inc(dtile_in, 16)

        @block.tensor
        def _(pe):
            def block_products(out, slot, blk, hi, lo, first, last, half=None):
                cols = slice(blk * P, blk * P + P)
                for n, (w, x) in enumerate(((WH, hi), (WH, lo), (WL, hi))):
                    w = w[:, slot, cols]
                    lhs, rhs = (w, x) if half is None else (x[:, half * P:half * P + P], w)
                    mm = pe.matmul(out, lhs, rhs, start=(first and n == 0), stop=(last and n == 2))
                return mm

            def dense_tile(t, hi, lo, token_major=False, ready=None):
                pieces, _, depth = TILES[t]
                b = bank[t % BANKS]
                if t >= BANKS:
                    pe.wait_ge(*FREE[t - BANKS])
                halves = range(TB) if token_major else (None,)
                assert not token_major or len(pieces) == 1
                for slab, blocks in pieces:
                    pe.wait_ge(lo_ready, slab + 1)
                    for half in halves:
                        out = b[:, 0:T] if half is None else b[:, half * P:half * P + P]
                        for blk, k in blocks:
                            if ready:
                                pe.wait_ge(ready[0], ready[1] + k + 1)
                            mm = block_products(out, slab % R, blk, hi[:, k, :], lo[:, k, :], k == 0, k == depth - 1, half)
                    mm.then_inc(unit, 1)

            def layer(name, hi, lo, hooks=None, ready=None, **kw):
                for n in range(COUNT[name]):
                    dense_tile(FIRST[name] + n, hi, lo, ready=ready if n == 0 else None, **kw)
                    if hooks and n in hooks:
                        hooks[n]()

            def loop_layer(name, hi, lo, per, ready):
                t0, depth = FIRST[name], TILES[FIRST[name]][2]
                slabs = depth // BLOCKS
                s0 = TILES[t0][0][0][0]
                assert per * slabs % R == 0 and per % BANKS == 0 and COUNT[name] % per == 0
                own, first_taken = FREE[t0]
                for j in range(BANKS):
                    pe.wait_ge(*FREE[t0 + j - BANKS])

                def turn(it):
                    for j in range(per):
                        if not (isinstance(it, int) and first_taken + j <= BANKS):
                            pe.wait_ge(own, it * per + (first_taken + j - BANKS))
                        for s in range(slabs):
                            slab = s0 + j * slabs + s
                            pe.wait_ge(lo_ready, it * (per * slabs) + (slab + 1))
                            for blk in range(BLOCKS):
                                k = s * BLOCKS + blk
                                if j == 0:
                                    pe.wait_ge(ready[0], ready[1] + k + 1)
                                mm = block_products(bank[(t0 + j) % BANKS][:, 0:T], slab % R, blk, hi[:, k, :], lo[:, k, :],
                                                    k == 0, k == depth - 1)
                            mm.then_inc(unit, 1)

                if COUNT[name] == per or first_taken <= BANKS:
                    turn(0)
                if COUNT[name] > per:
                    with pe.Fori(0 if first_taken > BANKS else 1, COUNT[name] // per) as it:
                        turn(it)

            def mean_square(name):
                i = NORM[name]
                if i:
                    pe.wait_ge(std_ready, i)
                if name not in DIRECT:
                    pe.wait_ge(added, ADDS[i + 1])
                    pe.matmul(N4[:, 0:T], ones[:, 0:P], ACC[:, :], start=True, stop=True).then_inc(ms_ready, 1)
                    return
                n = NORMS[i][1]
                for k in range(n):
                    pe.wait_ge(squared, SQUARES[i] + k + 1)
                    mm = pe.matmul(N4[:, 0:T], ones[:, 0:P], SQ[:, (SQUARES[i] + k) % SQ_SLOTS, :], start=(k == 0), stop=(k == n - 1))
                    mm.then_inc(ms_ready if k == n - 1 else ms_part, 1)

            pe.wait_ge(tables, ALL_TABLES)
            mean_square("mix_pre")
            layer("dt", HH, HL, ready=(h_ready, 0))
            layer("xbc", HH, HL)

            def dt_columns():
                pe.wait_ge(acs_ready, 1)
                for b in range(TB):
                    for n, src in enumerate((ACS, DT)):
                        mm = pe.matmul(N5[:, (2 * b + n) * 16:(2 * b + n) * 16 + 16], src[:, b * P:b * P + P],
                                       ident[0:16, 0:16], start=True, stop=True)
                mm.then_inc(colt, 1)

            def cb():
                pe.wait_ge(act_in, XBC_TILES)
                for g in range(2):
                    b, bt, ct = (N6, N7)[g], BC[:, g, :], BC[:, 2 + g, :]
                    pe.matmul(b[:, 0:T], bt[:, 0:P], ct, start=True, stop=True)
                    pe.matmul(b[:, T:S3], bt[:, P:T], ct[:, P:T], start=True, stop=True).then_inc(cbt, 1)

            def turn_xs(b):
                pe.wait_ge(cbm_ready, 2)
                if b:
                    pe.wait_ge(xdt_ready, 2 * b)
                for j in range(SSM_TILES):
                    mm = pe.transpose((N6, N7)[j // 4][:, (j % 4) * P:(j % 4) * P + P], XS[:, j, b * P:b * P + P], ident[:, :])
                    if j % 4 == 3:
                        mm.then_inc(xst, 1)

            def lru_gates(j):
                if j == 0:
                    pe.wait_ge(blk_in, 64)
                    pe.wait_ge(conv, XBC_TILES + KD)
                else:
                    pe.wait_ge(rg_ready, 2 * j)
                b = N5
                pe.matmul(b[:, 0:T], BLKR[:, j, :], XC[:, j, :], start=True, stop=True)
                pe.matmul(b[:, T:2 * T], BLKI[:, j, :], XC[:, j, :], start=True, stop=True).then_inc(rg_mm, 1)

            def head_bcast(h):
                if h >= 1:
                    pe.wait_ge(seg_ready, h)
                pe.matmul(N4[:, 0:T], ident[0:16, h:h + 1].to_broadcast([16, P]), ACS[:, :],
                          start=True, stop=True).then_inc(bcast, 1)

            def head_y(h):
                pe.wait_ge(m_ready, h + 1)
                if h >= 4 and h % 2 == 0:
                    pe.wait_ge(ys_ready, h // 2 - 1)
                b, rows = (N6, N7)[h // 2 % 2], slice(64 * (h % 2), 64 * (h % 2) + 64)
                pe.matmul(b[rows, 0:T], XDT[:, 0, h, :], M[:, h % 2, 0:T], start=True, stop=False)
                pe.matmul(b[rows, P:T], XDT[:, 1, h, :], M[:, h % 2, T:S3], start=False, stop=True).then_inc(y_mm, 1)

            def heads(n):
                if n < SSM_HEADS:
                    head_bcast(n)
                if n >= 1:
                    head_y(n - 1)

            layer("ly", HH, HL, {0: dt_columns, 1: cb, 3: lambda: turn_xs(0), 5: lambda: turn_xs(1)})
            pe.wait_ge(cols_ready, 1)
            pe.wait_ge(xdt_ready, 4)
            layer("lx", HH, HL, {n: (lambda n=n: heads(n)) for n in range(8)})
            layer("z", HH, HL, {n: (lambda n=n: heads(n + 8)) for n in range(8)})

            def after_g0(n):
                if n == 0:
                    heads(SSM_HEADS)
                if n == 3:
                    mean_square("ssm0")
                if n == 4:
                    mean_square("ssm1")
                lru_gates(n)

            layer("g0", HH, HL, {n: (lambda n=n: after_g0(n)) for n in range(8)})
            layer("proj_ssm", FH, FL, ready=(ya_ready, 0))
            layer("g1", HH, HL)
            layer("proj_lru", FH[:, 8:16, :], FL[:, 8:16, :], ready=(yb_ready, 0))
            layer("mix_out", FH, FL, ready=(mg_ready, 0))
            mean_square("mix_post")
            mean_square("ffn_pre")
            loop_layer("ffn_up_a", HH, HL, 8, (h_ready, 8))
            loop_layer("ffn_down_a", FH, FL, 4, (f_ready, 0))
            loop_layer("ffn_up_b", HH, HL, 8, (h_ready, 8))
            loop_layer("ffn_down_b", FH, FL, 8, (f_ready, F_TILES))
            mean_square("ffn_post")

            mean_square("mix2_0")
            layer("fa", HH, HL, ready=(h_ready, 16))
            layer("q_fox", HH, HL)
            layer("k_fox", HH, HL)
            layer("v_fox", HH, HL, token_major=True)

            def score_head(kind, n, h, q, k):
                if n >= 2:
                    pe.wait_ge(s_max, 2 * (n - 1))
                b = (N4, N5)[n % 2]
                rows = slice(64 * (h % 2), 64 * (h % 2) + 64)
                for qb, lo, cols in ((0, 0, P), (1, P, T)):
                    if kind == "mla":
                        mm = pe.matmul(b[:, lo:lo + cols], q[:, h, qb * P:qb * P + P], k[:, h, 0:cols], start=True, stop=True)
                        continue
                    mm = pe.matmul(b[:, lo:lo + cols], q[rows, h // 2, qb * P:qb * P + P], k[rows, h // 2, 0:cols],
                                   start=True, stop=(kind != "fox"))
                    if kind == "fox":
                        mm = pe.matmul(b[:, lo:lo + cols], AQ[rows, h // 2, qb * P:qb * P + P], BK[rows, h // 2, 0:cols],
                                       start=False, stop=True)
                mm.then_inc(s_mm, 1)

            def turn_head(n):
                pe.wait_ge(p_norm, n + 1)
                if n >= 1:
                    pe.wait_ge(pt_ready, n)
                for c in range(3):
                    mm = pe.transpose(N6[:, c * P:c * P + P], M[:, n % 2, c * P:c * P + P], ident[:, :])
                mm.then_inc(pt_mm, 1)

            def weigh_head(n, h, v, w, w_ready, count):
                pe.wait_ge(w_ready, count)
                pair = n // 2
                if h % 2 == 0 and pair >= 1:
                    pe.wait_ge(o_ready, pair)
                rows, c = slice(64 * (h % 2), 64 * (h % 2) + 64), slice(64 * h, 64 * h + 64)
                pe.matmul(N7[rows, 0:T], v[:, 0, c], w[:, 0:T], start=True, stop=False)
                pe.matmul(N7[rows, P:T], v[:, 1, c], w[:, T:S3], start=False, stop=True).then_inc(pv_mm, 1)

            def softmax_step(i, kind, n0, o0, q, k, v):
                if i < HEADS:
                    score_head(kind, n0 + i, i, q, k)
                if 1 <= i <= HEADS:
                    turn_head(n0 + i - 1)
                if 2 <= i <= HEADS + 1:
                    h = i - 2
                    weigh_head(o0 + h, h, v, PT[:, (n0 + h) % 2, :], pt_ready, n0 + h + 1)

            def fox(i):
                if i == 0:
                    pe.wait_ge(evac, taken("v_fox", 3))
                    pe.wait_ge(dtile_in, 32 * HEADS)
                softmax_step(i, "fox", 0, 0, Q, K, V)

            layer("q_chk", HH, HL, {n: (lambda n=n: fox(n)) for n in range(4)})
            layer("k_chk", HH, HL, {n: (lambda n=n: fox(n + 4)) for n in range(4)})
            layer("v_chk", HH, HL, {n: (lambda n=n: fox(n + 8)) for n in range(2)}, token_major=True)
            pe.wait_ge(evac, taken("v_chk", 3))
            for i in range(HEADS + 2):
                softmax_step(i, "chk", 8, 8, Q2, K2, V2)
            layer("ab_out", FH, FL, ready=(o_ready, 0))
            mean_square("mlp2_0")

            def mlp(which, h0, f0):
                loop_layer(f"mlp_up{which}a", HH, HL, 4, (h_ready, h0))
                loop_layer(f"mlp_down{which}a", FH, FL, 4, (f_ready, f0))
                loop_layer(f"mlp_up{which}b", HH, HL, 4, (h_ready, h0))
                loop_layer(f"mlp_down{which}b", FH, FL, 4, (f_ready, f0 + F_TILES))

            mlp(0, 24, FFN_PAIRS)
            mean_square("mix2_1")
            layer("q_sb", HH, HL, ready=(h_ready, 32))
            layer("k_sb", HH, HL)
            layer("v_sb", HH, HL, token_major=True)

            def sb_scores(h):
                if h >= 2:
                    pe.wait_ge(arg_ready, h - 1)
                b = (N5, N6)[h % 2]
                rows = slice(64 * (h % 2), 64 * (h % 2) + 64)
                pe.matmul(b[:, 0:T], K[rows, h // 2, 0:P], Q[rows, h // 2, :], start=True, stop=False, skip_group_check=True)
                pe.matmul(b[:, T:S3], K[rows, h // 2, P:T], Q[rows, h // 2, P:T], start=False, stop=False,
                          skip_group_check=True).then_inc(s_mm, 1)

            def sb_suffix(h):
                pe.wait_ge(lm_ready, 2 * (h + 1))
                b, lm = (N5, N6)[h % 2], S[:, h % 2, :]
                pe.matmul(b[:, 0:T], neg_tri[:, :], lm[:, 0:T], start=False, stop=False, skip_group_check=True)
                pe.matmul(b[:, P:T], neg_one[:, :], lm[:, T:S3], start=False, stop=False, skip_group_check=True)
                pe.matmul(b[:, T:S3], neg_tri[:, :], lm[:, T:S3], start=False, stop=True,
                          skip_group_check=True).then_inc(arg_mm, 1)

            def stick(i):
                if i == 0:
                    pe.wait_ge(evac, taken("v_sb", 3))
                if i < HEADS:
                    sb_scores(i)
                if 1 <= i <= HEADS:
                    sb_suffix(i - 1)
                if 2 <= i <= HEADS + 1:
                    h = i - 2
                    weigh_head(16 + h, h, V, M[:, h % 2, :], a_exp, h + 1)

            layer("c_q", HH, HL, {n: (lambda n=n: stick(n)) for n in range(3)})
            layer("c_kv", HH, HL, {n: (lambda n=n: stick(n + 3)) for n in range(2)})
            layer("k_rope", HH, HL, {n: (lambda n=n: stick(n + 5)) for n in range(2)})
            mean_square("q_norm")
            mean_square("kv_norm")
            for i in range(7, HEADS + 2):
                stick(i)
            layer("q_mla", HH, HL, ready=(h_ready, 40))
            layer("k_mla", HH[:, Q_KT:, :], HL[:, Q_KT:, :], ready=(h_ready, 40 + Q_KT))
            layer("v_mla", HH[:, Q_KT:, :], HL[:, Q_KT:, :], token_major=True)
            pe.wait_ge(evac, taken("v_mla", 3))
            pe.wait_ge(dve_take, taken("q_mla", HEADS - 1))
            pe.wait_ge(kcopy, 1)
            for i in range(HEADS + 2):
                softmax_step(i, "mla", 16, 24, Q, K, V)
            layer("cd_out", FH, FL, ready=(o_ready, 8))
            mean_square("mlp2_1")
            mlp(1, 45, FFN_PAIRS + MLP_TILES)
            mean_square("final")

        @block.scalar
        def _(act):
            rounded = [0]

            def round_slab(i, turn=0, per=0):
                act.wait_ge(slab_in[i % R], turn * (16 * per // R) + 16 * (i // R + 1))
                if i >= R:
                    act.wait_ge(unit, turn * per + LAST_UNIT[i - R])
                act.activation(WH[:, i % R, :], RAW[:, i % R, :], ACT.Copy).then_inc(hi_ready, 1)

            def ahead(name, n):
                while rounded[0] < min(slab_of(name, n) + R, SLABS):
                    round_slab(rounded[0])
                    rounded[0] += 1

            def square(name, k, src):
                i = NORM[name]
                if SQUARES[i] + k >= SQ_SLOTS:
                    act.wait_ge(*square_used(SQUARES[i] + k - SQ_SLOTS))
                act.activation(SQ[:, (SQUARES[i] + k) % SQ_SLOTS, :], src, ACT.Square).then_inc(squared, 1)

            def std(name):
                i = NORM[name]
                act.wait_ge(ms_ready, i + 1)
                act.activation(RS[:, i % 3, :], N4[:, 0:T], ACT.Sqrt, bias=EPSC[:, :], scale=NORMS[i][2]).then_inc(std_ready, 1)

            def residual_square(name, k, count):
                act.wait_ge(x_ready, count)
                square(name, k, X[:, k, :])

            def round_hidden(base, last_reader=None, n=KD, src=HT):
                if last_reader:
                    act.wait_ge(unit, unit_of(last_reader, COUNT[last_reader] - 1))
                for k in range(n):
                    act.wait_ge(h32, base + k + 1)
                    act.activation(HH[:, k, :], src[:, k % src.shape[1], :], ACT.Copy).then_inc(h_hi, 1)

            def softplus_exp(i, out, in_):
                act.wait_ge(sp_in, i + 1)
                act.activation(out, in_, ACT.Exp).then_inc(sp_exp, 1)

            def tile(name, n):
                act.wait_ge(unit, unit_of(name, n))
                return tile_bank(name, n)[:, 0:T]

            act.wait_ge(x_in, 32)
            for k in range(KD):
                square("mix_pre", k, X[:, k, :])
            act.wait_ge(tables, ALL_TABLES)
            round_slab(0)
            rounded[0] = 1
            std("mix_pre")
            act.wait_ge(consts_in, 16)
            round_hidden(0)
            ahead("dt", 0)
            act.activation(NEGA[:, :], col("a_log", rows=slice(0, 16)), ACT.Exp).then_inc(nega, 1)
            softplus_exp(0, SP[0:16, 2, :], SP[0:16, 1, :])

            def tap(name, n, out):
                act.activation(out, tile(name, n), ACT.Identity, bias=col(name + "_b", n),
                               scale=col(name + "_w", 4 * n + 3)).then_inc(conv0, 1)

            def silu(n):
                act.wait_ge(conv, n + 1)
                act.activation(A[:, n, :], A[:, n, :], ACT.Silu).then_inc(act_in, 1)

            for n in range(XBC_TILES):
                ahead("xbc", n)
                tap("xbc", n, A[:, n, :])
                if n == 2:
                    softplus_exp(1, LSP[:, 2, :], LSP[:, 1, :])
                if n >= 1:
                    silu(n - 1)
            silu(XBC_TILES - 1)
            for n in range(KD):
                ahead("ly", n)
                act.activation(GATE[:, n, :], tile("ly", n), ACT.Gelu_apprx_tanh).then_inc(evac, 1)

            def decay(h):
                act.wait_ge(seg_ready, h + 1)
                act.activation(S[:, h % 2, :], S[:, h % 2, :], ACT.Exp).then_inc(decay_ready, 1)

            for n in range(KD):
                ahead("lx", n)
                tap("lx", n, XC[:, n, :])
                decay(n)
            for n in range(KD):
                ahead("z", n)
                act.activation(ZS[:, n, :], tile("z", n), ACT.Tanh, scale=0.5).then_inc(zs_ready, 1)
                decay(8 + n)
            act.wait_ge(half_bias, 3)

            def round_ya(k):
                act.wait_ge(yn_ready, k + 1)
                act.activation(FH[:, k, :], YS[:, k, :], ACT.Copy).then_inc(ya_hi, 1)

            for n in range(KD):
                ahead("g0", n)
                if n in (4, 5):
                    std(("ssm0", "ssm1")[n - 4])
                act.activation(G[:, n, :], tile("g0", n), ACT.Tanh, bias=HB[:, n:n + 1], scale=0.5).then_inc(evac, 1)
                if n == 0:
                    act.wait_ge(ys_ready, SSM_TILES)
                if n in (1, 2):
                    for k in range(4):
                        act.wait_ge(yg_ready, 4 * (n - 1) + k + 1)
                        square(("ssm0", "ssm1")[n - 1], k, YS[:, 4 * (n - 1) + k, :])
                act.wait_ge(rg_mm, n + 1)
                act.activation(TH[:, n, :], N5[:, 0:T], ACT.Tanh, bias=HB[:, 16 + n:17 + n], scale=0.5).then_inc(rg_ready, 1)
                act.activation(IG[:, n, :], N5[:, T:2 * T], ACT.Tanh, bias=HB[:, 24 + n:25 + n], scale=0.5).then_inc(rg_ready, 1)
                if n in (6, 7):
                    for k in range(4):
                        round_ya(4 * (n - 6) + k)
            act.wait_ge(lam_ready, 2)
            for n in range(KD):
                ahead("proj_ssm", n)
                act.wait_ge(rg_ready, 2 * n + 1)
                act.activation(AG[:, n, :], TH[:, n, :], ACT.Exp, bias=LSP[:, 4, n:n + 1], scale=LSP[:, 4, n:n + 1]).then_inc(ag_ready, 1)
                act.activation(TH[:, n, :], TH[:, n, :], ACT.Tanh, bias=LSP[:, 3, n:n + 1], scale=LSP[:, 3, n:n + 1]).then_inc(th_ready, 1)

            def round_yb(k):
                act.wait_ge(yb32, k + 1)
                act.activation(FH[:, KD + k, :], GATE[:, k, :], ACT.Copy).then_inc(yb_hi, 1)

            for n in range(KD):
                ahead("g1", n)
                act.wait_ge(dve_take, taken("proj_ssm", n))
                act.activation(G[:, n, :], tile("g1", n), ACT.Tanh, bias=HB[:, 8 + n:9 + n], scale=0.5).then_inc(evac, 1)
                if n == 0:
                    for j in range(KD):
                        act.wait_ge(m2_ready, j + 1)
                        act.activation(TH[:, j, :], TH[:, j, :], ACT.Sqrt, scale=0.25).then_inc(mult_ready, 1)
                if n >= 2:
                    round_yb(n - 2)
            round_yb(KD - 2)
            round_yb(KD - 1)

            def round_merged(k):
                act.wait_ge(mg32, k + 1)
                act.activation(FH[:, k, :], MG[:, k, :], ACT.Copy).then_inc(mg_hi, 1)

            for n in range(KD):
                ahead("proj_lru", n)
                act.wait_ge(unit, unit_of("proj_lru", n))
                round_merged(n)
            for n in range(KD):
                ahead("mix_out", n)
                p = tile("mix_out", n)
                act.activation(Y[:, n, :], p, ACT.Copy).then_inc(y_evac, 1)
                square("mix_post", n, p)
            std("mix_post")
            for k in range(KD):
                residual_square("ffn_pre", k, k + 1)
            std("ffn_pre")
            round_hidden(8, "g1")

            c0 = taken("ffn_up_a")

            def ffn_turn(name, p0, it, first_turn, slab0):
                u0, turn = unit_of(name, 0), (0 if first_turn else it)
                for j in range(2):
                    p = it * 2 + (p0 + j)
                    for half in range(2):
                        at = p * 2 + half
                        round_slab(slab0 + 2 * j + half, turn, R)
                        act.wait_ge(unit, it * 4 + (u0 + 2 * j + half))
                        if half == 0 and not (first_turn and p0 == 0):
                            act.wait_ge(f_ready, p + (-1))
                        b = tile_bank(name, 2 * j + half)
                        act.activation(CV[:, 2 * j + half, :], b[:, 0:T], ACT.Identity,
                                       bias=C[:, dyn(at + COL["ffn_b"])], scale=C[:, dyn(at * 3 + (COL["ffn_w"] + 2))]).then_inc(conv0, 1)
                        if half == 0 and not (first_turn and j == 0):
                            act.wait_ge(f32_ready, p * 1)
                            act.activation(FH[:, dyn(it * 2 + (j - 1)), :], CV[:, 2 * ((j + 1) % 2), :], ACT.Copy).then_inc(f_hi, 1)
                    act.wait_ge(conv, p * 2 + c0)
                    act.activation(CV[:, 2 * j, :], CV[:, 2 * j, :], ACT.Gelu_apprx_tanh).then_inc(gelu_done, 1)

            def ffn_up(name, p0):
                slab0, turns = rounded[0], COUNT[name] // 4
                ffn_turn(name, p0, 0, True, slab0)
                with act.Fori(1, turns) as it:
                    ffn_turn(name, p0, it, False, slab0)
                rounded[0] += 4 * turns
                act.wait_ge(f32_ready, p0 + 2 * turns)
                act.activation(FH[:, 2 * turns - 1, :], CV[:, 2, :], ACT.Copy).then_inc(f_hi, 1)

            ffn_up("ffn_up_a", 0)
            for n in range(KD):
                ahead("ffn_down_a", n)
                act.activation(Y[:, n, :], tile("ffn_down_a", n), ACT.Copy).then_inc(evac, 1)
            ffn_up("ffn_up_b", F_TILES)
            for n in range(KD):
                ahead("ffn_down_b", n)
                act.wait_ge(y_sum, n + 1)
                square("ffn_post", n, Y[:, n, :])
            std("ffn_post")
            for k in range(KD):
                residual_square("mix2_0", k, KD + k + 1)
            std("mix2_0")
            round_hidden(16, "ffn_up_b")

            def evac_tile(name, n, out, scale=1.0, rows=slice(0, P)):
                ahead(name, n)
                act.activation(out[rows, n, :], tile(name, n)[rows, :], ACT.Copy, scale=scale).then_inc(evac, 1)

            def evac_v(name, n, v):
                ahead(name, n)
                src = tile(name, n).rearrange("p (b n) -> p b n", b=TB)
                act.activation(v[:, :, n * P:n * P + P], src, ACT.Copy).then_inc(evac, 1)

            def out_pair(pair):
                act.wait_ge(pv_mm, 2 * pair + 2)
                act.activation(FH[:, pair % 8, :], N7[:, 0:T], ACT.Copy).then_inc(o_hi, 1)

            def softmax_step(i, n0, o0, scale):
                if i < HEADS:
                    n = n0 + i
                    act.wait_ge(s_bias, n + 1)
                    for qb, (lo, cols) in enumerate(((0, P), (P, T))):
                        act.activation(S[:, n % 2, lo:lo + cols], S[:, n % 2, lo:lo + cols], ACT.Exp,
                                       bias=ST[:, n % 2, 2 + qb:3 + qb], scale=scale,
                                       accum_out=ST[:, n % 2, 4 + qb:5 + qb]).then_inc(p_exp, 1)
                if 1 <= i <= HEADS:
                    n = n0 + i - 1
                    act.wait_ge(pt_mm, n + 1)
                    if n >= 2:
                        act.wait_ge(pv_mm, o0 + i - 2)
                    act.activation(PT[:, n % 2, :], N6[:, 0:S3], ACT.Copy).then_inc(pt_ready, 1)
                if i >= 3 and i % 2:
                    out_pair((o0 + i - 3) // 2)

            ahead("fa", 0)
            softplus_exp(2, SP[0:HEADS, 2, :], SP[0:HEADS, 1, :])
            for n in range(4):
                evac_tile("q_fox", n, Q, 0.125)
            for n in range(4):
                evac_tile("k_fox", n, K)
            for n in range(4):
                evac_v("v_fox", n, V)
            for n in range(4):
                evac_tile("q_chk", n, Q2, 0.125)
                softmax_step(n, 0, 0, 1.0)
            for n in range(4):
                evac_tile("k_chk", n, K2)
                softmax_step(n + 4, 0, 0, 1.0)
            for n in range(4):
                evac_v("v_chk", n, V2)
                if n < 2:
                    softmax_step(n + 8, 0, 0, 1.0)
            for i in range(HEADS + 2):
                softmax_step(i, 8, 8, 1.0)

            def residual_layer(name, norm):
                for n in range(KD):
                    ahead(name, n)
                    if norm:
                        residual_square(norm, n, taken(name, n))
                if norm:
                    std(norm)

            residual_layer("ab_out", "mlp2_0")
            round_hidden(24, "v_chk")

            def mlp_up(name, f0):
                slab0, u0, e0 = rounded[0], unit_of(name, 0), taken(name)

                def relu(it, j, turn):
                    round_slab(slab0 + j, turn, R)
                    act.wait_ge(unit, it * 4 + (u0 + j))
                    act.wait_ge(f_ready, it * 4 + (f0 + j - 3))
                    act.activation(RT[:, j, :], tile_bank(name, j)[:, 0:T], ACT.Relu).then_inc(evac, 1)

                def round_square(it, j):
                    act.wait_ge(evac, it * 4 + (e0 + j))
                    act.activation(FH[:, dyn(it * 4 + j), :], RT[:, j % 4, :], ACT.Square).then_inc(f_hi, 1)

                with act.Fori(0, F_TILES // 4) as it:
                    for j in range(4):
                        relu(it, j, it)
                        round_square(it, j)
                rounded[0] += F_TILES

            mlp_up("mlp_up0a", FFN_PAIRS)
            for n in range(KD):
                ahead("mlp_down0a", n)
                if n == 3:
                    act.wait_ge(ang_ready, 2)
                    act.activation(SIN[64:P, :], ANG[64:P, 4, :], ACT.Sin).then_inc(sin_ready, 1)
                    act.activation(COS[64:P, :], ANG[64:P, 5, :], ACT.Sin).then_inc(sin_ready, 1)
            mlp_up("mlp_up0b", FFN_PAIRS + F_TILES)
            residual_layer("mlp_down0b", "mix2_1")
            round_hidden(32, "mlp_up0b")
            for n in range(4):
                evac_tile("q_sb", n, Q, 0.125)
            for n in range(4):
                evac_tile("k_sb", n, K)
            for n in range(4):
                evac_v("v_sb", n, V)
            act.preload_act_table_set("natural_log_exp_and_others")

            def stick_step(i):
                if i < HEADS:
                    s = S[:, i % 2, :]
                    act.wait_ge(s_mm, 16 + i + 1)
                    if i >= 2:
                        act.wait_ge(arg_mm, i - 1)
                    act.activation(s, (N5, N6)[i % 2][:, 0:S3], ACT.Abs).then_inc(z_abs, 1)
                    act.wait_ge(z_abs, i + 1)
                    act.activation(s, s, ACT.Exp, scale=-1.0).then_inc(z_exp, 1)
                    act.wait_ge(z_exp, i + 1)
                    act.activation(s, s, ACT.Ln, bias=1.0).then_inc(z_ln, 1)
                if 1 <= i <= HEADS:
                    act.wait_ge(arg_ready, i)
                    act.activation(M[:, (i - 1) % 2, :], M[:, (i - 1) % 2, :], ACT.Exp).then_inc(a_exp, 1)
                if i >= 3 and i % 2:
                    out_pair(8 + (i - 3) // 2)

            for n in range(Q_KT):
                evac_tile("c_q", n, LAT)
                act.wait_ge(evac, taken("c_q", n))
                square("q_norm", n, LAT[:, n, :])
                stick_step(n)
            for n in range(KV_KT):
                evac_tile("c_kv", n, LAT[:, Q_KT:, :])
                act.wait_ge(evac, taken("c_kv", n))
                square("kv_norm", n, LAT[:, Q_KT + n, :])
                stick_step(Q_KT + n)
            for n in range(2):
                evac_tile("k_rope", n, KR)
                stick_step(5 + n)
            std("q_norm")
            std("kv_norm")
            act.preload_act_table_set("natural_log_exp_and_others")
            stick_step(7)
            round_hidden(40, "k_rope", n=Q_KT + KV_KT, src=LAT)
            stick_step(8)
            stick_step(9)
            for n in range(HEADS):
                ahead("q_mla", n)
            for n in range(HEADS):
                evac_tile("k_mla", n, K, rows=slice(0, 64))
            for n in range(4):
                evac_v("v_mla", n, V)
            for i in range(HEADS + 2):
                softmax_step(i, 16, 24, (64 + 32) ** -0.5)
            residual_layer("cd_out", "mlp2_1")
            round_hidden(45, "v_mla")
            mlp_up("mlp_up1a", FFN_PAIRS + 2 * F_TILES)
            residual_layer("mlp_down1a", None)
            mlp_up("mlp_up1b", FFN_PAIRS + 3 * F_TILES)
            residual_layer("mlp_down1b", "final")

        @block.vector
        def _(dve):
            steps, split = [0], [0]
            stt, tt, ts = dve.scalar_tensor_tensor, dve.tensor_tensor, dve.tensor_scalar

            def link(ins):
                steps[0] += 1
                ins.then_inc(step, 1)
                dve.wait_ge(step, steps[0])

            def less(out, whole, part):
                return tt(out, whole, part.bitcast(fp32), ALU.subtract)

            def split_slab(i, turn=0, per=0):
                dve.wait_ge(hi_ready, turn * per + (i + 1))
                less(WL[:, i % R, :], RAW[:, i % R, :], WH[:, i % R, :]).then_inc(lo_ready, 1)

            def ahead(name, n):
                while split[0] < min(slab_of(name, n) + R, SLABS):
                    split_slab(split[0])
                    split[0] += 1

            def add_square(name, k):
                i = NORM[name]
                if k == 0:
                    return
                sq = lambda n: SQ[:, (SQUARES[i] + n) % SQ_SLOTS, :]
                dve.wait_ge(squared, SQUARES[i] + k + 1)
                if k == 1:
                    if i:
                        dve.wait_ge(ms_ready, i)
                    tt(ACC[:, :], sq(0), sq(1), ALU.add).then_inc(added, 1)
                else:
                    dve.wait_ge(added, ADDS[i] + k - 1)
                    tt(ACC[:, :], ACC[:, :], sq(k), ALU.add).then_inc(added, 1)

            def rstd(name):
                i = NORM[name]
                dve.wait_ge(std_ready, i + 1)
                dve.reciprocal(RS[:, i % 3, :], RS[:, i % 3, :]).then_inc(rstd_ready, 1)
                dve.wait_ge(rstd_ready, i + 1)
                return RS[:, i % 3, :]

            def low_hidden(k, base, src):
                dve.wait_ge(h_hi, base + k + 1)
                less(HL[:, k, :], src[:, k % src.shape[1], :], HH[:, k, :]).then_inc(h_ready, 1)

            def pre_norm(name, base, c=None, at=0):
                r = rstd(name)
                for k in range(KD):
                    stt(out=HT[:, k % 4, :], in0=X[:, k, :], scalar=col(c or name, at + k), in1=r, op0=ALU.mult, op1=ALU.mult).then_inc(h32, 1)
                    if k >= 1:
                        low_hidden(k - 1, base, HT)
                low_hidden(KD - 1, base, HT)

            def softplus(i, v, src, bias, scale, t, out, s, bank_taken=None):
                first = ts(v, src, scale, bias, ALU.mult, ALU.add)
                if bank_taken:
                    first.then_inc(u_taken, 1)
                    dve.wait_ge(u_taken, bank_taken)
                else:
                    link(first)
                stt(out=t[0], in0=v, scalar=-1.0, in1=v, op0=ALU.mult, op1=ALU.min).then_inc(sp_in, 1)
                dve.wait_ge(sp_exp, i + 1)
                e, p, q = t[1], t[0], t[2]
                link(ts(q, e, 2.0, None, ALU.add))
                link(dve.reciprocal(q, q))
                link(tt(e, e, q, ALU.mult))
                link(tt(q, e, e, ALU.mult))
                link(ts(p, q, 1 / 15, None, ALU.mult))
                for n in (13, 11, 9, 7, 5, 3):
                    link(stt(out=p, in0=p, scalar=1 / n, in1=q, op0=ALU.add, op1=ALU.mult))
                link(stt(out=p, in0=p, scalar=1.0, in1=e, op0=ALU.add, op1=ALU.mult))
                link(ts(v, v, 0.0, None, ALU.max))
                stt(out=out, in0=p, scalar=2.0, in1=v, op0=ALU.mult, op1=ALU.add).then_inc(s, 1)

            split_slab(0)
            split[0] = 1
            dve.wait_ge(consts_in, 16)
            pre_norm("mix_pre", 0)
            ahead("dt", 0)

            rows = slice(0, SSM_HEADS)
            dve.wait_ge(unit, unit_of("dt", 0))
            softplus(0, SP[rows, 0, :], tile_bank("dt", 0)[rows, 0:T], col("dt_bias", rows=rows), 1.0,
                     [SP[rows, 1, :], SP[rows, 2, :], SP[rows, 3, :]], DT[:, :], dt_ready, 1)
            dve.wait_ge(dt_ready, 1)
            dve.wait_ge(nega, 1)
            link(ts(SP[rows, 4, :], DT[:, :], NEGA[:, :], -1.0, ALU.mult, ALU.mult))
            dve.wait_ge(tables, ALL_TABLES)
            dve.tensor_tensor_scan(ACS[:, :], ones[rows, :], SP[rows, 4, :], 0.0, ALU.mult, ALU.add).then_inc(acs_ready, 1)

            started = [0]

            def taps(name, n, out, k=4):
                started[0] += 1
                dve.wait_ge(conv0, started[0])
                p = tile_bank(name, n)
                for back in range(1, k):
                    last = stt(out=out[:, back:T], in0=p[:, 0:T - back], scalar=col(name + "_w", k * n + k - 1 - back),
                               in1=out[:, back:T], op0=ALU.mult, op1=ALU.add)
                    if back < k - 1:
                        link(last)
                last.then_inc(conv, 1)

            for n in range(XBC_TILES):
                ahead("xbc", n)
                taps("xbc", n, A[:, n, :])
                if n == 2:
                    softplus(1, LSP[:, 0, :], col_n("lam", KD), 0.0, -1.0, [LSP[:, 1, :], LSP[:, 2, :], LSP[:, 5, :]], LSP[:, 0, :], lam_ready)
                    dve.wait_ge(lam_ready, 1)
                    link(ts(LSP[:, 3, :], LSP[:, 0, :], 4.0, None, ALU.mult))
                    ts(LSP[:, 4, :], LSP[:, 0, :], -4.0, None, ALU.mult).then_inc(lam_ready, 1)
                    for m, (name, width) in enumerate((("gate_b", 16), ("br", 8), ("bi", 8))):
                        ts(HB[:, (0, 16, 24)[m]:(0, 16, 24)[m] + width], col_n(name, width), 0.5, None, ALU.mult).then_inc(half_bias, 1)

            def turned_xs(b):
                for half in range(2):
                    dve.wait_ge(xst, 2 * b + half + 1)
                    hs = slice(8 * half, 8 * half + 8)
                    tt(XDT[:, b, hs, :], (N6, N7)[half][:, :].rearrange("p (h d) -> p h d", d=64),
                       COLS[:, b, 1, hs].unsqueeze(2).to_broadcast([P, 8, 64]), ALU.mult).then_inc(xdt_ready, 1)

            for n in range(KD):
                ahead("ly", n)
                if n == 0:
                    dve.wait_ge(colt, 1)
                    dve.tensor_copy(COLS[:, :, :, :].rearrange("p b n h -> p (b n h)"), N5[:, 0:64]).then_inc(cols_ready, 1)
                    dve.wait_ge(cols_ready, 1)
                if n == 1:
                    dve.wait_ge(cbt, 2)
                    for g in range(2):
                        tt(CBM[:, g, :], (N6, N7)[g][:, 0:S3], keep_incl[:, :], ALU.mult).then_inc(cbm_ready, 1)
                if n in (3, 5):
                    turned_xs((n - 3) // 2)

            def decay_args(h):
                dve.wait_ge(bcast, h + 1)
                ts(S[:, h % 2, 0:T], N4[:, 0:T], COLS[:, 0, 0, h:h + 1], 0.0, ALU.subtract, ALU.min)
                ts(S[:, h % 2, T:S3], N4[:, P:T], COLS[:, 1, 0, h:h + 1], 0.0, ALU.subtract, ALU.min).then_inc(seg_ready, 1)

            def decay_cb(h):
                dve.wait_ge(decay_ready, h + 1)
                if h >= 2:
                    dve.wait_ge(y_mm, h - 1)
                tt(M[:, h % 2, :], S[:, h % 2, :], CBM[:, h // 8, :], ALU.mult).then_inc(m_ready, 1)

            def skip(j):
                dve.wait_ge(y_mm, 2 * j + 2)
                stt(out=YS[:, j, :], in0=XS[:, j, :], scalar=col("skip", j), in1=(N6, N7)[j % 2][:, 0:T],
                    op0=ALU.mult, op1=ALU.add).then_inc(ys_ready, 1)

            def gate_y(j):
                dve.wait_ge(ys_ready, j + 1)
                dve.wait_ge(dve_take, taken("z", j))
                stt(out=YS[:, j, :], in0=YS[:, j, :], scalar=0.5, in1=ZS[:, j, :], op0=ALU.mult, op1=ALU.mult).then_inc(yg_ready, 1)

            for n in range(KD):
                ahead("lx", n)
                taps("lx", n, XC[:, n, :])
                decay_args(n)
                if n >= 2 and n % 2 == 0:
                    skip(n // 2 - 1)
                decay_cb(n)
            for n in range(KD):
                ahead("z", n)
                dve.wait_ge(zs_ready, n + 1)
                stt(out=ZS[:, n, :], in0=ZS[:, n, :], scalar=1.0, in1=tile_bank("z", n)[:, 0:T], op0=ALU.add, op1=ALU.mult).then_inc(dve_take, 1)
                decay_args(8 + n)
                if n % 2 == 0:
                    skip(3 + n // 2)
                if n < 7:
                    gate_y(n)
                decay_cb(8 + n)

            def recurrence_in(j):
                dve.wait_ge(rg_ready, 2 * j + 2)
                stt(out=IG[:, j, :], in0=IG[:, j, :], scalar=1.0, in1=XC[:, j, :], op0=ALU.add, op1=ALU.mult).then_inc(ix_ready, 1)

            def low_ya(k):
                dve.wait_ge(ya_hi, k + 1)
                less(FL[:, k, :], YS[:, k, :], FH[:, k, :]).then_inc(ya_ready, 1)

            for n in range(KD):
                ahead("g0", n)
                if n == 0:
                    skip(7)
                    gate_y(7)
                dve.wait_ge(evac, taken("g0", n))
                ts(G[:, n, :], G[:, n, :], 0.5, 0.5, ALU.mult, ALU.add).then_inc(g_ready, 1)
                if n in (1, 3):
                    for k in range(4):
                        add_square(("ssm0", "ssm1")[n // 2], k)
                if n in (4, 5):
                    r = rstd(("ssm0", "ssm1")[n - 4])
                    for k in range(4 * (n - 4), 4 * (n - 4) + 4):
                        stt(out=YS[:, k, :], in0=YS[:, k, :], scalar=col("ssm_norm", k), in1=r, op0=ALU.mult, op1=ALU.mult).then_inc(yn_ready, 1)
                if n >= 1:
                    recurrence_in(n - 1)
                if n in (6, 7):
                    for k in range(4):
                        low_ya(4 * (n - 6) + k)
            recurrence_in(KD - 1)
            for n in range(KD):
                ahead("proj_ssm", n)
                dve.wait_ge(ag_ready, n + 1)
                link(tt(HT[:, n % 4, :], AG[:, n, :], AG[:, n, :], ALU.mult))
                dve.wait_ge(th_ready, n + 1)
                stt(out=TH[:, n, :], in0=HT[:, n % 4, :], scalar=1.0, in1=TH[:, n, :], op0=ALU.add, op1=ALU.mult).then_inc(m2_ready, 1)
                dve.wait_ge(unit, unit_of("proj_ssm", n))
                dve.wait_ge(g_ready, n + 1)
                tt(MG[:, n, :], tile_bank("proj_ssm", n)[:, 0:T], G[:, n, :], ALU.mult).then_inc(dve_take, 1)

            def low_yb(k):
                dve.wait_ge(yb_hi, k + 1)
                less(FL[:, KD + k, :], GATE[:, k, :], FH[:, KD + k, :]).then_inc(yb_ready, 1)

            def recurrence(j):
                dve.wait_ge(mult_ready, j + 1)
                dve.wait_ge(ix_ready, j + 1)
                link(tt(IG[:, j, :], IG[:, j, :], TH[:, j, :], ALU.mult))
                link(dve.tensor_tensor_scan(XC[:, j, :], AG[:, j, :], IG[:, j, :], 0.0, ALU.mult, ALU.add))
                tt(GATE[:, j, :], XC[:, j, :], GATE[:, j, :], ALU.mult).then_inc(yb32, 1)

            for n in range(KD):
                ahead("g1", n)
                dve.wait_ge(evac, taken("g1", n))
                ts(G[:, n, :], G[:, n, :], 0.5, 0.5, ALU.mult, ALU.add).then_inc(g_ready, 1)
                if n >= 1:
                    recurrence(n - 1)
                if n >= 2:
                    low_yb(n - 2)
            recurrence(KD - 1)
            low_yb(KD - 2)
            low_yb(KD - 1)

            def low_merged(k):
                dve.wait_ge(mg_hi, k + 1)
                less(FL[:, k, :], MG[:, k, :], FH[:, k, :]).then_inc(mg_ready, 1)

            for n in range(KD):
                ahead("proj_lru", n)
                dve.wait_ge(unit, unit_of("proj_lru", n))
                dve.wait_ge(g_ready, KD + n + 1)
                tt(HT[:, n % 4, :], tile_bank("proj_lru", n)[:, 0:T], G[:, n, :], ALU.mult).then_inc(dve_take, 1)
                dve.wait_ge(dve_take, taken("proj_lru", n))
                tt(MG[:, n, :], MG[:, n, :], HT[:, n % 4, :], ALU.add).then_inc(mg32, 1)
                if n >= 1:
                    low_merged(n - 1)
            low_merged(KD - 1)

            def post_norm(name):
                r = rstd(name)
                for k in range(KD):
                    link(stt(out=Y[:, k, :], in0=Y[:, k, :], scalar=col(name, k), in1=r, op0=ALU.mult, op1=ALU.mult))
                    tt(X[:, k, :], X[:, k, :], Y[:, k, :], ALU.add).then_inc(x_ready, 1)

            for n in range(KD):
                ahead("mix_out", n)
                add_square("mix_post", n)
            post_norm("mix_post")
            pre_norm("ffn_pre", 8)

            first_start, first_conv = started[0], taken("ffn_up_a") - 1

            def low_inner(k, j, count):
                dve.wait_ge(f_hi, count)
                less(FL[:, dyn(k), :], CV[:, 2 * j, :], FH[:, dyn(k), :]).then_inc(f_ready, 1)

            def ffn_turn(name, p0, it, first_turn, slab0):
                turn = 0 if first_turn else it
                for j in range(2):
                    p = it * 2 + (p0 + j)
                    for half in range(2):
                        split_slab(slab0 + 2 * j + half, turn, R)
                        dve.wait_ge(conv0, p * 2 + (first_start + 1 + half))
                        b, out = tile_bank(name, 2 * j + half), CV[:, 2 * j + half, :]
                        for back in (1, 2):
                            last = stt(out=out[:, back:T], in0=b[:, 0:T - back], scalar=C[:, dyn((p * 2 + half) * 3 + (COL["ffn_w"] + 2 - back))],
                                       in1=out[:, back:T], op0=ALU.mult, op1=ALU.add)
                            if back == 1:
                                last.then_inc(tap_done, 1)
                                dve.wait_ge(tap_done, p * 2 + (half + 1))
                        last.then_inc(conv, 1)
                        if half == 0 and not (first_turn and j == 0):
                            low_inner(it * 2 + (j - 1), (j + 1) % 2, p * 1)
                    dve.wait_ge(gelu_done, p * 1 + 1)
                    dve.wait_ge(conv, p * 2 + (first_conv + 2))
                    tt(CV[:, 2 * j, :], CV[:, 2 * j, :], CV[:, 2 * j + 1, :], ALU.mult).then_inc(f32_ready, 1)

            def ffn_up(name, p0):
                slab0, turns = split[0], COUNT[name] // 4
                ffn_turn(name, p0, 0, True, slab0)
                with dve.Fori(1, turns) as it:
                    ffn_turn(name, p0, it, False, slab0)
                split[0] += 4 * turns
                low_inner(2 * turns - 1, 1, p0 + 2 * turns)

            ffn_up("ffn_up_a", 0)
            for n in range(KD):
                ahead("ffn_down_a", n)
            ffn_up("ffn_up_b", F_TILES)
            for n in range(KD):
                ahead("ffn_down_b", n)
                dve.wait_ge(evac, taken("ffn_down_a", n))
                dve.wait_ge(unit, unit_of("ffn_down_b", n))
                tt(Y[:, n, :], Y[:, n, :], tile_bank("ffn_down_b", n)[:, 0:T], ALU.add).then_inc(y_sum, 1)
                add_square("ffn_post", n)
            post_norm("ffn_post")
            pre_norm("mix2_0", 16, "mix2")

            rows = slice(0, HEADS)
            ts(NB[:, :], col("b_forget", rows=rows), -1.0, None, ALU.mult).then_inc(cum_ready, 1)
            ahead("fa", 0)
            dve.wait_ge(unit, unit_of("fa", 0))
            dve.wait_ge(cum_ready, 1)
            softplus(2, SP[rows, 0, :], tile_bank("fa", 0)[rows, 0:T], NB[:, :], -1.0, [SP[rows, 1, :], SP[rows, 2, :], SP[rows, 3, :]],
                     SP[rows, 4, :], cum_ready, 2)
            dve.wait_ge(cum_ready, 2)
            dve.tensor_tensor_scan(NCUM, ones[rows, :], SP[rows, 4, :], 0.0, ALU.mult, ALU.add).then_inc(cum_ready, 1)
            dve.wait_ge(cum_ready, 3)
            ts(CUM, NCUM, -1.0, None, ALU.mult).then_inc(cum_ready, 1)

            def out_pair(pair):
                dve.wait_ge(o_hi, pair + 1)
                less(FL[:, pair % 8, :], N7[:, 0:T], FH[:, pair % 8, :]).then_inc(o_ready, 1)

            def scores_max(kind, i, n0, scale):
                n = n0 + i
                dve.wait_ge(s_mm, (n if kind != "mla" else n + HEADS) + 1)
                if kind == "chk":
                    dve.wait_ge(bias_ready, i + 1)
                if n >= 2:
                    dve.wait_ge(p_norm, n - 1)
                add = {"fox": neg_causal[:, :], "mla": neg_chunk[:, :], "chk": BIAS[:, i, :]}[kind]
                b = (N4, N5)[n % 2]
                for qb, (lo, cols) in enumerate(((0, P), (P, T))):
                    dve.tensor_tensor_reduce(out=S[:, n % 2, lo:lo + cols], in0=b[:, lo:lo + cols], in1=add[:, lo:lo + cols],
                                             scale=1.0, scalar=-3.0e38, op0=ALU.add, op1=ALU.max,
                                             accum_out=ST[:, n % 2, qb:qb + 1]).then_inc(s_max, 1)
                dve.wait_ge(s_max, 2 * (n + 1))
                ts(ST[:, n % 2, 2:4], ST[:, n % 2, 0:2], -scale, None, ALU.mult).then_inc(s_bias, 1)

            def normalised(n):
                dve.wait_ge(p_exp, 2 * (n + 1))
                if n >= 2:
                    dve.wait_ge(pt_mm, n - 1)
                link(dve.reciprocal(ST[:, n % 2, 6:8], ST[:, n % 2, 4:6]))
                ts(M[:, n % 2, 0:P], S[:, n % 2, 0:P], ST[:, n % 2, 6:7], None, ALU.mult)
                ts(M[:, n % 2, P:S3], S[:, n % 2, P:S3], ST[:, n % 2, 7:8], None, ALU.mult).then_inc(p_norm, 1)

            def softmax_step(kind, i, n0, o0, scale, norm_first):
                if norm_first and 1 <= i <= HEADS:
                    normalised(n0 + i - 1)
                if i < HEADS:
                    scores_max(kind, i, n0, scale)
                if not norm_first and 1 <= i <= HEADS:
                    normalised(n0 + i - 1)
                if i >= 3 and i % 2:
                    out_pair((o0 + i - 3) // 2)

            for name in ("q_fox", "k_fox", "v_fox"):
                for n in range(4):
                    ahead(name, n)
            for m, name in enumerate(("q_chk", "k_chk", "v_chk")):
                for n in range(4):
                    ahead(name, n)
                    if 4 * m + n < HEADS + 2:
                        softmax_step("fox", 4 * m + n, 0, 0, 1.0, True)
            for i in range(HEADS + 2):
                softmax_step("chk", i, 8, 8, 1.0, False)

            def add_residual(name, norm=None):
                for n in range(COUNT[name]):
                    ahead(name, n)
                    dve.wait_ge(unit, unit_of(name, n))
                    tt(X[:, n, :], X[:, n, :], tile_bank(name, n)[:, 0:T], ALU.add).then_inc(x_ready, 1)
                    if norm and n >= 1:
                        add_square(norm, n - 1)
                if norm:
                    add_square(norm, COUNT[name] - 1)

            def mlp_up(name, f0):
                slab0 = split[0]
                with dve.Fori(0, F_TILES // 4) as it:
                    for j in range(4):
                        split_slab(slab0 + j, it, R)
                        dve.wait_ge(evac, it * 4 + (taken(name) + j))
                        dve.wait_ge(f_hi, it * 4 + (f0 + j + 1))
                        tt(RT[:, j, :], RT[:, j, :], RT[:, j, :], ALU.mult).then_inc(relu_done, 1)
                        dve.wait_ge(relu_done, it * 4 + (f0 - FFN_PAIRS + j + 1))
                        less(FL[:, dyn(it * 4 + j), :], RT[:, j, :], FH[:, dyn(it * 4 + j), :]).then_inc(f_ready, 1)
                split[0] += F_TILES

            add_residual("ab_out", "mlp2_0")
            pre_norm("mlp2_0", 24, "mlp2")
            mlp_up("mlp_up0a", FFN_PAIRS)

            hi = slice(64, P)
            ang = lambda n: ANG[hi, n, :]
            ahead("mlp_down0a", 0)
            dve.wait_ge(pos_in, 16)
            link(dve.tensor_copy(ang(0), POS[hi, :]))
            link(ts(ang(1), ang(0), col("inv_freq", rows=hi), None, ALU.mult))
            link(ts(ang(2), ang(1), 1 / TWO_PI, None, ALU.mult))
            link(ts(ang(3), ang(2), ROUND, None, ALU.add))
            link(ts(ang(2), ang(3), -ROUND, None, ALU.add))
            for n, part in enumerate(TWO_PI_PARTS):
                link(stt(out=ang((3, 1, 3)[n]), in0=ang(2), scalar=-part, in1=ang((1, 3, 1)[n]), op0=ALU.mult, op1=ALU.add))
            link(ts(ang(1), ang(3), TWO_PI / 4, None, ALU.add))
            link(ts(ang(2), ang(1), PI_DOWN, -TWO_PI, ALU.is_gt, ALU.mult))
            link(tt(ang(1), ang(1), ang(2), ALU.add))
            ts(ang(4), ang(3), PI_DOWN, -PI_DOWN, ALU.min, ALU.max).then_inc(ang_ready, 1)
            ts(ang(5), ang(1), PI_DOWN, -PI_DOWN, ALU.min, ALU.max).then_inc(ang_ready, 1)

            add_residual("mlp_down0a")
            mlp_up("mlp_up0b", FFN_PAIRS + F_TILES)
            dve.wait_ge(sin_ready, 2)
            ts(SIN[hi, :], SIN[hi, :], col("rope_sign", rows=hi), None, ALU.mult).then_inc(trig_ready, 1)
            dve.memset(TQ[0:64, :], 1.0).then_inc(trig_ready, 1)
            dve.wait_ge(trig_ready, 2)
            dve.tensor_copy(TQ[64:96, :], COS[64:96, :]).then_inc(trig_ready, 1)
            dve.tensor_copy(TQ[96:P, :], SIN[96:P, :]).then_inc(trig_ready, 1)
            add_residual("mlp_down0b", "mix2_1")
            pre_norm("mix2_1", 32, "mix2", KD)
            for name in ("q_sb", "k_sb", "v_sb"):
                for n in range(4):
                    ahead(name, n)

            def stick_step(i):
                if 1 <= i <= HEADS:
                    h, b = i - 1, (N5, N6)[(i - 1) % 2]
                    dve.wait_ge(arg_mm, h + 1)
                    if h >= 2:
                        dve.wait_ge(pv_mm, 16 + h - 1)
                    tt(M[:, h % 2, :], b[:, 0:S3], neg_strict[:, :], ALU.add).then_inc(arg_ready, 1)
                if i < HEADS:
                    h, b, s = i, (N5, N6)[i % 2], S[:, i % 2, :]
                    dve.wait_ge(z_ln, h + 1)
                    stt(out=s, in0=b[:, 0:S3], scalar=0.0, in1=s, op0=ALU.max, op1=ALU.add).then_inc(lm_ready, 1)
                    dve.wait_ge(lm_ready, 2 * h + 1)
                    tt(s, s, keep_strict[:, :], ALU.mult).then_inc(lm_ready, 1)
                if i >= 3 and i % 2:
                    out_pair(8 + (i - 3) // 2)

            for n in range(Q_KT):
                ahead("c_q", n)
                stick_step(n)
                add_square("q_norm", n)
            for n in range(KV_KT):
                ahead("c_kv", n)
                stick_step(Q_KT + n)
            for n in range(2):
                ahead("k_rope", n)
                stick_step(5 + n)
            add_square("kv_norm", 1)
            stick_step(7)
            for name, k0, n in (("q_norm", 0, Q_KT), ("kv_norm", Q_KT, KV_KT)):
                r = rstd(name)
                for k in range(n):
                    stt(out=LAT[:, k0 + k, :], in0=LAT[:, k0 + k, :], scalar=col(name, k), in1=r, op0=ALU.mult, op1=ALU.mult).then_inc(h32, 1)
            stick_step(8)
            for k in range(Q_KT + KV_KT):
                low_hidden(k, 40, LAT)
            dve.wait_ge(evac, taken("k_rope", 1))
            dve.wait_ge(trig_ready, 4)
            dve.wait_ge(s_mm, 24)
            link(tt(KF[hi, :], KR[hi, 0, :], COS[hi, :], ALU.mult))
            link(tt(KR[hi, 1, :], KR[hi, 1, :], SIN[hi, :], ALU.mult))
            link(tt(KF[hi, :], KF[hi, :], KR[hi, 1, :], ALU.add))
            stick_step(9)
            dve.tensor_copy(K[hi, :, :], KF[hi, :].unsqueeze(1).to_broadcast([64, HEADS, T])).then_inc(kcopy, 1)
            for n in range(HEADS):
                ahead("q_mla", n)
                dve.wait_ge(unit, unit_of("q_mla", n))
                tt(Q[:, n, :], tile_bank("q_mla", n)[:, 0:T], TQ, ALU.mult).then_inc(dve_take, 1)
            for name in ("k_mla", "v_mla"):
                for n in range(COUNT[name]):
                    ahead(name, n)
            for i in range(HEADS + 2):
                softmax_step("mla", i, 16, 24, (64 + 32) ** -0.5, False)
            add_residual("cd_out", "mlp2_1")
            pre_norm("mlp2_1", 45, "mlp2", KD)
            mlp_up("mlp_up1a", FFN_PAIRS + 2 * F_TILES)
            add_residual("mlp_down1a")
            mlp_up("mlp_up1b", FFN_PAIRS + 3 * F_TILES)
            add_residual("mlp_down1b", "final")
            r = rstd("final")
            for k in range(KD):
                stt(out=Y[:, k, :], in0=X[:, k, :], scalar=col("final", k), in1=r, op0=ALU.mult, op1=ALU.mult).then_inc(out_ready, 1)


def features(v):
    return np.asarray(v).reshape(-1, P).T


def blocks(w):
    k, n = w.shape
    return w.reshape(k // P, P, n // P, P).transpose(2, 0, 1, 3).reshape(-1, P, P)


def kernel(**given):
    import concourse.bacc as bacc
    from concourse.bass_utils import run_bass_kernel_spmd

    inp = {k: np.asarray(v) for k, v in given.items()}
    f32 = np.float32
    w_in = inp["w_in"][0]
    at = np.cumsum([0, 1024, 1536, 16, 1024, 1024, 2048])
    z, xbc, dt, ly, lx, g = (w_in[:, a:b] for a, b in zip(at[:-1], at[1:]))
    up = inp["w_ffn_up"][0].reshape(D, 2, FFN_PAIRS, P).transpose(0, 2, 1, 3).reshape(D, -1)
    w_ab, w_cd = inp["w_in_ab_2"][0], inp["w_in_cd_2"][0]
    at = np.cumsum([0, 512, 512, 512, 8, 512, 512, 512])
    qa, ka, va, fa, qb, kb, vb = (w_ab[:, a:b] for a, b in zip(at[:-1], at[1:]))
    at = np.cumsum([0, 512, 512, 512, 384, 256, 32])
    qc, kc, vc, cq, ckv, kr = (w_cd[:, a:b] for a, b in zip(at[:-1], at[1:]))
    swap = lambda w: np.concatenate([w[..., 16:32], w[..., 0:16]], axis=-1)
    none = np.zeros((D, 64), f32)
    rope = np.concatenate([none, kr, kr, none, swap(kr), swap(kr)], axis=1)
    uq = inp["w_uq_2"][0].reshape(-1, HEADS, 96)
    uq = np.concatenate([uq, swap(uq[..., 64:96])], axis=-1).reshape(-1, HEADS * P)
    ukv = inp["w_ukv_2"][0].reshape(-1, HEADS, P)
    uk = np.concatenate([ukv[..., 0:64], np.zeros_like(ukv[..., 0:64])], axis=-1).reshape(-1, HEADS * P)
    uv = ukv[..., 64:128].reshape(-1, HEADS * 64)
    ups, downs = inp["w_up_2"], inp["w_down_2"]
    widen = lambda w: np.pad(w, ((0, 0), (0, P - w.shape[1])))
    down = inp["w_ffn_down"][0]
    n_up, n_in = 2 * F_TILES * P, F_TILES * P

    def mlp(l):
        return [ups[l][:, :n_in], downs[l][:n_in], ups[l][:, n_in:], downs[l][n_in:]]

    weights = [widen(dt), xbc, ly, lx, z, g[:, :D], inp["w_proj_ssm"][0], g[:, D:], inp["w_proj_lru"][0], inp["w_out"][0],
               up[:, :n_up], down[:n_in], up[:, n_up:], down[n_in:], widen(fa), qa, ka, va, qb, kb, vb,
               inp["w_out_ab_2"][0], *mlp(0), qc, kc, vc, cq, ckv, rope, uq, uk, uv, inp["w_out_cd_2"][0], *mlp(1)]
    for w, (name, count, depth) in zip(weights, LAYERS, strict=True):
        assert w.shape == (depth * P, count * P), (name, w.shape)
    stream = np.concatenate([blocks(w) for w in weights])
    assert len(stream) == SLABS * BLOCKS
    stream = stream.reshape(SLABS, BLOCKS, P, P).transpose(0, 2, 1, 3).reshape(SLABS, P, BLOCKS * P)

    consts = np.zeros((P, NCOL), f32)

    def put(name, v, row=0):
        consts[row:row + v.shape[0], COL[name]:COL[name] + v.shape[1]] = v

    def taps(w):
        return w.reshape(len(w), -1, P).transpose(2, 1, 0).reshape(P, -1)

    by_turns = lambda v: v.reshape(-1, 2, FFN_PAIRS, P).transpose(0, 2, 1, 3).reshape(len(v), -1)
    put("mix_pre", features(inp["mix_pre_norm"]))
    put("mix_post", features(inp["mix_post_norm"]))
    put("xbc_w", taps(inp["ssm_conv_w"][0]))
    put("xbc_b", features(inp["ssm_conv_b"]))
    put("skip", features(np.repeat(inp["ssm_d"][0], 64)))
    put("ssm_norm", features(inp["ssm_norm"]))
    put("lx_w", taps(inp["lru_conv_w"][0]))
    put("lx_b", features(inp["lru_conv_b"]))
    put("br", features(inp["lru_br"]))
    put("bi", features(inp["lru_bi"]))
    put("lam", features(inp["lru_lambda"]))
    put("gate_b", features(inp["gate_b"]))
    put("ffn_pre", features(inp["ffn_pre_norm"]))
    put("ffn_post", features(inp["ffn_post_norm"]))
    put("ffn_w", taps(by_turns(inp["ffn_conv_w"][0])))
    put("ffn_b", features(by_turns(inp["ffn_conv_b"])))
    put("mix2", features(inp["norm_mix_2"]))
    put("mlp2", features(inp["norm_mlp_2"]))
    put("final", features(inp["norm_final_2"]))
    put("q_norm", features(inp["q_norm_2"]))
    put("kv_norm", features(inp["kv_norm_2"]))
    put("dt_bias", inp["ssm_dt_bias"].T)
    put("a_log", inp["ssm_a_log"].T)
    put("b_forget", inp["b_forget_2"].T)
    half = 16
    inv_freq = (f32(10000.0) ** (-np.arange(half, dtype=f32) / f32(half))).astype(f32)
    put("inv_freq", np.tile(inv_freq, 4)[:, None], 64)
    put("rope_sign", np.tile(np.repeat(np.array([-1, 1], f32), half), 2)[:, None], 64)

    q, k = np.arange(P)[:, None], np.arange(P)[None, :]
    rel = np.concatenate([q - k, q + P - k, q - k], axis=1) + CHUNK - 1
    rel = inp["rel_bias_2"][0][:, np.clip(rel, 0, N_REL - 1)].transpose(1, 0, 2)

    diag = lambda w: w.reshape(KD, 2, 64, 64).transpose(1, 2, 0, 3)
    arrays = dict(
        x_t=inp["x"][0].T.reshape(KD, P, T).transpose(1, 0, 2), consts=consts, positions=inp["positions_2"].astype(np.int32),
        stream=stream, lru_r=diag(inp["lru_wr"][0]), lru_i=diag(inp["lru_wi"][0]), rel=rel)
    nc = bacc.Bacc("TRN2", target_bir_lowering=False, num_devices=1)
    arrays = {n: np.ascontiguousarray(v) for n, v in arrays.items()}
    aps = {n: nc.dram_tensor(f"in_{n}", v.shape, mybir.dt.from_np(v.dtype), kind="ExternalInput").ap() for n, v in arrays.items()}
    out = nc.dram_tensor("out_t", (P, KD, T), mybir.dt.float32, kind="ExternalOutput").ap()
    build(nc, out_t=out, **aps)
    r = run_bass_kernel_spmd(nc, [{f"in_{n}": v for n, v in arrays.items()}], core_ids=[0])
    got = r.results[0]["out_t"]
    return np.ascontiguousarray(got.transpose(2, 1, 0).reshape(1, T, D))
```

```python
import concourse.bass as bass
import numpy as np
from concourse import mybir

P = 128
T = 256
TB = T // P
D = 1024
KD = D // P
EPS = 1e-6
NEG = -1.0e30
CHUNK = 64

SSM_TILES = 8
XBC_TILES = 12
SSM_HEADS = 16
FFN_PAIRS = 24
MLP_TILES = 32
F_TILES = 16
HEADS = 8
N_REL = 320
Q_KT, KV_KT = 3, 2

R = 4
BLOCKS = 8
BANKS = 4
S3 = 3 * P


LAYERS = [
    ("dt", 1, KD), ("xbc", XBC_TILES, KD), ("ly", KD, KD), ("lx", KD, KD), ("z", KD, KD), ("g0", KD, KD),
    ("proj_ssm", KD, KD), ("g1", KD, KD), ("proj_lru", KD, KD), ("mix_out", KD, KD),
    ("ffn_up_a", 2 * F_TILES, KD), ("ffn_down_a", KD, F_TILES),
    ("ffn_up_b", 2 * (FFN_PAIRS - F_TILES), KD), ("ffn_down_b", KD, FFN_PAIRS - F_TILES),
    ("fa", 1, KD), ("q_fox", 4, KD), ("k_fox", 4, KD), ("v_fox", 4, KD),
    ("q_chk", 4, KD), ("k_chk", 4, KD), ("v_chk", 4, KD), ("ab_out_a", KD, 4), ("ab_out_b", KD, 4),
    ("mlp_up0a", F_TILES, KD), ("mlp_down0a", KD, F_TILES), ("mlp_up0b", F_TILES, KD), ("mlp_down0b", KD, F_TILES),
    ("c_q", Q_KT, KD), ("c_kv", KV_KT, KD), ("q_sb", 4, KD), ("k_sb", 4, KD), ("v_sb", 4, KD), ("k_rope", 2, KD),
    ("q_mla", HEADS, Q_KT), ("k_mla", HEADS, KV_KT), ("v_mla", 4, KV_KT), ("cd_out_a", KD, 4), ("cd_out_b", KD, 4),
    ("mlp_up1a", F_TILES, KD), ("mlp_down1a", KD, F_TILES), ("mlp_up1b", F_TILES, KD), ("mlp_down1b", KD, F_TILES),
]


def plan():
    first, tiles, block, units, last_unit = {}, [], 0, 0, {}
    for name, count, depth in LAYERS:
        first[name] = len(tiles)
        for _ in range(count):
            pieces = []
            for k in range(depth):
                slab = block // BLOCKS
                if not pieces or pieces[-1][0] != slab:
                    pieces.append((slab, []))
                pieces[-1][1].append((block % BLOCKS, k))
                block += 1
            units += len(pieces)
            for n, (slab, _) in enumerate(pieces):
                last_unit[slab] = units - len(pieces) + n + 1
            tiles.append((pieces, units, depth))
    return first, tiles, -(-block // BLOCKS), last_unit


FIRST, TILES, SLABS, LAST_UNIT = plan()
COUNT = {name: count for name, count, _ in LAYERS}


def columns():
    at, n = {}, 0
    for name, width in [
        ("mix_pre", 8), ("mix_post", 8), ("xbc_w", 48), ("xbc_b", 12), ("skip", 8), ("ssm_norm", 8), ("lx_w", 32),
        ("lx_b", 8), ("br", 8), ("bi", 8), ("lam", 8), ("gate_b", 16), ("ffn_pre", 8), ("ffn_post", 8),
        ("ffn_w", 3 * 48), ("ffn_b", 48), ("mix2", 16), ("mlp2", 16), ("final", 8), ("q_norm", 3), ("kv_norm", 2),
        ("dt_bias", 1), ("a_log", 1), ("b_forget", 1), ("inv_freq", 1), ("rope_sign", 1),
    ]:
        at[name] = n
        n += width
    return at, n


COL, NCOL = columns()

TWO_PI = 6.283185307179586
TWO_PI_PARTS = (6.28125, 0.0019340515136718750, TWO_PI - 6.28125 - 0.0019340515136718750)
PI_DOWN = 3.1415925
ROUND = 12582912.0

NORMS = [
    ("mix_pre", 8, 1 / D), ("ssm0", 4, 2 / D), ("ssm1", 4, 2 / D), ("mix_post", 8, 1 / D), ("ffn_pre", 8, 1 / D),
    ("ffn_post", 8, 1 / D), ("mix2_0", 8, 1 / D), ("mlp2_0", 8, 1 / D), ("mix2_1", 8, 1 / D),
    ("q_norm", Q_KT, 1 / (Q_KT * P)), ("kv_norm", KV_KT, 1 / (KV_KT * P)), ("mlp2_1", 8, 1 / D), ("final", 8, 1 / D),
]
NORM = {name: i for i, (name, _, _) in enumerate(NORMS)}
DIRECT = ("mix_pre", "ffn_pre", "mix2_0", "mlp2_0", "mlp2_1")
ADDS = [sum(n - 1 for name, n, _ in NORMS[:i] if name not in DIRECT) for i in range(len(NORMS) + 1)]
PARTS = [sum(n - 1 for name, n, _ in NORMS[:i] if name in DIRECT) for i in range(len(NORMS) + 1)]
SQ_SLOTS = 4
SQUARES = [sum(n for _, n, _ in NORMS[:i]) for i in range(len(NORMS) + 1)]


def build(nc, x_t, consts, positions, stream, lru_r, lru_i, rel, out_t):
    fp32, fp32r, bf16, i32 = mybir.dt.float32, mybir.dt.float32r, mybir.dt.bfloat16, mybir.dt.int32
    ALU, ACT = mybir.AluOpType, mybir.ActivationFunctionType
    sb = lambda name, *shape, dt=fp32: nc.alloc_sbuf_tensor(name, list(shape), dt)

    RAW = sb("weights_raw", P, R, BLOCKS * P)
    WH = sb("weights_hi", P, R, BLOCKS * P, dt=fp32r)
    WL = sb("weights_lo", P, R, BLOCKS * P, dt=fp32r)
    C = sb("consts", P, NCOL)
    X = sb("residual", P, KD, T)
    HH, HL = (sb(f"hidden_{part}", P, KD, T, dt=fp32r) for part in ("hi", "lo"))
    FH, FL = (sb(f"inner_{part}", P, F_TILES, T, dt=fp32r) for part in ("hi", "lo"))
    SQ = sb("squares", P, SQ_SLOTS, T)
    ACC = sb("square_sum", P, T)
    RS = sb("rstd", P, 3, T)
    A = sb("arena", P, 72, T)
    ident = sb("ident", P, P)
    ones = sb("ones", P, T)
    keep_incl = sb("keep_incl", P, S3, dt=bf16)
    keep_strict = sb("keep_strict", P, S3, dt=bf16)
    neg_strict = sb("neg_strict", P, S3, dt=bf16)
    neg_causal = sb("neg_causal", P, S3, dt=bf16)
    neg_chunk = sb("neg_chunk", P, S3, dt=bf16)
    neg_tri = sb("neg_tri", P, P)
    neg_one = sb("neg_one", P, P)
    S = sb("scores", P, 2, S3)
    M = sb("weights", P, 2, S3)
    PT = sb("weights_turned", P, 2, S3)
    ST = sb("stats", P, 2, 8)
    POS = sb("positions_sb", P, T, dt=i32)
    EPSC = sb("eps_column", P, 1)
    a = lambda lo, n: A[:, lo:lo + n, :]
    flat = lambda lo, n: A[:, lo:lo + n, :].rearrange("p a t -> p (a t)")
    XS, BC, XC, GATE, ZS, G = a(0, 8), a(8, 4), a(12, 8), a(20, 8), a(28, 8), a(36, 8)
    CBM = flat(8, 3).rearrange("p (g n) -> p g n", g=2)
    XDT = flat(44, 8).rearrange("p (b h d) -> p b h d", b=TB, d=64)
    YS, IG = a(52, 8), a(60, 8)
    TH, AG = XS, a(44, 8)
    MG = ZS
    Y = XC
    HT = a(68, 4)
    BLKR, BLKI = IG[:, :, 0:P], IG[:, :, P:T]
    CV = a(28, 4)
    SP = a(51, 5)
    Q, K = a(0, 8), a(8, 8)
    V = flat(16, 4).rearrange("p (b n) -> p b n", b=TB)
    Q2, K2 = a(20, 4), a(24, 4)
    V2 = flat(28, 4).rearrange("p (b n) -> p b n", b=TB)
    AQ, BK = a(32, 4), a(36, 4)
    CUM, NCUM = A[0:HEADS, 40, :], A[0:HEADS, 41, :]
    LAT = a(42, 5)
    KF, TQ, COS, SIN, KR, ANG = A[:, 47, :], A[:, 48, :], A[:, 49, :], A[:, 50, :], a(51, 2), a(20, 6)
    BIAS = flat(56, 12).rearrange("p (h n) -> p h n", n=S3)
    RT = a(0, 4)
    DT, ACS = sb("dt_steps", 16, T), sb("a_cumsum", 16, T)
    NEGA = sb("neg_a", 16, 1)
    COLS = sb("dt_columns", P, TB, 2, SSM_HEADS)
    LSP = sb("lru_softplus", P, 6, KD)
    HB = sb("half_biases", P, 32)
    NB = sb("neg_b_forget", HEADS, 1)

    bank = [nc.alloc_psum_tensor(f"bank{i}", [P, 512], fp32) for i in range(8)]
    N4, N5, N6, N7 = bank[4:]

    def sems(names):
        return [nc.alloc_semaphore(name) for name in names.split()]

    slab_in = [nc.alloc_semaphore(f"slab_in{s}") for s in range(R)]
    consts_in, blk_in, bias_in, pos_in = sems("consts_in blk_in bias_in pos_in")
    x_in = sems("x_in0 x_in1")
    tables, blk_zero, bias_ready = sems("tables blk_zero bias_ready")
    unit, = sems("unit_done")
    hi_ready, = sems("weights_hi_ready")
    lo_ready = [nc.alloc_semaphore(f"weights_lo_ready{s}") for s in range(R)]
    squared, added, ms_part, ms_ready = sems("squared squares_added ms_part ms_ready")
    std_ready, rstd_ready = sems("std_ready rstd_ready")
    h32, h_hi, h_ready, x_ready, step = sems("h_float32 h_hi h_ready x_ready dve_step")
    evac, conv, conv0, act_in, dve_take, y_evac = sems("evac conv_done conv_started act_in_place dve_take y_evac")
    tap_done, u_taken, y_sum = sems("tap_done u_taken y_sum")
    sp_in, sp_exp, dt_ready, nega, acs_ready = sems("softplus_in softplus_exp dt_ready neg_a acs_ready")
    colt, cols_ready, xst, xdt_ready, cbt, cbm_ready = sems("colt cols_ready xs_turned xdt_ready cb_done cbm_ready")
    bcast, seg_ready, decay_ready, m_ready, y_mm = sems("acs_broadcast seg_ready decay_ready m_ready y_mm")
    ys_ready, yg_ready, yn_ready, ya_hi, ya_ready = sems("ys_ready yg_ready yn_ready ya_hi ya_ready")
    lam_ready, half_bias, rg_mm, rg_ready, ag_ready, th_ready = sems("lam_ready half_bias rg_mm rg_ready ag_ready th_ready")
    m2_ready, ix_ready, mult_ready, bx_ready, scanned = sems("m2_ready ix_ready mult_ready bx_ready scanned")
    y_normed, = sems("y_normed")
    yb32, yb_hi, yb_ready, mg32, mg_hi, mg_ready = sems("yb_float32 yb_hi yb_ready merged_float32 merged_hi merged_ready")
    gelu_done, f32_ready, f_hi, f_ready = sems("gelu_done f_float32 f_hi f_ready")
    relu_done, zs_ready = sems("relu_done zs_ready")
    cum_ready, dtile_zero, dtile_in = sems("cum_ready dtile_zero dtile_in")
    s_mm, s_max, s_bias, p_exp, p_norm, pt_mm = sems("scores_done scores_max exp_bias weights_exp weights_normed turned")
    pt_ready, pv_mm, o_hi, o_ready = sems("turned_out pv_done heads_hi heads_out")
    z_abs, z_exp, z_ln, lm_ready, arg_mm, arg_ready, a_exp = sems("z_abs z_exp z_ln lm_ready arg_mm arg_ready a_exp")
    ang_ready, sin_ready, trig_ready, kcopy = sems("ang_ready sin_ready trig_ready kcopy")
    out_ready, stored = sems("out_ready stored")

    FREE, counts = {}, {x_ready: 2 * KD}

    def frees(layer, s):
        for n in range(COUNT[layer]):
            counts[s] = counts.get(s, 0) + 1
            FREE[FIRST[layer] + n] = (s, counts[s])

    def taken(layer, n=0):
        return FREE[FIRST[layer] + n][1]

    for names, s in [("dt", u_taken), ("xbc", conv), ("ly", evac), ("lx", conv), ("z", dve_take), ("g0", evac),
                     ("proj_ssm", dve_take), ("g1", evac), ("proj_lru", dve_take), ("ffn_up_a", conv),
                     ("ffn_down_a", evac), ("ffn_up_b", conv), ("ffn_down_b", y_sum), ("fa", u_taken),
                     ("q_fox k_fox v_fox q_chk k_chk v_chk", evac), ("ab_out_a ab_out_b", x_ready), ("mlp_up0a", evac),
                     ("mlp_down0a", x_ready), ("mlp_up0b", evac), ("mlp_down0b", x_ready),
                     ("c_q c_kv q_sb k_sb v_sb k_rope", evac), ("q_mla", dve_take), ("k_mla v_mla", evac),
                     ("cd_out_a cd_out_b", x_ready), ("mlp_up1a", evac), ("mlp_down1a", x_ready), ("mlp_up1b", evac),
                     ("mlp_down1b", x_ready)]:
        for name in names.split():
            frees(name, s)
    for n in range(KD):
        FREE[FIRST["mix_out"] + n] = (squared, SQUARES[NORM["mix_post"]] + n + 1)

    def col(name, n=0, rows=slice(0, P)):
        return C[rows, COL[name] + n:COL[name] + n + 1]

    def col_n(name, n):
        return C[:, COL[name]:COL[name] + n]

    def dyn(i):
        return slice(i, i + 1) if isinstance(i, int) else bass.ds(i, 1)

    def tile_bank(layer, n):
        return bank[(FIRST[layer] + n) % BANKS]

    def unit_of(layer, n):
        return TILES[FIRST[layer] + n][1]

    def slab_of(layer, n):
        return TILES[FIRST[layer] + n][0][-1][0]

    def square_used(q):
        i = max(i for i in range(len(NORMS)) if SQUARES[i] <= q)
        name, n, _ = NORMS[i]
        k = q - SQUARES[i]
        if name not in DIRECT:
            return added, ADDS[i] + max(k, 1)
        return (ms_ready, i + 1) if k == n - 1 else (ms_part, PARTS[i] + k + 1)

    ALL_TABLES = 22

    block = nc.Block()
    with block:
        @block.sync
        def _(sp):
            for half in range(2):
                sp.dma_start(X[:, 4 * half:4 * half + 4, :], x_t[:, 4 * half:4 * half + 4, :]).then_inc(x_in[half], 16)
            sp.dma_start(C[:, :], consts).then_inc(consts_in, 16)
            for s in range(R):
                sp.dma_start(RAW[:, s, :], stream[s]).then_inc(slab_in[s], 16)
            turns = SLABS // R

            def reload(turn, s):
                sp.wait_ge(lo_ready[s], turn * 1)
                sp.dma_start(RAW[:, s, :], stream[turn * R + s]).then_inc(slab_in[s], 16)

            middle = (slab_of("k_fox", 0) + 2 * R) // R
            with sp.Fori(1, middle) as it:
                for s in range(R):
                    reload(it, s)
            for s in range(R):
                reload(middle, s)
                if s == 0:
                    sp.wait_ge(dtile_zero, 6)
                    sp.wait_ge(cum_ready, 4)
                for h in range(2 * s, 2 * s + 2):
                    row = 64 * (h % 2)
                    sp.dma_start(AQ[row + 1:row + 2, h // 2, :], CUM[h:h + 1, :]).then_inc(dtile_in, 16)
                    sp.dma_start(BK[row:row + 1, h // 2, :], NCUM[h:h + 1, :]).then_inc(dtile_in, 16)
            with sp.Fori(middle + 1, turns) as it:
                for s in range(R):
                    reload(it, s)
            for i in range(R * turns, SLABS):
                sp.wait_ge(lo_ready[i % R], i // R)
                sp.dma_start(RAW[:, i % R, :], stream[i]).then_inc(slab_in[i % R], 16)
            for k in range(KD):
                sp.wait_ge(out_ready, k + 1)
                sp.dma_start(out_t[:, k, :], Y[:, k, :]).then_inc(stored, 16)
            sp.wait_ge(stored, 16 * KD)

        @block.gpsimd
        def _(pool):
            pool.dma_start(POS[:, :], positions.to_broadcast([P, T])).then_inc(pos_in, 16)
            for tile, value in ((ones, 1.0), (EPSC, EPS)):
                pool.memset(tile[:, :], value).then_inc(tables, 1)
            pool.memset(BLKR, 0.0).then_inc(blk_zero, 1)
            pool.memset(BLKI, 0.0).then_inc(blk_zero, 1)
            pool.wait_ge(blk_zero, 2)
            for dst, src in ((BLKR, lru_r), (BLKI, lru_i)):
                for half in range(2):
                    rows = slice(64 * half, 64 * half + 64)
                    pool.dma_start(dst[rows, :, rows], src[half]).then_inc(blk_in, 16)
            fills = [(ident, 0.0), (keep_incl, 1.0), (keep_strict, 1.0), (neg_strict, 0.0),
                     (neg_causal, 0.0), (neg_chunk, 0.0), (neg_tri, -1.0), (neg_one, -1.0)]
            for tile, value in fills:
                pool.memset(tile[:, :], value).then_inc(tables, 1)
            pool.wait_ge(tables, 2 + len(fills))
            pool.affine_select(out=ident[:, :], in_=ident[:, :], compare_op=ALU.not_equal, fill=1.0, base=0,
                               pattern=[[-1, P]], channel_multiplier=1).then_inc(tables, 1)
            for tile, fill, base, row, colm in [(keep_incl, 0.0, 0, -1, 1), (keep_strict, 0.0, -1, -1, 1),
                                                (neg_strict, NEG, -1, -1, 1), (neg_causal, NEG, 0, 1, -1)]:
                for d in (0, 2):
                    part = tile[:, d * P:d * P + P]
                    pool.affine_select(out=part, in_=part, compare_op=ALU.is_ge, fill=fill, base=base,
                                       pattern=[[colm, P]], channel_multiplier=row).then_inc(tables, 1)
            for d in (0, 2):
                part = neg_chunk[:, d * P + CHUNK:d * P + P]
                pool.affine_select(out=part, in_=part, compare_op=ALU.is_ge, fill=NEG, base=-CHUNK,
                                   pattern=[[0, CHUNK]], channel_multiplier=1).then_inc(tables, 1)
            pool.affine_select(out=neg_tri[:, :], in_=neg_tri[:, :], compare_op=ALU.is_ge, fill=0.0, base=0,
                               pattern=[[-1, P]], channel_multiplier=1).then_inc(tables, 1)
            split = [R - 1]

            def split_slab(i, turn=0):
                pool.wait_ge(hi_ready, turn * R + (i + 1))
                pool.tensor_tensor(WL[:, R - 1, :], RAW[:, R - 1, :], WH[:, R - 1, :].bitcast(fp32), ALU.subtract).then_inc(lo_ready[R - 1], 1)

            def ahead(name, n):
                while split[0] < min(slab_of(name, n) + R, SLABS):
                    split_slab(split[0])
                    split[0] += R

            def through(name):
                turns = (min(slab_of(name, COUNT[name] - 1) + R, SLABS) - split[0] + R - 1) // R
                with pool.Fori(0, turns) as it:
                    split_slab(split[0], it)
                split[0] += R * turns

            through("proj_ssm")

            def recurrence_out(j):
                pool.wait_ge(scanned, j + 1)
                pool.tensor_tensor(GATE[:, j, :], XC[:, j, :], GATE[:, j, :], ALU.mult).then_inc(yb32, 1)

            for n in range(KD):
                ahead("g1", n)
                pool.wait_ge(mult_ready, n + 1)
                pool.wait_ge(ix_ready, n + 1)
                pool.tensor_tensor(IG[:, n, :], IG[:, n, :], TH[:, n, :], ALU.mult).then_inc(bx_ready, 1)
                if n >= 1:
                    recurrence_out(n - 1)
            recurrence_out(KD - 1)
            for n in range(KD):
                ahead("proj_lru", n)
                pool.wait_ge(dve_take, taken("proj_lru", n))
                pool.tensor_tensor(MG[:, n, :], MG[:, n, :], HT[:, n % 4, :], ALU.add).then_inc(mg32, 1)
            through("mix_out")

            def post_add():
                for k in range(KD):
                    pool.wait_ge(y_normed, posts[0] + k + 1)
                    pool.tensor_tensor(X[:, k, :], X[:, k, :], Y[:, k, :], ALU.add).then_inc(x_ready, 1)
                posts[0] += KD

            posts = [0]
            post_add()
            pool.dma_start(BIAS, rel).then_inc(bias_in, 16)
            for h in range(HEADS):
                ahead("ffn_up_a", R * h)
                pool.wait_ge(bias_in, 16)
                pool.tensor_tensor(BIAS[:, h, :], BIAS[:, h, :], neg_chunk[:, :], ALU.add).then_inc(bias_ready, 1)
            through("ffn_up_a")
            pool.memset(AQ, 0.0).then_inc(dtile_zero, 1)
            ahead("ffn_down_a", 1)
            pool.memset(BK, 0.0).then_inc(dtile_zero, 1)
            ahead("ffn_down_a", 3)
            pool.wait_ge(dtile_zero, 2)
            pool.wait_ge(lo_ready[R - 1], split[0] // R)
            for base in (0, 64):
                pool.memset(AQ[base:base + 2], 1.0).then_inc(dtile_zero, 1)
                pool.memset(BK[base:base + 2], 1.0).then_inc(dtile_zero, 1)
            pool.wait_ge(dtile_zero, 6)
            through("ffn_down_b")
            post_add()
            through("mlp_down1b")

        @block.tensor
        def _(pe):
            def block_products(out, slot, blk, hi, lo, first, last, half=None):
                cols = slice(blk * P, blk * P + P)
                for n, (w, x) in enumerate(((WH, hi), (WH, lo), (WL, hi))):
                    w = w[:, slot, cols]
                    lhs, rhs = (w, x) if half is None else (x[:, half * P:half * P + P], w)
                    mm = pe.matmul(out, lhs, rhs, start=(first and n == 0), stop=(last and n == 2))
                return mm

            def dense_tile(t, hi, lo, token_major=False, ready=None):
                pieces, _, depth = TILES[t]
                b = bank[t % BANKS]
                if t >= BANKS:
                    pe.wait_ge(*FREE[t - BANKS])
                halves = range(TB) if token_major else (None,)
                assert not token_major or len(pieces) == 1
                for slab, blocks in pieces:
                    pe.wait_ge(lo_ready[slab % R], slab // R + 1)
                    for half in halves:
                        out = b[:, 0:T] if half is None else b[:, half * P:half * P + P]
                        for blk, k in blocks:
                            if ready:
                                pe.wait_ge(ready[0], ready[1] + k + 1)
                            mm = block_products(out, slab % R, blk, hi[:, k, :], lo[:, k, :], k == 0, k == depth - 1, half)
                    mm.then_inc(unit, 1)

            in_front = set()

            def front(name, hi, lo, ready, count=3):
                tiles = range(FIRST[name], FIRST[name] + count)
                in_front.update(tiles)
                for t in tiles:
                    if t >= BANKS:
                        pe.wait_ge(*FREE[t - BANKS])
                for k in range(KD):
                    pe.wait_ge(ready[0], ready[1] + k + 1)
                    for t in tiles:
                        slab, blocks = TILES[t][0][0]
                        if k == 0:
                            pe.wait_ge(lo_ready[slab % R], slab // R + 1)
                        mm = block_products(bank[t % BANKS][:, 0:T], slab % R, blocks[k][0], hi[:, k, :], lo[:, k, :], k == 0, k == KD - 1)
                        if k == KD - 1:
                            mm.then_inc(unit, 1)

            def layer(name, hi, lo, hooks=None, ready=None, **kw):
                for n in range(COUNT[name]):
                    if FIRST[name] + n not in in_front:
                        dense_tile(FIRST[name] + n, hi, lo, ready=ready if n == 0 else None, **kw)
                    if hooks and n in hooks:
                        hooks[n]()

            def loop_layer(name, hi, lo, per, ready=None):
                t0, depth = FIRST[name], TILES[FIRST[name]][2]
                slabs = depth // BLOCKS
                s0 = TILES[t0][0][0][0]
                assert per * slabs % R == 0 and per % BANKS == 0 and COUNT[name] % per == 0
                own, first_taken = FREE[t0]
                for n in range(per):
                    if t0 + n not in in_front:
                        dense_tile(t0 + n, hi, lo, ready=ready if n == 0 else None)
                if COUNT[name] == per:
                    return
                with pe.Fori(1, COUNT[name] // per) as it:
                    for j in range(per):
                        pe.wait_ge(own, it * per + (first_taken + j - BANKS))
                        for s in range(slabs):
                            slab = s0 + j * slabs + s
                            pe.wait_ge(lo_ready[slab % R], it * (per * slabs // R) + (slab // R + 1))
                            for blk in range(BLOCKS):
                                k = s * BLOCKS + blk
                                mm = block_products(bank[(t0 + j) % BANKS][:, 0:T], slab % R, blk, hi[:, k, :], lo[:, k, :],
                                                    k == 0, k == depth - 1)
                            mm.then_inc(unit, 1)

            def mean_square(name):
                i = NORM[name]
                if i:
                    pe.wait_ge(std_ready, i)
                if name not in DIRECT:
                    pe.wait_ge(added, ADDS[i + 1])
                    pe.matmul(N4[:, 0:T], ones[:, 0:P], ACC[:, :], start=True, stop=True).then_inc(ms_ready, 1)
                    return
                n = NORMS[i][1]
                for k in range(n):
                    pe.wait_ge(squared, SQUARES[i] + k + 1)
                    mm = pe.matmul(N4[:, 0:T], ones[:, 0:P], SQ[:, (SQUARES[i] + k) % SQ_SLOTS, :], start=(k == 0), stop=(k == n - 1))
                    mm.then_inc(ms_ready if k == n - 1 else ms_part, 1)

            pe.wait_ge(tables, 2)
            mean_square("mix_pre")
            front("dt", HH, HL, (h_ready, 0))
            layer("xbc", HH, HL)

            def dt_columns():
                pe.wait_ge(acs_ready, 1)
                pe.wait_ge(tables, ALL_TABLES)
                for b in range(TB):
                    for n, src in enumerate((ACS, DT)):
                        mm = pe.matmul(N5[:, (2 * b + n) * 16:(2 * b + n) * 16 + 16], src[:, b * P:b * P + P],
                                       ident[0:16, 0:16], start=True, stop=True)
                mm.then_inc(colt, 1)

            def cb():
                pe.wait_ge(act_in, XBC_TILES)
                for g in range(2):
                    b, bt, ct = (N6, N7)[g], BC[:, g, :], BC[:, 2 + g, :]
                    pe.matmul(b[:, 0:T], bt[:, 0:P], ct, start=True, stop=True)
                    pe.matmul(b[:, T:S3], bt[:, P:T], ct[:, P:T], start=True, stop=True).then_inc(cbt, 1)

            def turn_xs(b):
                pe.wait_ge(cbm_ready, 2)
                if b:
                    pe.wait_ge(xdt_ready, 2 * b)
                for j in range(SSM_TILES):
                    mm = pe.transpose((N6, N7)[j // 4][:, (j % 4) * P:(j % 4) * P + P], XS[:, j, b * P:b * P + P], ident[:, :])
                    if j % 4 == 3:
                        mm.then_inc(xst, 1)

            def lru_gates(j):
                if j == 0:
                    pe.wait_ge(blk_in, 64)
                    pe.wait_ge(conv, XBC_TILES + KD)
                else:
                    pe.wait_ge(rg_ready, 2 * j)
                b = N5
                pe.matmul(b[:, 0:T], BLKR[:, j, :], XC[:, j, :], start=True, stop=True)
                pe.matmul(b[:, T:2 * T], BLKI[:, j, :], XC[:, j, :], start=True, stop=True).then_inc(rg_mm, 1)

            def head_bcast(h):
                if h >= 1:
                    pe.wait_ge(seg_ready, h)
                pe.matmul(N4[:, 0:T], ident[0:16, h:h + 1].to_broadcast([16, P]), ACS[:, :],
                          start=True, stop=True).then_inc(bcast, 1)

            def head_y(h):
                pe.wait_ge(m_ready, h + 1)
                if h >= 4 and h % 2 == 0:
                    pe.wait_ge(ys_ready, h // 2 - 1)
                b, rows = (N6, N7)[h // 2 % 2], slice(64 * (h % 2), 64 * (h % 2) + 64)
                pe.matmul(b[rows, 0:T], XDT[:, 0, h, :], M[:, h % 2, 0:T], start=True, stop=False)
                pe.matmul(b[rows, P:T], XDT[:, 1, h, :], M[:, h % 2, T:S3], start=False, stop=True).then_inc(y_mm, 1)

            def heads(n):
                if n < SSM_HEADS:
                    head_bcast(n)
                if n >= 1:
                    head_y(n - 1)

            layer("ly", HH, HL, {0: dt_columns, 1: cb, 3: lambda: turn_xs(0), 5: lambda: turn_xs(1)})
            pe.wait_ge(cols_ready, 1)
            pe.wait_ge(xdt_ready, 4)
            layer("lx", HH, HL, {n: (lambda n=n: heads(n)) for n in range(8)})
            layer("z", HH, HL, {n: (lambda n=n: heads(n + 8)) for n in range(8)})

            def after_g0(n):
                if n == 0:
                    heads(SSM_HEADS)
                if n == 3:
                    mean_square("ssm0")
                if n == 4:
                    mean_square("ssm1")
                lru_gates(n)

            layer("g0", HH, HL, {n: (lambda n=n: after_g0(n)) for n in range(8)})
            layer("proj_ssm", FH, FL, ready=(ya_ready, 0))
            layer("g1", HH, HL)
            layer("proj_lru", FH[:, 8:16, :], FL[:, 8:16, :], ready=(yb_ready, 0))
            layer("mix_out", FH, FL, ready=(mg_ready, 0))
            mean_square("mix_post")
            mean_square("ffn_pre")
            front("ffn_up_a", HH, HL, (h_ready, 8))
            loop_layer("ffn_up_a", HH, HL, 8)
            loop_layer("ffn_down_a", FH, FL, 4, (f_ready, 0))
            loop_layer("ffn_up_b", HH, HL, 8)
            loop_layer("ffn_down_b", FH, FL, 8, (f_ready, F_TILES))
            mean_square("ffn_post")

            mean_square("mix2_0")
            front("fa", HH, HL, (h_ready, 16))
            layer("q_fox", HH, HL)
            layer("k_fox", HH, HL)
            layer("v_fox", HH, HL, token_major=True)

            def score_head(kind, n, h, q, k):
                if n >= 2:
                    pe.wait_ge(s_max, 2 * (n - 1))
                b = (N4, N5)[n % 2]
                rows = slice(64 * (h % 2), 64 * (h % 2) + 64)
                for qb, lo, cols in ((0, 0, P), (1, P, T)):
                    if kind == "mla":
                        mm = pe.matmul(b[:, lo:lo + cols], q[:, h, qb * P:qb * P + P], k[:, h, 0:cols], start=True, stop=True)
                        continue
                    mm = pe.matmul(b[:, lo:lo + cols], q[rows, h // 2, qb * P:qb * P + P], k[rows, h // 2, 0:cols],
                                   start=True, stop=(kind != "fox"))
                    if kind == "fox":
                        mm = pe.matmul(b[:, lo:lo + cols], AQ[rows, h // 2, qb * P:qb * P + P], BK[rows, h // 2, 0:cols],
                                       start=False, stop=True)
                mm.then_inc(s_mm, 1)

            def turn_head(n):
                pe.wait_ge(p_norm, n + 1)
                if n >= 1:
                    pe.wait_ge(pt_ready, n)
                for c in range(3):
                    mm = pe.transpose(N6[:, c * P:c * P + P], M[:, n % 2, c * P:c * P + P], ident[:, :])
                mm.then_inc(pt_mm, 1)

            def weigh_head(n, h, v, w, w_ready, count):
                pe.wait_ge(w_ready, count)
                pair = n // 2
                if h % 2 == 0 and pair >= 1:
                    pe.wait_ge(o_ready, pair)
                rows, c = slice(64 * (h % 2), 64 * (h % 2) + 64), slice(64 * h, 64 * h + 64)
                pe.matmul(N7[rows, 0:T], v[:, 0, c], w[:, 0:T], start=True, stop=False)
                pe.matmul(N7[rows, P:T], v[:, 1, c], w[:, T:S3], start=False, stop=True).then_inc(pv_mm, 1)

            def softmax_step(i, kind, n0, o0, q, k, v):
                if i < HEADS:
                    score_head(kind, n0 + i, i, q, k)
                if 1 <= i <= HEADS:
                    turn_head(n0 + i - 1)
                if 2 <= i <= HEADS + 1:
                    h = i - 2
                    weigh_head(o0 + h, h, v, PT[:, (n0 + h) % 2, :], pt_ready, n0 + h + 1)

            def softmax_over(name, ready, kind, n0, o0, q, k, v):
                score_head(kind, n0, 0, q, k)
                for i in range(HEADS + 2):
                    if i + 1 < HEADS:
                        score_head(kind, n0 + i + 1, i + 1, q, k)
                    if i < COUNT[name]:
                        dense_tile(FIRST[name] + i, FH, FL, ready=ready if i == 0 else None)
                    if 1 <= i <= HEADS:
                        turn_head(n0 + i - 1)
                    if 2 <= i:
                        h = i - 2
                        weigh_head(o0 + h, h, v, PT[:, (n0 + h) % 2, :], pt_ready, n0 + h + 1)

            def fox(i):
                if i == 0:
                    pe.wait_ge(evac, taken("v_fox", 3))
                    pe.wait_ge(dtile_in, 32 * HEADS)
                softmax_step(i, "fox", 0, 0, Q, K, V)

            layer("q_chk", HH, HL, {n: (lambda n=n: fox(n)) for n in range(4)})
            layer("k_chk", HH, HL, {n: (lambda n=n: fox(n + 4)) for n in range(4)})
            layer("v_chk", HH, HL, {n: (lambda n=n: fox(n + 8)) for n in range(2)}, token_major=True)
            pe.wait_ge(evac, taken("v_chk", 3))
            softmax_over("ab_out_a", (o_ready, 0), "chk", 8, 8, Q2, K2, V2)
            layer("ab_out_b", FH[:, 4:8, :], FL[:, 4:8, :], ready=(o_ready, 4))
            mean_square("mlp2_0")

            def mlp(which, h0, f0):
                front(f"mlp_up{which}a", HH, HL, (h_ready, h0))
                loop_layer(f"mlp_up{which}a", HH, HL, 4)
                loop_layer(f"mlp_down{which}a", FH, FL, 4, (f_ready, f0))
                loop_layer(f"mlp_up{which}b", HH, HL, 4)
                loop_layer(f"mlp_down{which}b", FH, FL, 4, (f_ready, f0 + F_TILES))

            mlp(0, 24, FFN_PAIRS)
            mean_square("mix2_1")
            front("c_q", HH, HL, (h_ready, 32))
            layer("c_kv", HH, HL)
            layer("q_sb", HH, HL, {0: lambda: mean_square("q_norm"), 2: lambda: mean_square("kv_norm")})
            layer("k_sb", HH, HL)
            layer("v_sb", HH, HL, token_major=True)

            def sb_scores(h):
                if h >= 2:
                    pe.wait_ge(arg_ready, h - 1)
                b = (N5, N6)[h % 2]
                rows = slice(64 * (h % 2), 64 * (h % 2) + 64)
                pe.matmul(b[:, 0:T], K2[rows, h // 2, 0:P], Q2[rows, h // 2, :], start=True, stop=False, skip_group_check=True)
                pe.matmul(b[:, T:S3], K2[rows, h // 2, P:T], Q2[rows, h // 2, P:T], start=False, stop=False,
                          skip_group_check=True).then_inc(s_mm, 1)

            def sb_suffix(h):
                pe.wait_ge(lm_ready, 2 * (h + 1))
                b, lm = (N5, N6)[h % 2], S[:, h % 2, :]
                pe.matmul(b[:, 0:T], neg_tri[:, :], lm[:, 0:T], start=False, stop=False, skip_group_check=True)
                pe.matmul(b[:, P:T], neg_one[:, :], lm[:, T:S3], start=False, stop=False, skip_group_check=True)
                pe.matmul(b[:, T:S3], neg_tri[:, :], lm[:, T:S3], start=False, stop=True,
                          skip_group_check=True).then_inc(arg_mm, 1)

            def stick(i):
                if i == 0:
                    pe.wait_ge(evac, taken("v_sb", 3))
                if i < HEADS:
                    sb_scores(i)
                if 1 <= i <= HEADS:
                    sb_suffix(i - 1)
                if 2 <= i <= HEADS + 1:
                    h = i - 2
                    weigh_head(16 + h, h, V2, M[:, h % 2, :], a_exp, h + 1)

            layer("k_rope", HH, HL, {n: (lambda n=n: stick(n)) for n in range(2)})
            layer("q_mla", HH, HL, {n: (lambda n=n: stick(n + 2)) for n in range(HEADS)}, ready=(h_ready, 40))
            layer("k_mla", HH[:, Q_KT:, :], HL[:, Q_KT:, :], ready=(h_ready, 40 + Q_KT))
            layer("v_mla", HH[:, Q_KT:, :], HL[:, Q_KT:, :], token_major=True)
            pe.wait_ge(evac, taken("v_mla", 3))
            pe.wait_ge(dve_take, taken("q_mla", HEADS - 1))
            pe.wait_ge(kcopy, 1)
            softmax_over("cd_out_a", (o_ready, 8), "mla", 16, 24, Q, K, V)
            layer("cd_out_b", FH[:, 4:8, :], FL[:, 4:8, :], ready=(o_ready, 12))
            mean_square("mlp2_1")
            mlp(1, 45, FFN_PAIRS + MLP_TILES)
            mean_square("final")

        @block.scalar
        def _(act):
            rounded = [0]

            def round_slab(i, turn=0, per=0):
                act.wait_ge(slab_in[i % R], turn * (16 * per // R) + 16 * (i // R + 1))
                if i >= R:
                    act.wait_ge(unit, turn * per + LAST_UNIT[i - R])
                act.activation(WH[:, i % R, :], RAW[:, i % R, :], ACT.Copy).then_inc(hi_ready, 1)

            def ahead(name, n):
                while rounded[0] < min(slab_of(name, n) + R, SLABS):
                    round_slab(rounded[0])
                    rounded[0] += 1

            def square(name, k, src):
                i = NORM[name]
                if SQUARES[i] + k >= SQ_SLOTS:
                    act.wait_ge(*square_used(SQUARES[i] + k - SQ_SLOTS))
                act.activation(SQ[:, (SQUARES[i] + k) % SQ_SLOTS, :], src, ACT.Square).then_inc(squared, 1)

            def std(name):
                i = NORM[name]
                act.wait_ge(ms_ready, i + 1)
                act.activation(RS[:, i % 3, :], N4[:, 0:T], ACT.Sqrt, bias=EPSC[:, :], scale=NORMS[i][2]).then_inc(std_ready, 1)

            def residual_square(name, k, count):
                act.wait_ge(x_ready, count)
                square(name, k, X[:, k, :])

            def round_next():
                round_slab(rounded[0])
                rounded[0] += 1

            def round_hidden(base, last_reader=None, n=KD, src=HT, between=()):
                if last_reader:
                    act.wait_ge(unit, unit_of(last_reader, COUNT[last_reader] - 1))
                for k in range(n):
                    act.wait_ge(h32, base + k + 1)
                    act.activation(HH[:, k, :], src[:, k % src.shape[1], :], ACT.Copy).then_inc(h_hi, 1)
                    if k in between:
                        round_next()

            def softplus_exp(i, out, in_):
                act.wait_ge(sp_in, i + 1)
                act.activation(out, in_, ACT.Exp).then_inc(sp_exp, 1)

            def tile(name, n):
                act.wait_ge(unit, unit_of(name, n))
                return tile_bank(name, n)[:, 0:T]

            act.preload_act_table_set("sqrt_and_others")
            for k in range(KD):
                if k % 4 == 0:
                    act.wait_ge(x_in[k // 4], 16)
                square("mix_pre", k, X[:, k, :])
            act.wait_ge(tables, 2)
            round_slab(0)
            std("mix_pre")
            round_slab(1)
            rounded[0] = 2
            round_hidden(0, between=(2, 5))
            act.wait_ge(consts_in, 16)
            act.activation(NEGA[:, :], col("a_log", rows=slice(0, 16)), ACT.Exp).then_inc(nega, 1)
            softplus_exp(0, SP[0:16, 2, :], SP[0:16, 1, :])

            def tap(name, n, out):
                act.activation(out, tile(name, n), ACT.Identity, bias=col(name + "_b", n),
                               scale=col(name + "_w", 4 * n + 3)).then_inc(conv0, 1)

            def silu(n):
                act.wait_ge(conv, n + 1)
                act.activation(A[:, n, :], A[:, n, :], ACT.Silu).then_inc(act_in, 1)

            for n in range(XBC_TILES):
                ahead("xbc", n)
                tap("xbc", n, A[:, n, :])
                if n == 5:
                    softplus_exp(1, LSP[:, 2, :], LSP[:, 1, :])
                if n >= 1:
                    silu(n - 1)
            silu(XBC_TILES - 1)
            for n in range(KD):
                ahead("ly", n)
                act.activation(GATE[:, n, :], tile("ly", n), ACT.Gelu_apprx_tanh).then_inc(evac, 1)

            def decay(h):
                act.wait_ge(seg_ready, h + 1)
                act.activation(S[:, h % 2, :], S[:, h % 2, :], ACT.Exp).then_inc(decay_ready, 1)

            for n in range(KD):
                ahead("lx", n)
                tap("lx", n, XC[:, n, :])
                decay(n)
            for n in range(KD):
                ahead("z", n)
                act.activation(ZS[:, n, :], tile("z", n), ACT.Tanh, scale=0.5).then_inc(zs_ready, 1)
                decay(8 + n)
            act.wait_ge(half_bias, 3)

            def round_ya(k):
                act.wait_ge(yn_ready, k + 1)
                act.activation(FH[:, k, :], YS[:, k, :], ACT.Copy).then_inc(ya_hi, 1)

            for n in range(KD):
                ahead("g0", n)
                if n in (4, 5):
                    std(("ssm0", "ssm1")[n - 4])
                act.activation(G[:, n, :], tile("g0", n), ACT.Tanh, bias=HB[:, n:n + 1], scale=0.5).then_inc(evac, 1)
                if n == 0:
                    act.wait_ge(ys_ready, SSM_TILES)
                if n in (1, 2):
                    for k in range(4):
                        act.wait_ge(yg_ready, 4 * (n - 1) + k + 1)
                        square(("ssm0", "ssm1")[n - 1], k, YS[:, 4 * (n - 1) + k, :])
                act.wait_ge(rg_mm, n + 1)
                act.activation(TH[:, n, :], N5[:, 0:T], ACT.Tanh, bias=HB[:, 16 + n:17 + n], scale=0.5).then_inc(rg_ready, 1)
                act.activation(IG[:, n, :], N5[:, T:2 * T], ACT.Tanh, bias=HB[:, 24 + n:25 + n], scale=0.5).then_inc(rg_ready, 1)
                if n in (6, 7):
                    for k in range(4):
                        round_ya(4 * (n - 6) + k)
            act.wait_ge(lam_ready, 2)
            for n in range(KD):
                ahead("proj_ssm", n)
                act.wait_ge(rg_ready, 2 * n + 1)
                act.activation(AG[:, n, :], TH[:, n, :], ACT.Exp, bias=LSP[:, 4, n:n + 1], scale=LSP[:, 4, n:n + 1]).then_inc(ag_ready, 1)
                act.activation(TH[:, n, :], TH[:, n, :], ACT.Tanh, bias=LSP[:, 3, n:n + 1], scale=LSP[:, 3, n:n + 1]).then_inc(th_ready, 1)

            def round_yb(k):
                act.wait_ge(yb32, k + 1)
                act.activation(FH[:, KD + k, :], GATE[:, k, :], ACT.Copy).then_inc(yb_hi, 1)

            for n in range(KD):
                ahead("g1", n)
                act.wait_ge(dve_take, taken("proj_ssm", n))
                act.activation(G[:, n, :], tile("g1", n), ACT.Tanh, bias=HB[:, 8 + n:9 + n], scale=0.5).then_inc(evac, 1)
                if n == 0:
                    for j in range(KD):
                        act.wait_ge(m2_ready, j + 1)
                        act.activation(TH[:, j, :], TH[:, j, :], ACT.Sqrt, scale=0.25).then_inc(mult_ready, 1)
                if n >= 2:
                    round_yb(n - 2)
            round_yb(KD - 2)
            round_yb(KD - 1)

            def round_merged(k):
                act.wait_ge(mg32, k + 1)
                act.activation(FH[:, k, :], MG[:, k, :], ACT.Copy, scale=0.5).then_inc(mg_hi, 1)

            for n in range(KD):
                ahead("proj_lru", n)
                act.wait_ge(unit, unit_of("proj_lru", n))
                round_merged(n)
            act.preload_act_table_set("sqrt_and_others")
            for n in range(KD):
                ahead("mix_out", n)
                p = tile("mix_out", n)
                act.activation(Y[:, n, :], p, ACT.Copy).then_inc(y_evac, 1)
                square("mix_post", n, p)
            ahead("ffn_up_a", 0)
            std("mix_post")
            for k in range(KD):
                residual_square("ffn_pre", k, k + 1)
            std("ffn_pre")
            round_hidden(8, "g1")

            c0 = taken("ffn_up_a")

            def ffn_turn(name, p0, it, first_turn, slab0):
                u0, turn = unit_of(name, 0), (0 if first_turn else it)
                for j in range(2):
                    p = it * 2 + (p0 + j)
                    for half in range(2):
                        at = p * 2 + half
                        round_slab(slab0 + 2 * j + half, turn, R)
                        act.wait_ge(unit, it * 4 + (u0 + 2 * j + half))
                        if half == 0 and not (first_turn and p0 == 0):
                            act.wait_ge(f_ready, p + (-1))
                        b = tile_bank(name, 2 * j + half)
                        act.activation(CV[:, 2 * j + half, :], b[:, 0:T], ACT.Identity,
                                       bias=C[:, dyn(at + COL["ffn_b"])], scale=C[:, dyn(at * 3 + (COL["ffn_w"] + 2))]).then_inc(conv0, 1)
                        if half == 0 and not (first_turn and j == 0):
                            act.wait_ge(f32_ready, p * 1)
                            act.activation(FH[:, dyn(it * 2 + (j - 1)), :], CV[:, 2 * ((j + 1) % 2), :], ACT.Copy).then_inc(f_hi, 1)
                    act.wait_ge(conv, p * 2 + c0)
                    act.activation(CV[:, 2 * j, :], CV[:, 2 * j, :], ACT.Gelu_apprx_tanh).then_inc(gelu_done, 1)

            def ffn_up(name, p0, following):
                slab0, turns = rounded[0], COUNT[name] // 4
                ffn_turn(name, p0, 0, True, slab0)
                with act.Fori(1, turns) as it:
                    ffn_turn(name, p0, it, False, slab0)
                rounded[0] += 4 * turns
                ahead(*following)
                act.wait_ge(f32_ready, p0 + 2 * turns)
                act.activation(FH[:, 2 * turns - 1, :], CV[:, 2, :], ACT.Copy).then_inc(f_hi, 1)

            ffn_up("ffn_up_a", 0, ("ffn_down_a", 0))
            for n in range(KD):
                ahead("ffn_down_a", n)
                act.activation(Y[:, n, :], tile("ffn_down_a", n), ACT.Copy).then_inc(evac, 1)
            ffn_up("ffn_up_b", F_TILES, ("ffn_down_b", 0))
            act.preload_act_table_set("sqrt_and_others")
            for n in range(KD):
                ahead("ffn_down_b", n)
                act.wait_ge(y_sum, n + 1)
                square("ffn_post", n, Y[:, n, :])
            ahead("fa", 0)
            std("ffn_post")
            for k in range(KD):
                residual_square("mix2_0", k, KD + k + 1)
            std("mix2_0")
            round_hidden(16, "ffn_up_b")

            def evac_tile(name, n, out, scale=1.0, rows=slice(0, P)):
                ahead(name, n)
                act.activation(out[rows, n, :], tile(name, n)[rows, :], ACT.Copy, scale=scale).then_inc(evac, 1)

            def evac_v(name, n, v):
                ahead(name, n)
                src = tile(name, n).rearrange("p (b n) -> p b n", b=TB)
                act.activation(v[:, :, n * P:n * P + P], src, ACT.Copy).then_inc(evac, 1)

            def out_pair(pair):
                act.wait_ge(pv_mm, 2 * pair + 2)
                act.activation(FH[:, pair % 8, :], N7[:, 0:T], ACT.Copy).then_inc(o_hi, 1)

            def softmax_step(i, n0, o0, scale):
                if i >= 4 and i % 2 == 0:
                    out_pair((o0 + i - 4) // 2)
                if i < HEADS:
                    n = n0 + i
                    act.wait_ge(s_bias, n + 1)
                    for qb, (lo, cols) in enumerate(((0, P), (P, T))):
                        act.activation(S[:, n % 2, lo:lo + cols], S[:, n % 2, lo:lo + cols], ACT.Exp,
                                       bias=ST[:, n % 2, 2 + qb:3 + qb], scale=scale,
                                       accum_out=ST[:, n % 2, 4 + qb:5 + qb]).then_inc(p_exp, 1)
                if 1 <= i <= HEADS:
                    n = n0 + i - 1
                    act.wait_ge(pt_mm, n + 1)
                    if n >= 2:
                        act.wait_ge(pv_mm, o0 + i - 2)
                    act.activation(PT[:, n % 2, :], N6[:, 0:S3], ACT.Copy).then_inc(pt_ready, 1)

            ahead("fa", 0)
            softplus_exp(2, SP[0:HEADS, 2, :], SP[0:HEADS, 1, :])
            for n in range(4):
                evac_tile("q_fox", n, Q, 0.125)
            for n in range(4):
                evac_tile("k_fox", n, K)
            for n in range(4):
                evac_v("v_fox", n, V)
            for n in range(4):
                evac_tile("q_chk", n, Q2, 0.125)
                softmax_step(n, 0, 0, 1.0)
            for n in range(4):
                evac_tile("k_chk", n, K2)
                softmax_step(n + 4, 0, 0, 1.0)
            for n in range(4):
                evac_v("v_chk", n, V2)
                if n < 3:
                    softmax_step(n + 8, 0, 0, 1.0)
            def softmax_over(name, n0, o0, scale):
                for i in range(HEADS + 3):
                    softmax_step(i, n0, o0, scale)
                    if i < COUNT[name]:
                        ahead(name, i)

            softmax_over("ab_out_a", 8, 8, 1.0)

            def residual_layer(name, norm, following=None):
                if norm:
                    act.preload_act_table_set("sqrt_and_others")
                for n in range(KD):
                    ahead(name, n)
                    if norm:
                        residual_square(norm, n, taken(name, n))
                if following:
                    ahead(following, 0)
                if norm:
                    std(norm)

            residual_layer("ab_out_b", "mlp2_0", "mlp_up0a")
            round_hidden(24, "v_chk")

            def mlp_up(name, f0):
                slab0, u0, e0 = rounded[0], unit_of(name, 0), taken(name)

                def relu(it, j, turn):
                    round_slab(slab0 + j, turn, R)
                    act.wait_ge(unit, it * 4 + (u0 + j))
                    act.wait_ge(f_ready, it * 4 + (f0 + j - 3))
                    act.activation(RT[:, j, :], tile_bank(name, j)[:, 0:T], ACT.Relu).then_inc(evac, 1)

                def round_square(it, j):
                    act.wait_ge(evac, it * 4 + (e0 + j))
                    act.activation(FH[:, dyn(it * 4 + j), :], RT[:, j % 4, :], ACT.Square).then_inc(f_hi, 1)

                with act.Fori(0, F_TILES // 4) as it:
                    for j in range(4):
                        relu(it, j, it)
                        round_square(it, j)
                rounded[0] += F_TILES

            mlp_up("mlp_up0a", FFN_PAIRS)
            for n in range(KD):
                ahead("mlp_down0a", n)
                if n == 3:
                    act.wait_ge(ang_ready, 2)
                    act.activation(SIN[64:P, :], ANG[64:P, 4, :], ACT.Sin).then_inc(sin_ready, 1)
                    act.activation(COS[64:P, :], ANG[64:P, 5, :], ACT.Sin).then_inc(sin_ready, 1)
            mlp_up("mlp_up0b", FFN_PAIRS + F_TILES)
            residual_layer("mlp_down0b", "mix2_1", "c_q")
            round_hidden(32, "mlp_up0b")
            for n in range(Q_KT):
                evac_tile("c_q", n, LAT)
                act.wait_ge(evac, taken("c_q", n))
                square("q_norm", n, LAT[:, n, :])
            for n in range(KV_KT):
                evac_tile("c_kv", n, LAT[:, Q_KT:, :])
                act.wait_ge(evac, taken("c_kv", n))
                square("kv_norm", n, LAT[:, Q_KT + n, :])
            for n in range(4):
                if n in (1, 3):
                    std(("q_norm", "kv_norm")[n // 2])
                evac_tile("q_sb", n, Q2, 0.125)
            for n in range(4):
                evac_tile("k_sb", n, K2)
            for n in range(4):
                evac_v("v_sb", n, V2)
            act.preload_act_table_set("natural_log_exp_and_others")

            def stick_step(i):
                if i < HEADS:
                    s = S[:, i % 2, :]
                    act.wait_ge(s_mm, 16 + i + 1)
                    if i >= 2:
                        act.wait_ge(arg_mm, i - 1)
                    act.activation(s, (N5, N6)[i % 2][:, 0:S3], ACT.Abs).then_inc(z_abs, 1)
                    act.wait_ge(z_abs, i + 1)
                    act.activation(s, s, ACT.Exp, scale=-1.0).then_inc(z_exp, 1)
                    act.wait_ge(z_exp, i + 1)
                    act.activation(s, s, ACT.Ln, bias=1.0).then_inc(z_ln, 1)
                if 1 <= i <= HEADS:
                    act.wait_ge(arg_ready, i)
                    act.activation(M[:, (i - 1) % 2, :], M[:, (i - 1) % 2, :], ACT.Exp).then_inc(a_exp, 1)
                if i >= 4 and i % 2 == 0:
                    out_pair(8 + (i - 4) // 2)

            for n in range(2):
                evac_tile("k_rope", n, KR)
                stick_step(n)
                if n == 1:
                    round_hidden(40, "k_rope", n=Q_KT + KV_KT, src=LAT)
            for n in range(HEADS):
                ahead("q_mla", n)
                stick_step(n + 2)
            stick_step(HEADS + 2)
            for n in range(HEADS):
                evac_tile("k_mla", n, K, rows=slice(0, 64))
            for n in range(4):
                evac_v("v_mla", n, V)
            softmax_over("cd_out_a", 16, 24, (64 + 32) ** -0.5)
            residual_layer("cd_out_b", "mlp2_1", "mlp_up1a")
            round_hidden(45, "v_mla")
            mlp_up("mlp_up1a", FFN_PAIRS + 2 * F_TILES)
            residual_layer("mlp_down1a", None)
            mlp_up("mlp_up1b", FFN_PAIRS + 3 * F_TILES)
            residual_layer("mlp_down1b", "final")

        @block.vector
        def _(dve):
            steps, split = [0], [0]
            stt, tt, ts = dve.scalar_tensor_tensor, dve.tensor_tensor, dve.tensor_scalar

            def link(ins):
                steps[0] += 1
                ins.then_inc(step, 1)
                dve.wait_ge(step, steps[0])

            def less(out, whole, part):
                return tt(out, whole, part.bitcast(fp32), ALU.subtract)

            def split_slab(i, turn=0, per=0):
                if i % R != R - 1:
                    dve.wait_ge(hi_ready, turn * per + (i + 1))
                    less(WL[:, i % R, :], RAW[:, i % R, :], WH[:, i % R, :]).then_inc(lo_ready[i % R], 1)

            def ahead(name, n):
                while split[0] < min(slab_of(name, n) + R, SLABS):
                    split_slab(split[0])
                    split[0] += 1

            def add_square(name, k):
                i = NORM[name]
                if k == 0 or name in DIRECT:
                    return
                sq = lambda n: SQ[:, (SQUARES[i] + n) % SQ_SLOTS, :]
                dve.wait_ge(squared, SQUARES[i] + k + 1)
                if k == 1:
                    if i:
                        dve.wait_ge(ms_ready, i)
                    tt(ACC[:, :], sq(0), sq(1), ALU.add).then_inc(added, 1)
                else:
                    dve.wait_ge(added, ADDS[i] + k - 1)
                    tt(ACC[:, :], ACC[:, :], sq(k), ALU.add).then_inc(added, 1)

            def rstd(name):
                i = NORM[name]
                dve.wait_ge(std_ready, i + 1)
                dve.reciprocal(RS[:, i % 3, :], RS[:, i % 3, :]).then_inc(rstd_ready, 1)
                dve.wait_ge(rstd_ready, i + 1)
                return RS[:, i % 3, :]

            def low_hidden(k, base, src):
                dve.wait_ge(h_hi, base + k + 1)
                less(HL[:, k, :], src[:, k % src.shape[1], :], HH[:, k, :]).then_inc(h_ready, 1)

            def split_next():
                split_slab(split[0])
                split[0] += 1

            def pre_norm(name, base, c=None, at=0, between=()):
                r = rstd(name)
                for k in range(KD):
                    stt(out=HT[:, k % 4, :], in0=X[:, k, :], scalar=col(c or name, at + k), in1=r, op0=ALU.mult, op1=ALU.mult).then_inc(h32, 1)
                    if k >= 1:
                        low_hidden(k - 1, base, HT)
                    if k in between:
                        split_next()
                low_hidden(KD - 1, base, HT)

            def softplus(part, i, v, src, bias, scale, t, out, s, bank_taken=None):
                e, p, q = t[1], t[0], t[2]
                if part == 0:
                    first = ts(v, src, scale, bias, ALU.mult, ALU.add)
                    if bank_taken:
                        first.then_inc(u_taken, 1)
                        dve.wait_ge(u_taken, bank_taken)
                    else:
                        link(first)
                    stt(out=t[0], in0=v, scalar=-1.0, in1=v, op0=ALU.mult, op1=ALU.min).then_inc(sp_in, 1)
                if part == 1:
                    dve.wait_ge(sp_exp, i + 1)
                    link(ts(q, e, 2.0, None, ALU.add))
                    link(dve.reciprocal(q, q))
                    link(tt(e, e, q, ALU.mult))
                    link(tt(q, e, e, ALU.mult))
                    link(ts(p, q, 1 / 15, None, ALU.mult))
                    link(ts(v, v, 0.0, None, ALU.max))
                if part == 2:
                    for n in (13, 11, 9, 7, 5, 3):
                        link(stt(out=p, in0=p, scalar=1 / n, in1=q, op0=ALU.add, op1=ALU.mult))
                    link(stt(out=p, in0=p, scalar=1.0, in1=e, op0=ALU.add, op1=ALU.mult))
                    stt(out=out, in0=p, scalar=2.0, in1=v, op0=ALU.mult, op1=ALU.add).then_inc(s, 1)

            split_slab(0)
            split[0] = 1
            dve.wait_ge(consts_in, 16)
            dve.wait_ge(x_in[0], 16)
            dve.wait_ge(x_in[1], 16)
            pre_norm("mix_pre", 0, between=(0, 3, 6))

            rows = slice(0, SSM_HEADS)

            def dt_part(part):
                if part == 0:
                    dve.wait_ge(unit, unit_of("dt", 0))
                softplus(part, 0, SP[rows, 0, :], tile_bank("dt", 0)[rows, 0:T], col("dt_bias", rows=rows), 1.0,
                         [SP[rows, 1, :], SP[rows, 2, :], SP[rows, 3, :]], DT[:, :], dt_ready, 1)
                if part == 2:
                    dve.wait_ge(dt_ready, 1)
                    dve.wait_ge(nega, 1)
                    link(ts(SP[rows, 4, :], DT[:, :], NEGA[:, :], -1.0, ALU.mult, ALU.mult))
                    dve.wait_ge(tables, ALL_TABLES)
                    dve.tensor_tensor_scan(ACS[:, :], ones[rows, :], SP[rows, 4, :], 0.0, ALU.mult, ALU.add).then_inc(acs_ready, 1)

            dt_part(0)

            started = [0]

            def taps(name, n, out, k=4):
                started[0] += 1
                dve.wait_ge(conv0, started[0])
                p = tile_bank(name, n)
                for back in range(1, k):
                    last = stt(out=out[:, back:T], in0=p[:, 0:T - back], scalar=col(name + "_w", k * n + k - 1 - back),
                               in1=out[:, back:T], op0=ALU.mult, op1=ALU.add)
                    if back < k - 1:
                        link(last)
                last.then_inc(conv, 1)

            for n in range(XBC_TILES):
                ahead("xbc", n)
                taps("xbc", n, A[:, n, :])
                if n in (1, 3):
                    dt_part((n + 1) // 2)
                if n in (4, 6, 8):
                    softplus((n - 4) // 2, 1, LSP[:, 0, :], col_n("lam", KD), 0.0, -1.0, [LSP[:, 1, :], LSP[:, 2, :], LSP[:, 5, :]],
                             LSP[:, 0, :], lam_ready)
                if n == 8:
                    dve.wait_ge(lam_ready, 1)
                    link(ts(LSP[:, 3, :], LSP[:, 0, :], 4.0, None, ALU.mult))
                    ts(LSP[:, 4, :], LSP[:, 0, :], -4.0, None, ALU.mult).then_inc(lam_ready, 1)
                    for m, (name, width) in enumerate((("gate_b", 16), ("br", 8), ("bi", 8))):
                        ts(HB[:, (0, 16, 24)[m]:(0, 16, 24)[m] + width], col_n(name, width), 0.5, None, ALU.mult).then_inc(half_bias, 1)

            def turned_xs(b):
                for half in range(2):
                    dve.wait_ge(xst, 2 * b + half + 1)
                    hs = slice(8 * half, 8 * half + 8)
                    tt(XDT[:, b, hs, :], (N6, N7)[half][:, :].rearrange("p (h d) -> p h d", d=64),
                       COLS[:, b, 1, hs].unsqueeze(2).to_broadcast([P, 8, 64]), ALU.mult).then_inc(xdt_ready, 1)

            for n in range(KD):
                ahead("ly", n)
                if n == 0:
                    dve.wait_ge(colt, 1)
                    dve.tensor_copy(COLS[:, :, :, :].rearrange("p b n h -> p (b n h)"), N5[:, 0:64]).then_inc(cols_ready, 1)
                    dve.wait_ge(cols_ready, 1)
                if n == 1:
                    dve.wait_ge(cbt, 2)
                    for g in range(2):
                        tt(CBM[:, g, :], (N6, N7)[g][:, 0:S3], keep_incl[:, :], ALU.mult).then_inc(cbm_ready, 1)
                if n in (3, 5):
                    turned_xs((n - 3) // 2)

            def decay_args(h):
                dve.wait_ge(bcast, h + 1)
                ts(S[:, h % 2, 0:T], N4[:, 0:T], COLS[:, 0, 0, h:h + 1], 0.0, ALU.subtract, ALU.min)
                ts(S[:, h % 2, T:S3], N4[:, P:T], COLS[:, 1, 0, h:h + 1], 0.0, ALU.subtract, ALU.min).then_inc(seg_ready, 1)

            def decay_cb(h):
                dve.wait_ge(decay_ready, h + 1)
                if h >= 2:
                    dve.wait_ge(y_mm, h - 1)
                tt(M[:, h % 2, :], S[:, h % 2, :], CBM[:, h // 8, :], ALU.mult).then_inc(m_ready, 1)

            def skip(j):
                dve.wait_ge(y_mm, 2 * j + 2)
                stt(out=YS[:, j, :], in0=XS[:, j, :], scalar=col("skip", j), in1=(N6, N7)[j % 2][:, 0:T],
                    op0=ALU.mult, op1=ALU.add).then_inc(ys_ready, 1)

            def gate_y(j):
                dve.wait_ge(ys_ready, j + 1)
                dve.wait_ge(dve_take, taken("z", j))
                stt(out=YS[:, j, :], in0=YS[:, j, :], scalar=0.5, in1=ZS[:, j, :], op0=ALU.mult, op1=ALU.mult).then_inc(yg_ready, 1)

            for n in range(KD):
                ahead("lx", n)
                taps("lx", n, XC[:, n, :])
                decay_args(n)
                if n >= 2 and n % 2 == 0:
                    skip(n // 2 - 1)
                decay_cb(n)
            for n in range(KD):
                ahead("z", n)
                dve.wait_ge(zs_ready, n + 1)
                stt(out=ZS[:, n, :], in0=ZS[:, n, :], scalar=1.0, in1=tile_bank("z", n)[:, 0:T], op0=ALU.add, op1=ALU.mult).then_inc(dve_take, 1)
                decay_args(8 + n)
                if n % 2 == 0:
                    skip(3 + n // 2)
                if n < 7:
                    gate_y(n)
                decay_cb(8 + n)

            def recurrence_in(j):
                dve.wait_ge(rg_ready, 2 * j + 2)
                stt(out=IG[:, j, :], in0=IG[:, j, :], scalar=1.0, in1=XC[:, j, :], op0=ALU.add, op1=ALU.mult).then_inc(ix_ready, 1)

            def low_ya(k):
                dve.wait_ge(ya_hi, k + 1)
                less(FL[:, k, :], YS[:, k, :], FH[:, k, :]).then_inc(ya_ready, 1)

            for n in range(KD):
                ahead("g0", n)
                if n == 0:
                    skip(7)
                    gate_y(7)
                if n in (1, 3):
                    for k in range(4):
                        add_square(("ssm0", "ssm1")[n // 2], k)
                if n in (4, 5):
                    r = rstd(("ssm0", "ssm1")[n - 4])
                    for k in range(4 * (n - 4), 4 * (n - 4) + 4):
                        stt(out=YS[:, k, :], in0=YS[:, k, :], scalar=col("ssm_norm", k), in1=r, op0=ALU.mult, op1=ALU.mult).then_inc(yn_ready, 1)
                if n >= 1:
                    recurrence_in(n - 1)
                if n in (6, 7):
                    for k in range(4):
                        low_ya(4 * (n - 6) + k)
            recurrence_in(KD - 1)
            for n in range(KD):
                ahead("proj_ssm", n)
                dve.wait_ge(ag_ready, n + 1)
                link(tt(HT[:, n % 4, :], AG[:, n, :], AG[:, n, :], ALU.mult))
                dve.wait_ge(th_ready, n + 1)
                stt(out=TH[:, n, :], in0=HT[:, n % 4, :], scalar=1.0, in1=TH[:, n, :], op0=ALU.add, op1=ALU.mult).then_inc(m2_ready, 1)
                dve.wait_ge(unit, unit_of("proj_ssm", n))
                dve.wait_ge(evac, taken("g0", n))
                stt(out=MG[:, n, :], in0=G[:, n, :], scalar=1.0, in1=tile_bank("proj_ssm", n)[:, 0:T], op0=ALU.add, op1=ALU.mult).then_inc(dve_take, 1)

            def low_yb(k):
                dve.wait_ge(yb_hi, k + 1)
                less(FL[:, KD + k, :], GATE[:, k, :], FH[:, KD + k, :]).then_inc(yb_ready, 1)

            def recurrence(j):
                dve.wait_ge(bx_ready, j + 1)
                dve.tensor_tensor_scan(XC[:, j, :], AG[:, j, :], IG[:, j, :], 0.0, ALU.mult, ALU.add).then_inc(scanned, 1)

            for n in range(KD):
                ahead("g1", n)
                if n >= 1:
                    recurrence(n - 1)
                if n >= 3:
                    low_yb(n - 3)
            recurrence(KD - 1)
            for k in range(KD - 3, KD):
                low_yb(k)

            def low_merged(k):
                dve.wait_ge(mg_hi, k + 1)
                stt(out=FL[:, k, :], in0=MG[:, k, :], scalar=0.5, in1=FH[:, k, :].bitcast(fp32), op0=ALU.mult, op1=ALU.subtract).then_inc(mg_ready, 1)

            for n in range(KD):
                ahead("proj_lru", n)
                dve.wait_ge(unit, unit_of("proj_lru", n))
                dve.wait_ge(evac, taken("g1", n))
                stt(out=HT[:, n % 4, :], in0=G[:, n, :], scalar=1.0, in1=tile_bank("proj_lru", n)[:, 0:T], op0=ALU.add, op1=ALU.mult).then_inc(dve_take, 1)
                if n >= 1:
                    low_merged(n - 1)
            low_merged(KD - 1)

            def post_norm(name):
                r = rstd(name)
                for k in range(KD):
                    stt(out=Y[:, k, :], in0=Y[:, k, :], scalar=col(name, k), in1=r, op0=ALU.mult, op1=ALU.mult).then_inc(y_normed, 1)

            for n in range(KD):
                ahead("mix_out", n)
                add_square("mix_post", n)
            post_norm("mix_post")
            pre_norm("ffn_pre", 8)
            ahead("ffn_up_a", 0)

            first_start, first_conv = started[0], taken("ffn_up_a") - 1

            def low_inner(k, j, count):
                dve.wait_ge(f_hi, count)
                less(FL[:, dyn(k), :], CV[:, 2 * j, :], FH[:, dyn(k), :]).then_inc(f_ready, 1)

            def ffn_turn(name, p0, it, first_turn, slab0):
                turn = 0 if first_turn else it
                for j in range(2):
                    p = it * 2 + (p0 + j)
                    for half in range(2):
                        split_slab(slab0 + 2 * j + half, turn, R)
                        dve.wait_ge(conv0, p * 2 + (first_start + 1 + half))
                        b, out = tile_bank(name, 2 * j + half), CV[:, 2 * j + half, :]
                        for back in (1, 2):
                            last = stt(out=out[:, back:T], in0=b[:, 0:T - back], scalar=C[:, dyn((p * 2 + half) * 3 + (COL["ffn_w"] + 2 - back))],
                                       in1=out[:, back:T], op0=ALU.mult, op1=ALU.add)
                            if back == 1:
                                last.then_inc(tap_done, 1)
                                dve.wait_ge(tap_done, p * 2 + (half + 1))
                        last.then_inc(conv, 1)
                        if half == 0 and not (first_turn and j == 0):
                            low_inner(it * 2 + (j - 1), (j + 1) % 2, p * 1)
                    dve.wait_ge(gelu_done, p * 1 + 1)
                    dve.wait_ge(conv, p * 2 + (first_conv + 2))
                    tt(CV[:, 2 * j, :], CV[:, 2 * j, :], CV[:, 2 * j + 1, :], ALU.mult).then_inc(f32_ready, 1)

            def ffn_up(name, p0, following):
                slab0, turns = split[0], COUNT[name] // 4
                ffn_turn(name, p0, 0, True, slab0)
                with dve.Fori(1, turns) as it:
                    ffn_turn(name, p0, it, False, slab0)
                split[0] += 4 * turns
                ahead(*following)
                low_inner(2 * turns - 1, 1, p0 + 2 * turns)

            ffn_up("ffn_up_a", 0, ("ffn_down_a", 0))
            for n in range(KD):
                ahead("ffn_down_a", n)
            ffn_up("ffn_up_b", F_TILES, ("ffn_down_b", 0))
            for n in range(KD):
                ahead("ffn_down_b", n)
                dve.wait_ge(evac, taken("ffn_down_a", n))
                dve.wait_ge(unit, unit_of("ffn_down_b", n))
                tt(Y[:, n, :], Y[:, n, :], tile_bank("ffn_down_b", n)[:, 0:T], ALU.add).then_inc(y_sum, 1)
                add_square("ffn_post", n)
            post_norm("ffn_post")
            pre_norm("mix2_0", 16, "mix2")

            rows = slice(0, HEADS)
            ts(NB[:, :], col("b_forget", rows=rows), -1.0, None, ALU.mult).then_inc(cum_ready, 1)

            def forget_part(part):
                if part == 0:
                    dve.wait_ge(unit, unit_of("fa", 0))
                    dve.wait_ge(cum_ready, 1)
                softplus(part, 2, SP[rows, 0, :], tile_bank("fa", 0)[rows, 0:T], NB[:, :], -1.0,
                         [SP[rows, 1, :], SP[rows, 2, :], SP[rows, 3, :]], SP[rows, 4, :], cum_ready, 2)
                if part == 2:
                    dve.wait_ge(cum_ready, 2)
                    dve.tensor_tensor_scan(NCUM, ones[rows, :], SP[rows, 4, :], 0.0, ALU.mult, ALU.add).then_inc(cum_ready, 1)
                    dve.wait_ge(cum_ready, 3)
                    ts(CUM, NCUM, -1.0, None, ALU.mult).then_inc(cum_ready, 1)

            ahead("fa", 0)
            forget_part(0)

            def out_pair(pair):
                dve.wait_ge(o_hi, pair + 1)
                less(FL[:, pair % 8, :], N7[:, 0:T], FH[:, pair % 8, :]).then_inc(o_ready, 1)

            def scores_max(kind, i, n0, scale):
                n = n0 + i
                dve.wait_ge(s_mm, (n if kind != "mla" else n + HEADS) + 1)
                if kind == "chk":
                    dve.wait_ge(bias_ready, i + 1)
                if n >= 2:
                    dve.wait_ge(p_norm, n - 1)
                add = {"fox": neg_causal[:, :], "mla": neg_chunk[:, :], "chk": BIAS[:, i, :]}[kind]
                b = (N4, N5)[n % 2]
                for qb, (lo, cols) in enumerate(((0, P), (P, T))):
                    dve.tensor_tensor_reduce(out=S[:, n % 2, lo:lo + cols], in0=b[:, lo:lo + cols], in1=add[:, lo:lo + cols],
                                             scale=1.0, scalar=-3.0e38, op0=ALU.add, op1=ALU.max,
                                             accum_out=ST[:, n % 2, qb:qb + 1]).then_inc(s_max, 1)
                dve.wait_ge(s_max, 2 * (n + 1))
                ts(ST[:, n % 2, 2:4], ST[:, n % 2, 0:2], -scale, None, ALU.mult).then_inc(s_bias, 1)

            def normalised(n):
                dve.wait_ge(p_exp, 2 * (n + 1))
                if n >= 2:
                    dve.wait_ge(pt_mm, n - 1)
                link(dve.reciprocal(ST[:, n % 2, 6:8], ST[:, n % 2, 4:6]))
                ts(M[:, n % 2, 0:P], S[:, n % 2, 0:P], ST[:, n % 2, 6:7], None, ALU.mult)
                ts(M[:, n % 2, P:S3], S[:, n % 2, P:S3], ST[:, n % 2, 7:8], None, ALU.mult).then_inc(p_norm, 1)

            def softmax_step(kind, i, n0, o0, scale, norm_first):
                if norm_first and 1 <= i <= HEADS:
                    normalised(n0 + i - 1)
                if i < HEADS:
                    scores_max(kind, i, n0, scale)
                if not norm_first and 1 <= i <= HEADS:
                    normalised(n0 + i - 1)
                if i >= 4 and i % 2 == 0:
                    out_pair((o0 + i - 4) // 2)

            for name in ("q_fox", "k_fox", "v_fox"):
                for n in range(4):
                    ahead(name, n)
                    if name == "q_fox" and n in (1, 2):
                        forget_part(n)
            for m, name in enumerate(("q_chk", "k_chk", "v_chk")):
                for n in range(4):
                    ahead(name, n)
                    if 4 * m + n < HEADS + 3:
                        softmax_step("fox", 4 * m + n, 0, 0, 1.0, True)
            def add_tile(name, n):
                ahead(name, n)
                dve.wait_ge(unit, unit_of(name, n))
                tt(X[:, n, :], X[:, n, :], tile_bank(name, n)[:, 0:T], ALU.add).then_inc(x_ready, 1)

            def softmax_over(name, kind, n0, o0, scale):
                for i in range(HEADS + 3):
                    softmax_step(kind, i, n0, o0, scale, False)
                    if i < COUNT[name]:
                        add_tile(name, i)

            def add_residual(name, norm=None):
                for n in range(COUNT[name]):
                    if norm:
                        dve.wait_ge(x_ready, taken(name, n) - KD)
                    add_tile(name, n)
                    if norm and n >= 1:
                        add_square(norm, n - 1)
                if norm:
                    add_square(norm, COUNT[name] - 1)

            softmax_over("ab_out_a", "chk", 8, 8, 1.0)

            def mlp_up(name, f0):
                slab0 = split[0]
                with dve.Fori(0, F_TILES // 4) as it:
                    for j in range(4):
                        split_slab(slab0 + j, it, R)
                        dve.wait_ge(evac, it * 4 + (taken(name) + j))
                        dve.wait_ge(f_hi, it * 4 + (f0 + j + 1))
                        tt(RT[:, j, :], RT[:, j, :], RT[:, j, :], ALU.mult).then_inc(relu_done, 1)
                        dve.wait_ge(relu_done, it * 4 + (f0 - FFN_PAIRS + j + 1))
                        less(FL[:, dyn(it * 4 + j), :], RT[:, j, :], FH[:, dyn(it * 4 + j), :]).then_inc(f_ready, 1)
                split[0] += F_TILES

            add_residual("ab_out_b", "mlp2_0")
            pre_norm("mlp2_0", 24, "mlp2")
            ahead("mlp_up0a", 0)
            mlp_up("mlp_up0a", FFN_PAIRS)

            hi = slice(64, P)
            ang = lambda n: ANG[hi, n, :]
            ahead("mlp_down0a", 0)
            dve.wait_ge(pos_in, 16)
            link(dve.tensor_copy(ang(0), POS[hi, :]))
            link(ts(ang(1), ang(0), col("inv_freq", rows=hi), None, ALU.mult))
            link(ts(ang(2), ang(1), 1 / TWO_PI, None, ALU.mult))
            link(ts(ang(3), ang(2), ROUND, None, ALU.add))
            link(ts(ang(2), ang(3), -ROUND, None, ALU.add))
            for n, part in enumerate(TWO_PI_PARTS):
                link(stt(out=ang((3, 1, 3)[n]), in0=ang(2), scalar=-part, in1=ang((1, 3, 1)[n]), op0=ALU.mult, op1=ALU.add))
            link(ts(ang(1), ang(3), TWO_PI / 4, None, ALU.add))
            link(ts(ang(2), ang(1), PI_DOWN, -TWO_PI, ALU.is_gt, ALU.mult))
            link(tt(ang(1), ang(1), ang(2), ALU.add))
            ts(ang(4), ang(3), PI_DOWN, -PI_DOWN, ALU.min, ALU.max).then_inc(ang_ready, 1)
            ts(ang(5), ang(1), PI_DOWN, -PI_DOWN, ALU.min, ALU.max).then_inc(ang_ready, 1)

            add_residual("mlp_down0a")
            mlp_up("mlp_up0b", FFN_PAIRS + F_TILES)
            dve.wait_ge(sin_ready, 2)
            ts(SIN[hi, :], SIN[hi, :], col("rope_sign", rows=hi), None, ALU.mult).then_inc(trig_ready, 1)
            dve.memset(TQ[0:64, :], 1.0).then_inc(trig_ready, 1)
            dve.wait_ge(trig_ready, 2)
            dve.tensor_copy(TQ[64:96, :], COS[64:96, :]).then_inc(trig_ready, 1)
            dve.tensor_copy(TQ[96:P, :], SIN[96:P, :]).then_inc(trig_ready, 1)
            add_residual("mlp_down0b", "mix2_1")
            pre_norm("mix2_1", 32, "mix2", KD)
            for n in range(Q_KT):
                ahead("c_q", n)
                add_square("q_norm", n)

            def latent(name, k0, n):
                r = rstd(name)
                for k in range(k0, k0 + n):
                    stt(out=LAT[:, k, :], in0=LAT[:, k, :], scalar=col(name, k - k0), in1=r, op0=ALU.mult, op1=ALU.mult).then_inc(h32, 1)

            for n in range(KV_KT):
                ahead("c_kv", n)
            for n in range(4):
                ahead("q_sb", n)
                if n == 1:
                    add_square("kv_norm", 1)
                    latent("q_norm", 0, Q_KT)
                if n == 3:
                    latent("kv_norm", Q_KT, KV_KT)
            for name in ("k_sb", "v_sb"):
                for n in range(4):
                    ahead(name, n)

            def stick_step(i):
                if 1 <= i <= HEADS:
                    h, b = i - 1, (N5, N6)[(i - 1) % 2]
                    dve.wait_ge(arg_mm, h + 1)
                    if h >= 2:
                        dve.wait_ge(pv_mm, 16 + h - 1)
                    tt(M[:, h % 2, :], b[:, 0:S3], neg_strict[:, :], ALU.add).then_inc(arg_ready, 1)
                if i < HEADS:
                    h, b, s = i, (N5, N6)[i % 2], S[:, i % 2, :]
                    dve.wait_ge(z_ln, h + 1)
                    stt(out=s, in0=b[:, 0:S3], scalar=0.0, in1=s, op0=ALU.max, op1=ALU.add).then_inc(lm_ready, 1)
                    dve.wait_ge(lm_ready, 2 * h + 1)
                    tt(s, s, keep_strict[:, :], ALU.mult).then_inc(lm_ready, 1)
                if i >= 4 and i % 2 == 0:
                    out_pair(8 + (i - 4) // 2)

            for n in range(2):
                ahead("k_rope", n)
                stick_step(n)
            for k in range(Q_KT + KV_KT):
                low_hidden(k, 40, LAT)
            for n in range(HEADS):
                ahead("q_mla", n)
                dve.wait_ge(unit, unit_of("q_mla", n))
                tt(Q[:, n, :], tile_bank("q_mla", n)[:, 0:T], TQ, ALU.mult).then_inc(dve_take, 1)
                stick_step(n + 2)
            stick_step(HEADS + 2)
            dve.wait_ge(evac, taken("k_rope", 1))
            dve.wait_ge(trig_ready, 4)
            link(tt(KF[hi, :], KR[hi, 0, :], COS[hi, :], ALU.mult))
            link(tt(KR[hi, 1, :], KR[hi, 1, :], SIN[hi, :], ALU.mult))
            link(tt(KF[hi, :], KF[hi, :], KR[hi, 1, :], ALU.add))
            dve.tensor_copy(K[hi, :, :], KF[hi, :].unsqueeze(1).to_broadcast([64, HEADS, T])).then_inc(kcopy, 1)
            for name in ("k_mla", "v_mla"):
                for n in range(COUNT[name]):
                    ahead(name, n)
            softmax_over("cd_out_a", "mla", 16, 24, (64 + 32) ** -0.5)
            add_residual("cd_out_b", "mlp2_1")
            pre_norm("mlp2_1", 45, "mlp2", KD)
            ahead("mlp_up1a", 0)
            mlp_up("mlp_up1a", FFN_PAIRS + 2 * F_TILES)
            add_residual("mlp_down1a")
            mlp_up("mlp_up1b", FFN_PAIRS + 3 * F_TILES)
            add_residual("mlp_down1b", "final")
            r = rstd("final")
            for k in range(KD):
                stt(out=Y[:, k, :], in0=X[:, k, :], scalar=col("final", k), in1=r, op0=ALU.mult, op1=ALU.mult).then_inc(out_ready, 1)


def features(v):
    return np.asarray(v).reshape(-1, P).T


def blocks(w):
    k, n = w.shape
    return w.reshape(k // P, P, n // P, P).transpose(2, 0, 1, 3).reshape(-1, P, P)


def kernel(**given):
    import concourse.bacc as bacc
    from concourse.bass_utils import run_bass_kernel_spmd

    inp = {k: np.asarray(v) for k, v in given.items()}
    f32 = np.float32
    w_in = inp["w_in"][0]
    at = np.cumsum([0, 1024, 1536, 16, 1024, 1024, 2048])
    z, xbc, dt, ly, lx, g = (w_in[:, a:b] for a, b in zip(at[:-1], at[1:]))
    up = inp["w_ffn_up"][0].reshape(D, 2, FFN_PAIRS, P).transpose(0, 2, 1, 3).reshape(D, -1)
    w_ab, w_cd = inp["w_in_ab_2"][0], inp["w_in_cd_2"][0]
    at = np.cumsum([0, 512, 512, 512, 8, 512, 512, 512])
    qa, ka, va, fa, qb, kb, vb = (w_ab[:, a:b] for a, b in zip(at[:-1], at[1:]))
    at = np.cumsum([0, 512, 512, 512, 384, 256, 32])
    qc, kc, vc, cq, ckv, kr = (w_cd[:, a:b] for a, b in zip(at[:-1], at[1:]))
    swap = lambda w: np.concatenate([w[..., 16:32], w[..., 0:16]], axis=-1)
    none = np.zeros((D, 64), f32)
    rope = np.concatenate([none, kr, kr, none, swap(kr), swap(kr)], axis=1)
    uq = inp["w_uq_2"][0].reshape(-1, HEADS, 96)
    uq = np.concatenate([uq, swap(uq[..., 64:96])], axis=-1).reshape(-1, HEADS * P)
    ukv = inp["w_ukv_2"][0].reshape(-1, HEADS, P)
    uk = np.concatenate([ukv[..., 0:64], np.zeros_like(ukv[..., 0:64])], axis=-1).reshape(-1, HEADS * P)
    uv = ukv[..., 64:128].reshape(-1, HEADS * 64)
    ups, downs = inp["w_up_2"], inp["w_down_2"]
    widen = lambda w: np.pad(w, ((0, 0), (0, P - w.shape[1])))
    down = inp["w_ffn_down"][0]
    n_up, n_in = 2 * F_TILES * P, F_TILES * P

    halves = lambda w: (w[:D // 2], w[D // 2:])

    def mlp(l):
        return [ups[l][:, :n_in], downs[l][:n_in], ups[l][:, n_in:], downs[l][n_in:]]

    weights = [widen(dt), xbc, ly, lx, z, g[:, :D], inp["w_proj_ssm"][0], g[:, D:], inp["w_proj_lru"][0], inp["w_out"][0],
               up[:, :n_up], down[:n_in], up[:, n_up:], down[n_in:], widen(fa), qa, ka, va, qb, kb, vb,
               *halves(inp["w_out_ab_2"][0]), *mlp(0), cq, ckv, qc, kc, vc, rope, uq, uk, uv, *halves(inp["w_out_cd_2"][0]), *mlp(1)]
    for w, (name, count, depth) in zip(weights, LAYERS, strict=True):
        assert w.shape == (depth * P, count * P), (name, w.shape)
    stream = np.concatenate([blocks(w) for w in weights])
    assert len(stream) == SLABS * BLOCKS
    stream = stream.reshape(SLABS, BLOCKS, P, P).transpose(0, 2, 1, 3).reshape(SLABS, P, BLOCKS * P)

    consts = np.zeros((P, NCOL), f32)

    def put(name, v, row=0):
        consts[row:row + v.shape[0], COL[name]:COL[name] + v.shape[1]] = v

    def taps(w):
        return w.reshape(len(w), -1, P).transpose(2, 1, 0).reshape(P, -1)

    by_turns = lambda v: v.reshape(-1, 2, FFN_PAIRS, P).transpose(0, 2, 1, 3).reshape(len(v), -1)
    put("mix_pre", features(inp["mix_pre_norm"]))
    put("mix_post", features(inp["mix_post_norm"]))
    put("xbc_w", taps(inp["ssm_conv_w"][0]))
    put("xbc_b", features(inp["ssm_conv_b"]))
    put("skip", features(np.repeat(inp["ssm_d"][0], 64)))
    put("ssm_norm", features(inp["ssm_norm"]))
    put("lx_w", taps(inp["lru_conv_w"][0]))
    put("lx_b", features(inp["lru_conv_b"]))
    put("br", features(inp["lru_br"]))
    put("bi", features(inp["lru_bi"]))
    put("lam", features(inp["lru_lambda"]))
    put("gate_b", features(inp["gate_b"]))
    put("ffn_pre", features(inp["ffn_pre_norm"]))
    put("ffn_post", features(inp["ffn_post_norm"]))
    put("ffn_w", taps(by_turns(inp["ffn_conv_w"][0])))
    put("ffn_b", features(by_turns(inp["ffn_conv_b"])))
    put("mix2", features(inp["norm_mix_2"]))
    put("mlp2", features(inp["norm_mlp_2"]))
    put("final", features(inp["norm_final_2"]))
    put("q_norm", features(inp["q_norm_2"]))
    put("kv_norm", features(inp["kv_norm_2"]))
    put("dt_bias", inp["ssm_dt_bias"].T)
    put("a_log", inp["ssm_a_log"].T)
    put("b_forget", inp["b_forget_2"].T)
    half = 16
    inv_freq = (f32(10000.0) ** (-np.arange(half, dtype=f32) / f32(half))).astype(f32)
    put("inv_freq", np.tile(inv_freq, 4)[:, None], 64)
    put("rope_sign", np.tile(np.repeat(np.array([-1, 1], f32), half), 2)[:, None], 64)

    q, k = np.arange(P)[:, None], np.arange(P)[None, :]
    rel = np.concatenate([q - k, q + P - k, q - k], axis=1) + CHUNK - 1
    rel = inp["rel_bias_2"][0][:, np.clip(rel, 0, N_REL - 1)].transpose(1, 0, 2)

    diag = lambda w: w.reshape(KD, 2, 64, 64).transpose(1, 2, 0, 3)
    arrays = dict(
        x_t=inp["x"][0].T.reshape(KD, P, T).transpose(1, 0, 2), consts=consts, positions=inp["positions_2"].astype(np.int32),
        stream=stream, lru_r=diag(inp["lru_wr"][0]), lru_i=diag(inp["lru_wi"][0]), rel=rel)
    nc = bacc.Bacc("TRN2", target_bir_lowering=False, num_devices=1)
    arrays = {n: np.ascontiguousarray(v) for n, v in arrays.items()}
    aps = {n: nc.dram_tensor(f"in_{n}", v.shape, mybir.dt.from_np(v.dtype), kind="ExternalInput").ap() for n, v in arrays.items()}
    out = nc.dram_tensor("out_t", (P, KD, T), mybir.dt.float32, kind="ExternalOutput").ap()
    build(nc, out_t=out, **aps)
    r = run_bass_kernel_spmd(nc, [{f"in_{n}": v for n, v in arrays.items()}], core_ids=[0])
    got = r.results[0]["out_t"]
    return np.ascontiguousarray(got.transpose(2, 1, 0).reshape(1, T, D))
```

```python
import concourse.bass as bass
import numpy as np
from concourse import mybir

P = 128
T = 256
TB = T // P
D = 1024
KD = D // P
EPS = 1e-6
NEG = -1.0e30
CHUNK = 64

SSM_TILES = 8
XBC_TILES = 12
SSM_HEADS = 16
FFN_PAIRS = 24
MLP_TILES = 32
F_TILES = 16
HEADS = 8
N_REL = 320
Q_KT, KV_KT = 3, 2

R = 4
BLOCKS = 8
BANKS = 4
S3 = 3 * P


LAYERS = [
    ("dt", 1, KD), ("xbc", XBC_TILES, KD), ("ly", KD, KD), ("lx", KD, KD), ("z", KD, KD), ("g0", KD, KD),
    ("proj_ssm", KD, KD), ("g1", KD, KD), ("proj_lru", KD, KD), ("mix_out", KD, KD),
    ("ffn_up_a", 2 * F_TILES, KD), ("ffn_down_a", KD, F_TILES),
    ("ffn_up_b", 2 * (FFN_PAIRS - F_TILES), KD), ("ffn_down_b", KD, FFN_PAIRS - F_TILES),
    ("fa", 1, KD), ("q_fox", 4, KD), ("k_fox", 4, KD), ("v_fox", 4, KD),
    ("q_chk", 4, KD), ("k_chk", 4, KD), ("v_chk", 4, KD), ("ab_out_a", KD, 4), ("ab_out_b", KD, 4),
    ("mlp_up0a", F_TILES, KD), ("mlp_down0a", KD, F_TILES), ("mlp_up0b", F_TILES, KD), ("mlp_down0b", KD, F_TILES),
    ("c_q", Q_KT, KD), ("c_kv", KV_KT, KD), ("q_sb", 4, KD), ("k_sb", 4, KD), ("v_sb", 4, KD), ("k_rope", 2, KD),
    ("q_mla", HEADS, Q_KT), ("k_mla", HEADS, KV_KT), ("v_mla", 1, KD), ("cd_out_a", KD, 4), ("cd_out_b", KD, 4),
    ("mlp_up1a", F_TILES, KD), ("mlp_down1a", KD, F_TILES), ("mlp_up1b", F_TILES, KD), ("mlp_down1b", KD, F_TILES),
]

VALUES = ("v_fox", "v_chk", "v_sb", "v_mla")
WIDE = 4 * P


def plan():
    first, tiles, block, units, last_unit = {}, [], 0, 0, {}
    for name, count, depth in LAYERS:
        first[name] = len(tiles)
        for _ in range(count):
            pieces = []
            for k in range(depth):
                slab = block // BLOCKS
                if not pieces or pieces[-1][0] != slab:
                    pieces.append((slab, []))
                pieces[-1][1].append((block % BLOCKS, k))
                block += 1
            units += len(pieces)
            for n, (slab, _) in enumerate(pieces):
                last_unit[slab] = units - len(pieces) + n + 1
            tiles.append((pieces, units, depth))
    return first, tiles, -(-block // BLOCKS), last_unit


FIRST, TILES, SLABS, LAST_UNIT = plan()
COUNT = {name: count for name, count, _ in LAYERS}


def columns():
    at, n = {}, 0
    for name, width in [
        ("mix_pre", 8), ("mix_post", 8), ("xbc_w", 48), ("xbc_b", 12), ("skip", 8), ("ssm_norm", 8), ("lx_w", 32),
        ("lx_b", 8), ("br", 8), ("bi", 8), ("lam", 8), ("gate_b", 16), ("ffn_pre", 8), ("ffn_post", 8),
        ("ffn_w", 3 * 48), ("ffn_b", 48), ("mix2", 16), ("mlp2", 16), ("final", 8), ("q_norm", 3), ("kv_norm", 2),
        ("dt_bias", 1), ("a_log", 1), ("b_forget", 1), ("inv_freq", 1), ("rope_sign", 1),
    ]:
        at[name] = n
        n += width
    return at, n


COL, NCOL = columns()

TWO_PI = 6.283185307179586
TWO_PI_PARTS = (6.28125, 0.0019340515136718750, TWO_PI - 6.28125 - 0.0019340515136718750)
PI_DOWN = 3.1415925
ROUND = 12582912.0

NORMS = [
    ("mix_pre", 8, 1 / D), ("ssm0", 4, 2 / D), ("ssm1", 4, 2 / D), ("mix_post", 8, 1 / D), ("ffn_pre", 8, 1 / D),
    ("ffn_post", 8, 1 / D), ("mix2_0", 8, 1 / D), ("mlp2_0", 8, 1 / D), ("mix2_1", 8, 1 / D),
    ("q_norm", Q_KT, 1 / (Q_KT * P)), ("kv_norm", KV_KT, 1 / (KV_KT * P)), ("mlp2_1", 8, 1 / D), ("final", 8, 1 / D),
]
NORM = {name: i for i, (name, _, _) in enumerate(NORMS)}
ADDS = [sum(n - 2 for _, n, _ in NORMS[:i]) for i in range(len(NORMS) + 1)]
SQ_SLOTS = 8
SQUARES = [sum(n for _, n, _ in NORMS[:i]) for i in range(len(NORMS) + 1)]


def build(nc, x_t, consts, positions, stream, lru_r, lru_i, rel, out_t):
    fp32, fp32r, bf16, i32 = mybir.dt.float32, mybir.dt.float32r, mybir.dt.bfloat16, mybir.dt.int32
    ALU, ACT = mybir.AluOpType, mybir.ActivationFunctionType
    sb = lambda name, *shape, dt=fp32: nc.alloc_sbuf_tensor(name, list(shape), dt)

    RAW = sb("weights_raw", P, R, BLOCKS * P)
    WH = sb("weights_hi", P, R, BLOCKS * P, dt=fp32r)
    WL = sb("weights_lo", P, R, BLOCKS * P, dt=fp32r)
    C = sb("consts", P, NCOL)
    X = sb("residual", P, KD, T)
    HH, HL = (sb(f"hidden_{part}", P, KD, T, dt=fp32r) for part in ("hi", "lo"))
    FH, FL = (sb(f"inner_{part}", P, F_TILES, T, dt=fp32r) for part in ("hi", "lo"))
    SQ = sb("squares", P, SQ_SLOTS, T)
    ACC = sb("square_sum", P, T)
    RS = sb("rstd_columns", P, 3, TB)
    A = sb("arena", P, 72, T)
    ident = sb("ident", P, P)
    ones = sb("ones", P, T)
    keep_incl = sb("keep_incl", P, S3, dt=bf16)
    keep_strict = sb("keep_strict", P, S3, dt=bf16)
    neg_strict = sb("neg_strict", P, S3, dt=bf16)
    neg_causal = sb("neg_causal", P, S3, dt=bf16)
    neg_chunk = sb("neg_chunk", P, S3, dt=bf16)
    neg_tri = sb("neg_tri", P, P)
    neg_one = sb("neg_one", P, P)
    S = sb("scores", P, 2, S3)
    M = sb("weights", P, 2, S3)
    PT = sb("weights_turned", P, 2, S3)
    ST = sb("stats", P, 2, 8)
    POS = sb("positions_sb", P, T, dt=i32)
    EPSC = sb("eps_column", P, 1)
    a = lambda lo, n: A[:, lo:lo + n, :]
    flat = lambda lo, n: A[:, lo:lo + n, :].rearrange("p a t -> p (a t)")
    XS, BC, XC, GATE, ZS, G = a(0, 8), a(8, 4), a(12, 8), a(20, 8), a(28, 8), a(36, 8)
    CBM = flat(8, 3).rearrange("p (g n) -> p g n", g=2)
    XDT = flat(44, 8).rearrange("p (b h d) -> p b h d", b=TB, d=64)
    YS, IG = a(52, 8), a(60, 8)
    TH, AG = XS, a(44, 8)
    MG = ZS
    Y = XC
    HT = a(68, 4)
    BLKR, BLKI = IG[:, :, 0:P], IG[:, :, P:T]
    CV = a(28, 4)
    SP = a(51, 5)
    Q, K = a(0, 8), a(8, 8)
    V = flat(16, 4).rearrange("p (b n) -> p b n", b=TB)
    Q2, K2 = a(20, 4), a(24, 4)
    V2 = flat(28, 4).rearrange("p (b n) -> p b n", b=TB)
    AQ, BK = a(32, 4), a(36, 4)
    CUM, NCUM = A[0:HEADS, 40, :], A[0:HEADS, 41, :]
    LAT = a(42, 5)
    KF, TQ, COS, SIN, KR, ANG = A[:, 47, :], A[:, 48, :], A[:, 49, :], A[:, 50, :], a(51, 2), a(20, 6)
    BIAS = flat(56, 12).rearrange("p (h n) -> p h n", n=S3)
    RT = a(0, 4)
    DT, ACS = sb("dt_steps", 16, T), sb("a_cumsum", 16, T)
    NEGA = sb("neg_a", 16, 1)
    COLS = sb("dt_columns", P, TB, 2, SSM_HEADS)
    LSP = sb("lru_softplus", P, 6, KD)
    HB = sb("half_biases", P, 32)
    NB = sb("neg_b_forget", HEADS, 1)

    bank = [nc.alloc_psum_tensor(f"bank{i}", [P, 512], fp32) for i in range(8)]
    N4, N5, N6, N7 = bank[4:]
    Z = (N4, N5, N6)

    def sum_at(norm):
        return TB if norm == "ssm1" else 0

    def spread_at(norm):
        return N7[:, T:2 * T] if norm == "ssm1" else N7[:, 0:T]

    def sems(names):
        return [nc.alloc_semaphore(name) for name in names.split()]

    slab_in = [nc.alloc_semaphore(f"slab_in{s}") for s in range(R)]
    consts_in, blk_in, bias_in, pos_in = sems("consts_in blk_in bias_in pos_in")
    x_in = sems("x_in0 x_in1")
    tables, blk_zero, bias_ready = sems("tables blk_zero bias_ready")
    unit, = sems("unit_done")
    hi_ready, = sems("weights_hi_ready")
    lo_ready = [nc.alloc_semaphore(f"weights_lo_ready{s}") for s in range(R)]
    squared, added, ms_ready = sems("squared squares_added ms_ready")
    std_ready, rstd_ready, spread = sems("std_ready rstd_ready rstd_spread")
    h32, h_hi, h_ready, x_ready, step = sems("h_float32 h_hi h_ready x_ready dve_step")
    evac, conv, conv0, act_in, dve_take, y_evac = sems("evac conv_done conv_started act_in_place dve_take y_evac")
    tap_done, u_taken, y_sum = sems("tap_done u_taken y_sum")
    sp_in, sp_exp, dt_ready, nega, acs_ready = sems("softplus_in softplus_exp dt_ready neg_a acs_ready")
    colt, cols_ready, xst, xdt_ready, cbt, cbm_ready = sems("colt cols_ready xs_turned xdt_ready cb_done cbm_ready")
    bcast, seg_ready, decay_ready, m_ready, y_mm = sems("acs_broadcast seg_ready decay_ready m_ready y_mm")
    ys_ready, yg_ready, yn_ready, ya_hi, ya_ready = sems("ys_ready yg_ready yn_ready ya_hi ya_ready")
    lam_ready, half_bias, rg_mm, rg_ready, ag_ready, th_ready = sems("lam_ready half_bias rg_mm rg_ready ag_ready th_ready")
    m2_ready, ix_ready, mult_ready, bx_ready, scanned = sems("m2_ready ix_ready mult_ready bx_ready scanned")
    y_normed, = sems("y_normed")
    yb32, yb_hi, yb_ready, mg32, mg_hi, mg_ready = sems("yb_float32 yb_hi yb_ready merged_float32 merged_hi merged_ready")
    gelu_done, f32_ready, f_hi, f_ready = sems("gelu_done f_float32 f_hi f_ready")
    relu_done, zs_ready = sems("relu_done zs_ready")
    cum_ready, dtile_zero, dtile_in = sems("cum_ready dtile_zero dtile_in")
    s_mm, s_max, s_bias, p_exp, p_norm, pt_mm = sems("scores_done scores_max exp_bias weights_exp weights_normed turned")
    pt_ready, pv_mm, o_hi, o_ready = sems("turned_out pv_done heads_hi heads_out")
    z_abs, z_exp, z_ln, lm_ready, arg_mm, arg_ready, a_exp = sems("z_abs z_exp z_ln lm_ready arg_mm arg_ready a_exp")
    ang_ready, sin_ready, trig_ready, kcopy = sems("ang_ready sin_ready trig_ready kcopy")
    out_ready, stored = sems("out_ready stored")

    FREE, counts = {}, {x_ready: 2 * KD}

    def value_at(layer):
        return COUNT[layer] - TB if COUNT[layer] > 1 else 0

    def frees(layer, s):
        if layer in VALUES:
            c = counts[s]
            counts[s] += TB
            for n in range(COUNT[layer]):
                t = FIRST[layer] + n
                FREE[t] = (s, c + n + 1 - value_at(layer)) if n >= value_at(layer) else FREE[t - BANKS]
            return
        for n in range(COUNT[layer]):
            counts[s] = counts.get(s, 0) + 1
            FREE[FIRST[layer] + n] = (s, counts[s])

    def taken(layer, n=0):
        if layer in VALUES:
            return FREE[FIRST[layer] + value_at(layer)][1] + n
        return FREE[FIRST[layer] + n][1]

    for names, s in [("dt", u_taken), ("xbc", conv), ("ly", evac), ("lx", conv), ("z", dve_take), ("g0", evac),
                     ("proj_ssm", dve_take), ("g1", evac), ("proj_lru", dve_take), ("mix_out", y_evac), ("ffn_up_a", conv),
                     ("ffn_down_a", evac), ("ffn_up_b", conv), ("ffn_down_b", y_sum), ("fa", u_taken),
                     ("q_fox k_fox v_fox q_chk k_chk v_chk", evac), ("ab_out_a ab_out_b", x_ready), ("mlp_up0a", evac),
                     ("mlp_down0a", x_ready), ("mlp_up0b", evac), ("mlp_down0b", x_ready),
                     ("c_q c_kv q_sb k_sb v_sb k_rope", evac), ("q_mla", dve_take), ("k_mla v_mla", evac),
                     ("cd_out_a cd_out_b", x_ready), ("mlp_up1a", evac), ("mlp_down1a", x_ready), ("mlp_up1b", evac),
                     ("mlp_down1b", x_ready)]:
        for name in names.split():
            frees(name, s)

    def col(name, n=0, rows=slice(0, P)):
        return C[rows, COL[name] + n:COL[name] + n + 1]

    def col_n(name, n):
        return C[:, COL[name]:COL[name] + n]

    def dyn(i):
        return slice(i, i + 1) if isinstance(i, int) else bass.ds(i, 1)

    def tile_bank(layer, n):
        return bank[(FIRST[layer] + n) % BANKS]

    def unit_of(layer, n):
        return TILES[FIRST[layer] + n][1]

    def slab_of(layer, n):
        return TILES[FIRST[layer] + n][0][-1][0]

    def square_used(q):
        i = max(i for i in range(len(NORMS)) if SQUARES[i] <= q)
        k = q - SQUARES[i]
        n = NORMS[i][1]
        return (ms_ready, i + 1) if k == n - 1 or n == 2 else (added, ADDS[i] + max(k, 1))

    ALL_TABLES = 22

    block = nc.Block()
    with block:
        @block.sync
        def _(sp):
            for half in range(2):
                sp.dma_start(X[:, 4 * half:4 * half + 4, :], x_t[:, 4 * half:4 * half + 4, :]).then_inc(x_in[half], 16)
            sp.dma_start(C[:, :], consts).then_inc(consts_in, 16)
            for s in range(R):
                sp.dma_start(RAW[:, s, :], stream[s]).then_inc(slab_in[s], 16)
            turns = SLABS // R

            def reload(turn, s):
                sp.wait_ge(lo_ready[s], turn * 1)
                sp.dma_start(RAW[:, s, :], stream[turn * R + s]).then_inc(slab_in[s], 16)

            middle = (slab_of("k_fox", 0) + 2 * R) // R
            with sp.Fori(1, middle) as it:
                for s in range(R):
                    reload(it, s)
            for s in range(R):
                reload(middle, s)
                if s == 0:
                    sp.wait_ge(dtile_zero, 6)
                    sp.wait_ge(cum_ready, 4)
                for h in range(2 * s, 2 * s + 2):
                    row = 64 * (h % 2)
                    sp.dma_start(AQ[row + 1:row + 2, h // 2, :], CUM[h:h + 1, :]).then_inc(dtile_in, 16)
                    sp.dma_start(BK[row:row + 1, h // 2, :], NCUM[h:h + 1, :]).then_inc(dtile_in, 16)
            with sp.Fori(middle + 1, turns) as it:
                for s in range(R):
                    reload(it, s)
            for i in range(R * turns, SLABS):
                sp.wait_ge(lo_ready[i % R], i // R)
                sp.dma_start(RAW[:, i % R, :], stream[i]).then_inc(slab_in[i % R], 16)
            for k in range(KD):
                sp.wait_ge(out_ready, k + 1)
                sp.dma_start(out_t[:, k, :], Y[:, k, :]).then_inc(stored, 16)
            sp.wait_ge(stored, 16 * KD)

        @block.gpsimd
        def _(pool):
            pool.dma_start(POS[:, :], positions.to_broadcast([P, T])).then_inc(pos_in, 16)
            for tile, value in ((ones, 1.0), (EPSC, EPS), (ident, 0.0)):
                pool.memset(tile[:, :], value).then_inc(tables, 1)
            pool.wait_ge(tables, 3)
            pool.affine_select(out=ident[:, :], in_=ident[:, :], compare_op=ALU.not_equal, fill=1.0, base=0,
                               pattern=[[-1, P]], channel_multiplier=1).then_inc(tables, 1)
            pool.memset(BLKR, 0.0).then_inc(blk_zero, 1)
            pool.memset(BLKI, 0.0).then_inc(blk_zero, 1)
            pool.wait_ge(blk_zero, 2)
            for dst, src in ((BLKR, lru_r), (BLKI, lru_i)):
                for half in range(2):
                    rows = slice(64 * half, 64 * half + 64)
                    pool.dma_start(dst[rows, :, rows], src[half]).then_inc(blk_in, 16)
            fills = [(keep_incl, 1.0), (keep_strict, 1.0), (neg_strict, 0.0),
                     (neg_causal, 0.0), (neg_chunk, 0.0), (neg_tri, -1.0), (neg_one, -1.0)]
            for tile, value in fills:
                pool.memset(tile[:, :], value).then_inc(tables, 1)
            pool.wait_ge(tables, 4 + len(fills))
            for tile, fill, base, row, colm in [(keep_incl, 0.0, 0, -1, 1), (keep_strict, 0.0, -1, -1, 1),
                                                (neg_strict, NEG, -1, -1, 1), (neg_causal, NEG, 0, 1, -1)]:
                for d in (0, 2):
                    part = tile[:, d * P:d * P + P]
                    pool.affine_select(out=part, in_=part, compare_op=ALU.is_ge, fill=fill, base=base,
                                       pattern=[[colm, P]], channel_multiplier=row).then_inc(tables, 1)
            for d in (0, 2):
                part = neg_chunk[:, d * P + CHUNK:d * P + P]
                pool.affine_select(out=part, in_=part, compare_op=ALU.is_ge, fill=NEG, base=-CHUNK,
                                   pattern=[[0, CHUNK]], channel_multiplier=1).then_inc(tables, 1)
            pool.affine_select(out=neg_tri[:, :], in_=neg_tri[:, :], compare_op=ALU.is_ge, fill=0.0, base=0,
                               pattern=[[-1, P]], channel_multiplier=1).then_inc(tables, 1)
            split = [R - 1]

            def split_slab(i, turn=0):
                pool.wait_ge(hi_ready, turn * R + (i + 1))
                pool.tensor_tensor(WL[:, R - 1, :], RAW[:, R - 1, :], WH[:, R - 1, :].bitcast(fp32), ALU.subtract).then_inc(lo_ready[R - 1], 1)

            def ahead(name, n):
                while split[0] < min(slab_of(name, n) + R, SLABS):
                    split_slab(split[0])
                    split[0] += R

            def through(name):
                turns = (min(slab_of(name, COUNT[name] - 1) + R, SLABS) - split[0] + R - 1) // R
                with pool.Fori(0, turns) as it:
                    split_slab(split[0], it)
                split[0] += R * turns

            through("proj_ssm")

            def recurrence_out(j):
                pool.wait_ge(scanned, j + 1)
                pool.tensor_tensor(GATE[:, j, :], XC[:, j, :], GATE[:, j, :], ALU.mult).then_inc(yb32, 1)

            for n in range(KD):
                ahead("g1", n)
                pool.wait_ge(mult_ready, n + 1)
                pool.wait_ge(ix_ready, n + 1)
                pool.tensor_tensor(IG[:, n, :], IG[:, n, :], TH[:, n, :], ALU.mult).then_inc(bx_ready, 1)
                if n >= 1:
                    recurrence_out(n - 1)
            recurrence_out(KD - 1)
            for n in range(KD):
                ahead("proj_lru", n)
                pool.wait_ge(dve_take, taken("proj_lru", n))
                pool.tensor_tensor(MG[:, n, :], MG[:, n, :], HT[:, n % 4, :], ALU.add).then_inc(mg32, 1)
            through("mix_out")

            posts = [0]

            def post_add():
                for k in range(KD):
                    pool.wait_ge(y_normed, posts[0] + k + 1)
                    pool.tensor_tensor(X[:, k, :], X[:, k, :], Y[:, k, :], ALU.add).then_inc(x_ready, 1)
                posts[0] += KD

            post_add()
            pool.dma_start(BIAS, rel).then_inc(bias_in, 16)
            for h in range(HEADS):
                ahead("ffn_up_a", R * h)
                pool.wait_ge(bias_in, 16)
                pool.tensor_tensor(BIAS[:, h, :], BIAS[:, h, :], neg_chunk[:, :], ALU.add).then_inc(bias_ready, 1)
            through("ffn_up_a")
            pool.memset(AQ, 0.0).then_inc(dtile_zero, 1)
            ahead("ffn_down_a", 1)
            pool.memset(BK, 0.0).then_inc(dtile_zero, 1)
            ahead("ffn_down_a", 3)
            pool.wait_ge(dtile_zero, 2)
            pool.wait_ge(lo_ready[R - 1], split[0] // R)
            for base in (0, 64):
                pool.memset(AQ[base:base + 2], 1.0).then_inc(dtile_zero, 1)
                pool.memset(BK[base:base + 2], 1.0).then_inc(dtile_zero, 1)
            pool.wait_ge(dtile_zero, 6)
            through("ffn_down_b")
            post_add()

            def add_squares_with(name, norm):
                i = NORM[norm]
                sq = lambda n: SQ[:, (SQUARES[i] + n) % SQ_SLOTS, :]
                for n in range(COUNT[name]):
                    ahead(name, n)
                    if 1 <= n <= COUNT[name] - 2:
                        pool.wait_ge(squared, SQUARES[i] + n + 1)
                        pool.wait_ge(*((ms_ready, i) if n == 1 else (added, ADDS[i] + n - 1)))
                        pool.tensor_tensor(ACC[:, :], sq(0) if n == 1 else ACC[:, :], sq(n), ALU.add).then_inc(added, 1)

            through("ab_out_a")
            add_squares_with("ab_out_b", "mlp2_0")
            through("cd_out_a")
            add_squares_with("cd_out_b", "mlp2_1")
            through("mlp_down1b")

        @block.tensor
        def _(pe):
            def block_products(out, slot, blk, hi, lo, first, last):
                cols = slice(blk * P, blk * P + P)
                for n, (w, x) in enumerate(((WH, hi), (WH, lo), (WL, hi))):
                    mm = pe.matmul(out, w[:, slot, cols], x, start=(first and n == 0), stop=(last and n == 2))
                return mm

            def dense_tile(t, hi, lo, ready=None):
                pieces, _, depth = TILES[t]
                b = bank[t % BANKS]
                if t >= BANKS:
                    pe.wait_ge(*FREE[t - BANKS])
                for slab, blocks in pieces:
                    pe.wait_ge(lo_ready[slab % R], slab // R + 1)
                    for blk, k in blocks:
                        if ready:
                            pe.wait_ge(ready[0], ready[1] + k + 1)
                        mm = block_products(b[:, 0:T], slab % R, blk, hi[:, k, :], lo[:, k, :], k == 0, k == depth - 1)
                    mm.then_inc(unit, 1)

            def value_layer(name, hi, lo, second=None, hooks=None):
                t0, n_k = FIRST[name], 2 * COUNT[name]
                b0 = t0 + value_at(name)
                banks = (bank[b0 % BANKS], second or bank[(b0 + 1) % BANKS])
                for n in range(COUNT[name]):
                    (slab, _), = TILES[t0 + n][0]
                    pe.wait_ge(lo_ready[slab % R], slab // R + 1)
                    for k in (2 * n, 2 * n + 1):
                        cols = slice(k % 2 * WIDE, k % 2 * WIDE + WIDE)
                        for half in range(TB):
                            if k == 0 and (half == 0 or second is None):
                                pe.wait_ge(*FREE[b0 + half - BANKS])
                            for m, (w, x) in enumerate(((WH, hi), (WH, lo), (WL, hi))):
                                mm = pe.matmul(banks[half][:, :], x[:, k, half * P:half * P + P], w[:, slab % R, cols],
                                               start=(k == 0 and m == 0), stop=(k == n_k - 1 and m == 2))
                    mm.then_inc(unit, 1)
                    if hooks and n in hooks:
                        hooks[n]()

            in_front = set()

            def front(name, hi, lo, ready, count=3):
                tiles = range(FIRST[name], FIRST[name] + count)
                in_front.update(tiles)
                for t in tiles:
                    if t >= BANKS:
                        pe.wait_ge(*FREE[t - BANKS])
                depth = TILES[tiles[0]][2]
                for k in range(depth):
                    pe.wait_ge(ready[0], ready[1] + k + 1)
                    for t in tiles:
                        (slab, blocks), = TILES[t][0]
                        if k == 0:
                            pe.wait_ge(lo_ready[slab % R], slab // R + 1)
                        mm = block_products(bank[t % BANKS][:, 0:T], slab % R, blocks[k][0], hi[:, k, :], lo[:, k, :], k == 0, k == depth - 1)
                        if k == depth - 1:
                            mm.then_inc(unit, 1)

            def layer(name, hi, lo, hooks=None, ready=None, **kw):
                for n in range(COUNT[name]):
                    if FIRST[name] + n not in in_front:
                        dense_tile(FIRST[name] + n, hi, lo, ready=ready if n == 0 else None, **kw)
                    if hooks and n in hooks:
                        hooks[n]()

            def loop_layer(name, hi, lo, per, ready=None):
                t0, depth = FIRST[name], TILES[FIRST[name]][2]
                slabs = depth // BLOCKS
                s0 = TILES[t0][0][0][0]
                assert per * slabs % R == 0 and per % BANKS == 0 and COUNT[name] % per == 0
                own, first_taken = FREE[t0]
                for n in range(per):
                    if t0 + n not in in_front:
                        dense_tile(t0 + n, hi, lo, ready=ready if n == 0 else None)
                if COUNT[name] == per:
                    return
                with pe.Fori(1, COUNT[name] // per) as it:
                    for j in range(per):
                        pe.wait_ge(own, it * per + (first_taken + j - BANKS))
                        for s in range(slabs):
                            slab = s0 + j * slabs + s
                            pe.wait_ge(lo_ready[slab % R], it * (per * slabs // R) + (slab // R + 1))
                            for blk in range(BLOCKS):
                                k = s * BLOCKS + blk
                                mm = block_products(bank[(t0 + j) % BANKS][:, 0:T], slab % R, blk, hi[:, k, :], lo[:, k, :],
                                                    k == 0, k == depth - 1)
                            mm.then_inc(unit, 1)

            def sum_square(name):
                i = NORM[name]
                if i:
                    pe.wait_ge(std_ready, i if name != "ssm1" else i - 1)
                n = NORMS[i][1]
                sq = lambda k: SQ[:, (SQUARES[i] + k) % SQ_SLOTS, :]
                for last, term in enumerate((ACC if n > 2 else sq(0), sq(n - 1))):
                    if last:
                        pe.wait_ge(squared, SQUARES[i] + n)
                    elif n > 2:
                        pe.wait_ge(added, ADDS[i + 1])
                    else:
                        pe.wait_ge(squared, SQUARES[i] + 1)
                    for b in range(TB):
                        at = sum_at(name) + b
                        mm = pe.matmul(N4[:, at:at + 1], term[:, b * P:b * P + P], ones[:, 0:1], start=(not last and b == 0),
                                       stop=(last == 1 and b == TB - 1), skip_group_check=True)
                mm.then_inc(ms_ready, 1)

            def spread_rstd(name, wait=None):
                i = NORM[name]
                if wait:
                    pe.wait_ge(*wait)
                pe.wait_ge(rstd_ready, i + 1)
                for b in range(TB):
                    mm = pe.matmul(spread_at(name)[:, b * P:b * P + P], RS[:, i % 3, b:b + 1].to_broadcast([P, P]), ident[:, :], start=True, stop=True)
                mm.then_inc(spread, 1)

            def mean_square(name):
                sum_square(name)
                spread_rstd(name)

            pe.wait_ge(tables, 4)
            mean_square("mix_pre")
            front("dt", HH, HL, (h_ready, 0))
            layer("xbc", HH, HL)

            def dt_columns():
                pe.wait_ge(acs_ready, 1)
                pe.wait_ge(tables, ALL_TABLES)
                for b in range(TB):
                    for n, src in enumerate((ACS, DT)):
                        mm = pe.matmul(N5[:, (2 * b + n) * 16:(2 * b + n) * 16 + 16], src[:, b * P:b * P + P],
                                       ident[0:16, 0:16], start=True, stop=True)
                mm.then_inc(colt, 1)

            def cb():
                pe.wait_ge(act_in, XBC_TILES)
                for g in range(2):
                    b, bt, ct = (N6, N7)[g], BC[:, g, :], BC[:, 2 + g, :]
                    pe.matmul(b[:, 0:T], bt[:, 0:P], ct, start=True, stop=True)
                    pe.matmul(b[:, T:S3], bt[:, P:T], ct[:, P:T], start=True, stop=True).then_inc(cbt, 1)

            def turn_xs(b):
                pe.wait_ge(cbm_ready, 2)
                if b:
                    pe.wait_ge(xdt_ready, 2 * b)
                for j in range(SSM_TILES):
                    mm = pe.transpose((N6, N7)[j // 4][:, (j % 4) * P:(j % 4) * P + P], XS[:, j, b * P:b * P + P], ident[:, :])
                    if j % 4 == 3:
                        mm.then_inc(xst, 1)

            def lru_gates(j):
                if j == 0:
                    pe.wait_ge(blk_in, 64)
                    pe.wait_ge(conv, XBC_TILES + KD)
                else:
                    pe.wait_ge(rg_ready, 2 * j)
                b = N5
                pe.matmul(b[:, 0:T], BLKR[:, j, :], XC[:, j, :], start=True, stop=True)
                pe.matmul(b[:, T:2 * T], BLKI[:, j, :], XC[:, j, :], start=True, stop=True).then_inc(rg_mm, 1)

            def head_bcast(h):
                if h >= 1:
                    pe.wait_ge(seg_ready, h)
                pe.matmul(N4[:, 0:T], ident[0:16, h:h + 1].to_broadcast([16, P]), ACS[:, :],
                          start=True, stop=True).then_inc(bcast, 1)

            def head_y(h):
                if h == 0:
                    pe.wait_ge(xdt_ready, 4)
                pe.wait_ge(m_ready, h + 1)
                if h >= 4 and h % 2 == 0:
                    pe.wait_ge(ys_ready, h // 2 - 1)
                b, rows = (N6, N7)[h // 2 % 2], slice(64 * (h % 2), 64 * (h % 2) + 64)
                pe.matmul(b[rows, 0:T], XDT[:, 0, h, :], M[:, h % 2, 0:T], start=True, stop=False)
                pe.matmul(b[rows, P:T], XDT[:, 1, h, :], M[:, h % 2, T:S3], start=False, stop=True).then_inc(y_mm, 1)

            def heads(n):
                if n < SSM_HEADS:
                    head_bcast(n)
                if n >= 1:
                    head_y(n - 1)

            layer("ly", HH, HL, {1: cb, 5: dt_columns, 6: lambda: turn_xs(0), 7: lambda: turn_xs(1)})
            layer("lx", HH, HL, {n: (lambda n=n: heads(n)) for n in range(8)})
            layer("z", HH, HL, {n: (lambda n=n: heads(n + 8)) for n in range(8)})

            def after_g0(n):
                if n == 0:
                    heads(SSM_HEADS)
                if n in (2, 3):
                    sum_square(("ssm0", "ssm1")[n - 2])
                if n == 4:
                    spread_rstd("ssm0")
                    spread_rstd("ssm1")
                lru_gates(n)

            layer("g0", HH, HL, {n: (lambda n=n: after_g0(n)) for n in range(8)})
            front("proj_ssm", FH, FL, (ya_ready, 0), 2)
            layer("proj_ssm", FH, FL)
            layer("g1", HH, HL)
            front("proj_lru", FH[:, 8:16, :], FL[:, 8:16, :], (yb_ready, 0), 2)
            layer("proj_lru", FH[:, 8:16, :], FL[:, 8:16, :])
            front("mix_out", FH, FL, (mg_ready, 0), 2)
            layer("mix_out", FH, FL)
            mean_square("mix_post")
            mean_square("ffn_pre")
            front("ffn_up_a", HH, HL, (h_ready, 8))
            loop_layer("ffn_up_a", HH, HL, 8)
            loop_layer("ffn_down_a", FH, FL, 4, (f_ready, 0))
            loop_layer("ffn_up_b", HH, HL, 8)
            front("ffn_down_b", FH, FL, (f_ready, F_TILES), 2)
            loop_layer("ffn_down_b", FH, FL, 8)
            mean_square("ffn_post")

            mean_square("mix2_0")
            front("fa", HH, HL, (h_ready, 16))
            layer("q_fox", HH, HL)
            layer("k_fox", HH, HL)
            value_layer("v_fox", HH, HL)

            def score_head(kind, n, h, q, k):
                if n >= 2:
                    pe.wait_ge(s_max, 2 * (n - 1))
                b = (N4, N5)[n % 2]
                rows = slice(64 * (h % 2), 64 * (h % 2) + 64)
                for qb, lo, cols in ((0, 0, P), (1, P, T)):
                    if kind == "mla":
                        mm = pe.matmul(b[:, lo:lo + cols], q[:, h, qb * P:qb * P + P], k[:, h, 0:cols], start=True, stop=True)
                        continue
                    mm = pe.matmul(b[:, lo:lo + cols], q[rows, h // 2, qb * P:qb * P + P], k[rows, h // 2, 0:cols],
                                   start=True, stop=(kind != "fox"))
                    if kind == "fox":
                        mm = pe.matmul(b[:, lo:lo + cols], AQ[rows, h // 2, qb * P:qb * P + P], BK[rows, h // 2, 0:cols],
                                       start=False, stop=True)
                mm.then_inc(s_mm, 1)

            def turn_head(n):
                pe.wait_ge(p_norm, n + 1)
                if n >= 1:
                    pe.wait_ge(pt_ready, n)
                for c in range(3):
                    mm = pe.transpose(N6[:, c * P:c * P + P], M[:, n % 2, c * P:c * P + P], ident[:, :])
                mm.then_inc(pt_mm, 1)

            def weigh_head(n, h, v, w, w_ready, count):
                pe.wait_ge(w_ready, count)
                pair = n // 2
                if h % 2 == 0 and pair >= 1:
                    pe.wait_ge(o_ready, pair)
                rows, c = slice(64 * (h % 2), 64 * (h % 2) + 64), slice(64 * h, 64 * h + 64)
                pe.matmul(N7[rows, 0:T], v[:, 0, c], w[:, 0:T], start=True, stop=False)
                pe.matmul(N7[rows, P:T], v[:, 1, c], w[:, T:S3], start=False, stop=True).then_inc(pv_mm, 1)

            def softmax_step(i, kind, n0, o0, q, k, v, tile=None):
                if i == 0:
                    score_head(kind, n0, 0, q, k)
                if i + 1 < HEADS:
                    score_head(kind, n0 + i + 1, i + 1, q, k)
                if tile:
                    tile(i)
                if 1 <= i <= HEADS:
                    turn_head(n0 + i - 1)
                if 2 <= i <= HEADS + 1:
                    h = i - 2
                    weigh_head(o0 + h, h, v, PT[:, (n0 + h) % 2, :], pt_ready, n0 + h + 1)

            def softmax_over(name, ready, kind, n0, o0, q, k, v):
                def tile(i):
                    if i < COUNT[name]:
                        dense_tile(FIRST[name] + i, FH, FL, ready=ready if i == 0 else None)

                for i in range(HEADS + 2):
                    softmax_step(i, kind, n0, o0, q, k, v, tile)

            def fox(i):
                if i == 0:
                    pe.wait_ge(evac, taken("v_fox", 1))
                    pe.wait_ge(dtile_in, 32 * HEADS)
                softmax_step(i, "fox", 0, 0, Q, K, V)

            layer("q_chk", HH, HL, {n: (lambda n=n: fox(n)) for n in range(4)})
            layer("k_chk", HH, HL, {n: (lambda n=n: fox(n + 4)) for n in range(4)})
            value_layer("v_chk", HH, HL, hooks={n: (lambda n=n: fox(n + 8)) for n in range(2)})
            pe.wait_ge(evac, taken("v_chk", 1))
            softmax_over("ab_out_a", (o_ready, 0), "chk", 8, 8, Q2, K2, V2)
            front("ab_out_b", FH[:, 4:8, :], FL[:, 4:8, :], (o_ready, 4), 4)
            layer("ab_out_b", FH[:, 4:8, :], FL[:, 4:8, :])
            mean_square("mlp2_0")

            def mlp(which, h0, f0):
                front(f"mlp_up{which}a", HH, HL, (h_ready, h0))
                loop_layer(f"mlp_up{which}a", HH, HL, 4)
                loop_layer(f"mlp_down{which}a", FH, FL, 4, (f_ready, f0))
                loop_layer(f"mlp_up{which}b", HH, HL, 4)
                loop_layer(f"mlp_down{which}b", FH, FL, 4, (f_ready, f0 + F_TILES))

            mlp(0, 24, FFN_PAIRS)
            mean_square("mix2_1")
            front("c_q", HH, HL, (h_ready, 32))
            layer("c_kv", HH, HL)
            layer("q_sb", HH, HL, {0: lambda: sum_square("q_norm"), 1: lambda: spread_rstd("q_norm"), 2: lambda: sum_square("kv_norm"),
                                   3: lambda: spread_rstd("kv_norm", (h32, 40 + Q_KT))})
            layer("k_sb", HH, HL)
            value_layer("v_sb", HH, HL)

            def sb_scores(h):
                if h >= 3:
                    pe.wait_ge(arg_ready, h - 2)
                b = Z[h % 3]
                rows = slice(64 * (h % 2), 64 * (h % 2) + 64)
                pe.matmul(b[:, 0:T], K2[rows, h // 2, 0:P], Q2[rows, h // 2, :], start=True, stop=False, skip_group_check=True)
                pe.matmul(b[:, T:S3], K2[rows, h // 2, P:T], Q2[rows, h // 2, P:T], start=False, stop=False,
                          skip_group_check=True).then_inc(s_mm, 1)

            def sb_suffix(h):
                pe.wait_ge(lm_ready, 2 * (h + 1))
                b, lm = Z[h % 3], S[:, h % 2, :]
                pe.matmul(b[:, 0:T], neg_tri[:, :], lm[:, 0:T], start=False, stop=False, skip_group_check=True)
                pe.matmul(b[:, P:T], neg_one[:, :], lm[:, T:S3], start=False, stop=False, skip_group_check=True)
                pe.matmul(b[:, T:S3], neg_tri[:, :], lm[:, T:S3], start=False, stop=True,
                          skip_group_check=True).then_inc(arg_mm, 1)

            def stick(i):
                if i == 0:
                    pe.wait_ge(evac, taken("v_sb", 1))
                    sb_scores(0)
                if i + 1 < HEADS:
                    sb_scores(i + 1)
                if 1 <= i <= HEADS:
                    sb_suffix(i - 1)
                if 2 <= i <= HEADS + 1:
                    h = i - 2
                    weigh_head(16 + h, h, V2, M[:, h % 2, :], a_exp, h + 1)

            layer("k_rope", HH, HL, {n: (lambda n=n: stick(n)) for n in range(2)})
            layer("q_mla", FH[:, KD:, :], FL[:, KD:, :], {n: (lambda n=n: stick(n + 2)) for n in range(HEADS)}, ready=(h_ready, 40))
            layer("k_mla", FH[:, KD + Q_KT:, :], FL[:, KD + Q_KT:, :], ready=(h_ready, 40 + Q_KT))
            value_layer("v_mla", FH[:, KD + Q_KT:, :], FL[:, KD + Q_KT:, :], second=N4)
            pe.wait_ge(evac, taken("v_mla", 1))
            pe.wait_ge(dve_take, taken("q_mla", HEADS - 1))
            pe.wait_ge(kcopy, 1)
            softmax_over("cd_out_a", (o_ready, 8), "mla", 16, 24, Q, K, V)
            front("cd_out_b", FH[:, 4:8, :], FL[:, 4:8, :], (o_ready, 12), 4)
            layer("cd_out_b", FH[:, 4:8, :], FL[:, 4:8, :])
            mean_square("mlp2_1")
            mlp(1, 45, FFN_PAIRS + MLP_TILES)
            mean_square("final")

        @block.scalar
        def _(act):
            rounded = [0]

            def round_slab(i, turn=0, per=0):
                act.wait_ge(slab_in[i % R], turn * (16 * per // R) + 16 * (i // R + 1))
                if i >= R:
                    act.wait_ge(unit, turn * per + LAST_UNIT[i - R])
                act.activation(WH[:, i % R, :], RAW[:, i % R, :], ACT.Copy).then_inc(hi_ready, 1)

            def ahead(name, n):
                while rounded[0] < min(slab_of(name, n) + R, SLABS):
                    round_slab(rounded[0])
                    rounded[0] += 1

            def square(name, k, src):
                i = NORM[name]
                if SQUARES[i] + k >= SQ_SLOTS:
                    act.wait_ge(*square_used(SQUARES[i] + k - SQ_SLOTS))
                act.activation(SQ[:, (SQUARES[i] + k) % SQ_SLOTS, :], src, ACT.Square).then_inc(squared, 1)

            def std(name):
                i = NORM[name]
                act.wait_ge(ms_ready, i + 1)
                act.activation(RS[:, i % 3, :], N4[:, sum_at(name):sum_at(name) + TB], ACT.Sqrt, bias=EPSC[:, :], scale=NORMS[i][2]).then_inc(std_ready, 1)

            def residual_square(name, k, count):
                act.wait_ge(x_ready, count)
                square(name, k, X[:, k, :])

            def round_next():
                round_slab(rounded[0])
                rounded[0] += 1

            def round_hidden(base, last_reader=None, n=KD, src=HT, between=(), dst=HH):
                if last_reader:
                    act.wait_ge(unit, unit_of(last_reader, COUNT[last_reader] - 1))
                for k in range(n):
                    act.wait_ge(h32, base + k + 1)
                    act.activation(dst[:, k, :], src[:, k % src.shape[1], :], ACT.Copy).then_inc(h_hi, 1)
                    if k in between:
                        round_next()

            def softplus_exp(i, out, in_):
                act.wait_ge(sp_in, i + 1)
                act.activation(out, in_, ACT.Exp).then_inc(sp_exp, 1)

            def tile(name, n):
                act.wait_ge(unit, unit_of(name, n))
                return tile_bank(name, n)[:, 0:T]

            act.preload_act_table_set("sqrt_and_others")
            for k in range(KD):
                if k % 4 == 0:
                    act.wait_ge(x_in[k // 4], 16)
                square("mix_pre", k, X[:, k, :])
            act.wait_ge(tables, 2)
            round_slab(0)
            std("mix_pre")
            round_slab(1)
            rounded[0] = 2
            round_hidden(0, between=(2, 5))
            act.wait_ge(consts_in, 16)
            act.preload_act_table_set("silu_and_others")

            def tap(name, n, out):
                act.activation(out, tile(name, n), ACT.Identity, bias=col(name + "_b", n),
                               scale=col(name + "_w", 4 * n + 3)).then_inc(conv0, 1)

            def silu(n):
                act.wait_ge(conv, n + 1)
                act.activation(A[:, n, :], A[:, n, :], ACT.Silu).then_inc(act_in, 1)

            for n in range(XBC_TILES):
                ahead("xbc", n)
                tap("xbc", n, A[:, n, :])
                if n >= 1:
                    silu(n - 1)
            silu(XBC_TILES - 1)
            act.activation(NEGA[:, :], col("a_log", rows=slice(0, 16)), ACT.Exp).then_inc(nega, 1)
            softplus_exp(0, SP[0:16, 2, :], SP[0:16, 1, :])
            for n in range(KD):
                ahead("ly", n)
                act.activation(GATE[:, n, :], tile("ly", n), ACT.Gelu_apprx_tanh).then_inc(evac, 1)
            act.preload_act_table_set("exp_and_others")

            def decay(h):
                act.wait_ge(seg_ready, h + 1)
                act.activation(S[:, h % 2, :], S[:, h % 2, :], ACT.Exp).then_inc(decay_ready, 1)

            for n in range(KD):
                ahead("lx", n)
                tap("lx", n, XC[:, n, :])
                decay(n)
            for n in range(KD):
                ahead("z", n)
                act.activation(ZS[:, n, :], tile("z", n), ACT.Tanh, scale=0.5).then_inc(zs_ready, 1)
                decay(8 + n)
            act.wait_ge(half_bias, 3)

            def round_ya(k):
                act.wait_ge(yn_ready, k + 1)
                act.activation(FH[:, k, :], YS[:, k, :], ACT.Copy).then_inc(ya_hi, 1)

            for n in range(KD):
                ahead("g0", n)
                if n == 4:
                    act.wait_ge(ms_ready, NORM["ssm1"] + 1)
                    std("ssm0")
                    std("ssm1")
                act.activation(G[:, n, :], tile("g0", n), ACT.Tanh, bias=HB[:, n:n + 1], scale=0.5).then_inc(evac, 1)
                if n == 0:
                    act.wait_ge(ys_ready, SSM_TILES)
                if n == 1:
                    softplus_exp(1, LSP[:, 2, :], LSP[:, 1, :])
                if n in (1, 2):
                    for k in range(4):
                        act.wait_ge(yg_ready, 4 * (n - 1) + k + 1)
                        square(("ssm0", "ssm1")[n - 1], k, YS[:, 4 * (n - 1) + k, :])
                if n == 6:
                    for k in range(KD):
                        round_ya(k)
                act.wait_ge(rg_mm, n + 1)
                act.activation(TH[:, n, :], N5[:, 0:T], ACT.Tanh, bias=HB[:, 16 + n:17 + n], scale=0.5).then_inc(rg_ready, 1)
                act.activation(IG[:, n, :], N5[:, T:2 * T], ACT.Tanh, bias=HB[:, 24 + n:25 + n], scale=0.5).then_inc(rg_ready, 1)
            act.wait_ge(lam_ready, 2)
            for n in range(KD):
                ahead("proj_ssm", n)
                act.wait_ge(rg_ready, 2 * n + 1)
                act.activation(AG[:, n, :], TH[:, n, :], ACT.Exp, bias=LSP[:, 4, n:n + 1], scale=LSP[:, 4, n:n + 1]).then_inc(ag_ready, 1)
                act.activation(TH[:, n, :], TH[:, n, :], ACT.Tanh, bias=LSP[:, 3, n:n + 1], scale=LSP[:, 3, n:n + 1]).then_inc(th_ready, 1)

            def round_yb(k):
                act.wait_ge(yb32, k + 1)
                act.activation(FH[:, KD + k, :], GATE[:, k, :], ACT.Copy).then_inc(yb_hi, 1)

            for n in range(KD):
                ahead("g1", n)
                act.wait_ge(dve_take, taken("proj_ssm", n))
                act.activation(G[:, n, :], tile("g1", n), ACT.Tanh, bias=HB[:, 8 + n:9 + n], scale=0.5).then_inc(evac, 1)
                if n == 0:
                    for j in range(KD):
                        act.wait_ge(m2_ready, j + 1)
                        act.activation(TH[:, j, :], TH[:, j, :], ACT.Sqrt, scale=0.25).then_inc(mult_ready, 1)
                if n >= 2:
                    round_yb(n - 2)
            round_yb(KD - 2)
            round_yb(KD - 1)

            def round_merged(k):
                act.wait_ge(mg32, k + 1)
                act.activation(FH[:, k, :], MG[:, k, :], ACT.Copy, scale=0.5).then_inc(mg_hi, 1)

            for n in range(KD):
                ahead("proj_lru", n)
                act.wait_ge(unit, unit_of("proj_lru", n))
                round_merged(n)
            act.preload_act_table_set("sqrt_and_others")
            for n in range(KD):
                ahead("mix_out", n)
                p = tile("mix_out", n)
                square("mix_post", n, p)
                act.activation(Y[:, n, :], p, ACT.Copy).then_inc(y_evac, 1)
            ahead("ffn_up_a", 0)
            std("mix_post")
            for k in range(KD):
                residual_square("ffn_pre", k, k + 1)
            std("ffn_pre")
            act.preload_act_table_set("gelu_apprx_tanh_and_others")
            round_hidden(8, "g1")

            c0 = taken("ffn_up_a")

            def ffn_turn(name, p0, it, first_turn, slab0):
                u0, turn = unit_of(name, 0), (0 if first_turn else it)
                for j in range(2):
                    p = it * 2 + (p0 + j)
                    for half in range(2):
                        at = p * 2 + half
                        round_slab(slab0 + 2 * j + half, turn, R)
                        act.wait_ge(unit, it * 4 + (u0 + 2 * j + half))
                        if half == 0 and not (first_turn and p0 == 0):
                            act.wait_ge(f_ready, p + (-1))
                        b = tile_bank(name, 2 * j + half)
                        act.activation(CV[:, 2 * j + half, :], b[:, 0:T], ACT.Identity,
                                       bias=C[:, dyn(at + COL["ffn_b"])], scale=C[:, dyn(at * 3 + (COL["ffn_w"] + 2))]).then_inc(conv0, 1)
                        if half == 0 and not (first_turn and j == 0):
                            act.wait_ge(f32_ready, p * 1)
                            act.activation(FH[:, dyn(it * 2 + (j - 1)), :], CV[:, 2 * ((j + 1) % 2), :], ACT.Copy).then_inc(f_hi, 1)
                    act.wait_ge(conv, p * 2 + c0)
                    act.activation(CV[:, 2 * j, :], CV[:, 2 * j, :], ACT.Gelu_apprx_tanh).then_inc(gelu_done, 1)

            def ffn_up(name, p0, following):
                slab0, turns = rounded[0], COUNT[name] // 4
                ffn_turn(name, p0, 0, True, slab0)
                with act.Fori(1, turns) as it:
                    ffn_turn(name, p0, it, False, slab0)
                rounded[0] += 4 * turns
                ahead(*following)
                act.wait_ge(f32_ready, p0 + 2 * turns)
                act.activation(FH[:, 2 * turns - 1, :], CV[:, 2, :], ACT.Copy).then_inc(f_hi, 1)

            ffn_up("ffn_up_a", 0, ("ffn_down_a", 0))
            for n in range(KD):
                ahead("ffn_down_a", n)
                act.activation(Y[:, n, :], tile("ffn_down_a", n), ACT.Copy).then_inc(evac, 1)
            ffn_up("ffn_up_b", F_TILES, ("ffn_down_b", 0))
            act.preload_act_table_set("sqrt_and_others")
            for n in range(KD):
                ahead("ffn_down_b", n)
                act.wait_ge(y_sum, n + 1)
                square("ffn_post", n, Y[:, n, :])
            ahead("fa", 0)
            std("ffn_post")
            for k in range(KD):
                residual_square("mix2_0", k, KD + k + 1)
            std("mix2_0")
            act.preload_act_table_set("exp_and_others")
            round_hidden(16, "ffn_up_b")

            def evac_tile(name, n, out, scale=1.0, rows=slice(0, P)):
                ahead(name, n)
                act.activation(out[rows, n, :], tile(name, n)[rows, :], ACT.Copy, scale=scale).then_inc(evac, 1)

            def evac_values(name, v, second=None):
                act.wait_ge(unit, unit_of(name, COUNT[name] - 1))
                for half in range(TB):
                    b = second if second and half else bank[(FIRST[name] + value_at(name) + half) % BANKS]
                    act.activation(v[:, half, :], b[:, :], ACT.Copy).then_inc(evac, 1)

            def out_pair(pair):
                act.wait_ge(pv_mm, 2 * pair + 2)
                act.activation(FH[:, pair % 8, :], N7[:, 0:T], ACT.Copy).then_inc(o_hi, 1)

            def softmax_step(i, n0, o0, scale):
                if i >= 4 and i % 2 == 0:
                    out_pair((o0 + i - 4) // 2)
                if i < HEADS:
                    n = n0 + i
                    act.wait_ge(s_bias, n + 1)
                    for qb, (lo, cols) in enumerate(((0, P), (P, T))):
                        act.activation(S[:, n % 2, lo:lo + cols], S[:, n % 2, lo:lo + cols], ACT.Exp,
                                       bias=ST[:, n % 2, 2 + qb:3 + qb], scale=scale,
                                       accum_out=ST[:, n % 2, 4 + qb:5 + qb]).then_inc(p_exp, 1)
                if 1 <= i <= HEADS:
                    n = n0 + i - 1
                    act.wait_ge(pt_mm, n + 1)
                    if n >= 2:
                        act.wait_ge(pv_mm, o0 + i - 2)
                    act.activation(PT[:, n % 2, :], N6[:, 0:S3], ACT.Copy).then_inc(pt_ready, 1)

            ahead("q_fox", 0)
            softplus_exp(2, SP[0:HEADS, 2, :], SP[0:HEADS, 1, :])
            for n in range(4):
                evac_tile("q_fox", n, Q, 0.125)
            for n in range(4):
                evac_tile("k_fox", n, K)
            for n in range(4):
                ahead("v_fox", n)
            evac_values("v_fox", V)
            for n in range(4):
                evac_tile("q_chk", n, Q2, 0.125)
                softmax_step(n, 0, 0, 1.0)
            for n in range(4):
                evac_tile("k_chk", n, K2)
                softmax_step(n + 4, 0, 0, 1.0)
            for n in range(4):
                ahead("v_chk", n)
                if n == 3:
                    evac_values("v_chk", V2)
                if n < 3:
                    softmax_step(n + 8, 0, 0, 1.0)

            def softmax_over(name, n0, o0, scale):
                for i in range(HEADS + 3):
                    softmax_step(i, n0, o0, scale)
                    if i < COUNT[name]:
                        ahead(name, i)

            softmax_over("ab_out_a", 8, 8, 1.0)

            def residual_layer(name, norm, following=None):
                if norm:
                    act.preload_act_table_set("sqrt_and_others")
                for n in range(KD):
                    ahead(name, n)
                    if norm:
                        residual_square(norm, n, taken(name, n))
                if following:
                    ahead(following, 0)
                if norm:
                    std(norm)

            residual_layer("ab_out_b", "mlp2_0", "mlp_up0a")
            round_hidden(24, "v_chk")

            def mlp_up(name, f0):
                slab0, u0, e0 = rounded[0], unit_of(name, 0), taken(name)

                def relu(it, j, turn):
                    round_slab(slab0 + j, turn, R)
                    act.wait_ge(unit, it * 4 + (u0 + j))
                    act.wait_ge(f_ready, it * 4 + (f0 + j - 3))
                    act.activation(RT[:, j, :], tile_bank(name, j)[:, 0:T], ACT.Relu).then_inc(evac, 1)

                def round_square(it, j):
                    act.wait_ge(evac, it * 4 + (e0 + j))
                    act.activation(FH[:, dyn(it * 4 + j), :], RT[:, j % 4, :], ACT.Square).then_inc(f_hi, 1)

                with act.Fori(0, F_TILES // 4) as it:
                    for j in range(4):
                        relu(it, j, it)
                        round_square(it, j)
                rounded[0] += F_TILES

            mlp_up("mlp_up0a", FFN_PAIRS)
            for n in range(KD):
                ahead("mlp_down0a", n)
                if n == 3:
                    act.wait_ge(ang_ready, 2)
                    act.activation(SIN[64:P, :], ANG[64:P, 4, :], ACT.Sin).then_inc(sin_ready, 1)
                    act.activation(COS[64:P, :], ANG[64:P, 5, :], ACT.Sin).then_inc(sin_ready, 1)
            mlp_up("mlp_up0b", FFN_PAIRS + F_TILES)
            residual_layer("mlp_down0b", "mix2_1", "c_q")
            round_hidden(32, "mlp_up0b")
            for n in range(Q_KT):
                evac_tile("c_q", n, LAT)
                act.wait_ge(evac, taken("c_q", n))
                square("q_norm", n, LAT[:, n, :])
            for n in range(KV_KT):
                evac_tile("c_kv", n, LAT[:, Q_KT:, :])
                act.wait_ge(evac, taken("c_kv", n))
                square("kv_norm", n, LAT[:, Q_KT + n, :])
            for n in range(4):
                if n in (1, 3):
                    std(("q_norm", "kv_norm")[n // 2])
                evac_tile("q_sb", n, Q2, 0.125)
            for n in range(4):
                evac_tile("k_sb", n, K2)
                if n == 1:
                    round_hidden(40, n=Q_KT + KV_KT, src=LAT, dst=FH[:, KD:, :])
            for n in range(4):
                ahead("v_sb", n)
            evac_values("v_sb", V2)
            act.preload_act_table_set("natural_log_exp_and_others")

            def stick_step(i):
                if i >= 4 and i % 2 == 0:
                    out_pair(8 + (i - 4) // 2)
                if i < HEADS:
                    s = S[:, i % 2, :]
                    act.wait_ge(s_mm, 16 + i + 1)
                    if i >= 2:
                        act.wait_ge(arg_mm, i - 1)
                    act.activation(s, Z[i % 3][:, 0:S3], ACT.Abs).then_inc(z_abs, 1)
                    act.wait_ge(z_abs, i + 1)
                    act.activation(s, s, ACT.Exp, scale=-1.0).then_inc(z_exp, 1)
                    act.wait_ge(z_exp, i + 1)
                    act.activation(s, s, ACT.Ln, bias=1.0).then_inc(z_ln, 1)
                if 1 <= i <= HEADS:
                    act.wait_ge(arg_ready, i)
                    act.activation(M[:, (i - 1) % 2, :], M[:, (i - 1) % 2, :], ACT.Exp).then_inc(a_exp, 1)

            for n in range(2):
                evac_tile("k_rope", n, KR)
                stick_step(n)
            for n in range(HEADS):
                ahead("q_mla", n)
                stick_step(n + 2)
            stick_step(HEADS + 2)
            for n in range(HEADS):
                evac_tile("k_mla", n, K, rows=slice(0, 64))
            ahead("v_mla", 0)
            evac_values("v_mla", V, N4)
            softmax_over("cd_out_a", 16, 24, (64 + 32) ** -0.5)
            residual_layer("cd_out_b", "mlp2_1", "mlp_up1a")
            round_hidden(45, "v_mla")
            mlp_up("mlp_up1a", FFN_PAIRS + 2 * F_TILES)
            residual_layer("mlp_down1a", None)
            mlp_up("mlp_up1b", FFN_PAIRS + 3 * F_TILES)
            residual_layer("mlp_down1b", "final")

        @block.vector
        def _(dve):
            steps, split = [0], [0]
            stt, tt, ts = dve.scalar_tensor_tensor, dve.tensor_tensor, dve.tensor_scalar

            def link(ins):
                steps[0] += 1
                ins.then_inc(step, 1)
                dve.wait_ge(step, steps[0])

            def less(out, whole, part):
                return tt(out, whole, part.bitcast(fp32), ALU.subtract)

            def split_slab(i, turn=0, per=0):
                if i % R != R - 1:
                    dve.wait_ge(hi_ready, turn * per + (i + 1))
                    less(WL[:, i % R, :], RAW[:, i % R, :], WH[:, i % R, :]).then_inc(lo_ready[i % R], 1)

            def ahead(name, n):
                while split[0] < min(slab_of(name, n) + R - 1, SLABS):
                    split_slab(split[0])
                    split[0] += 1

            def add_square(name, k):
                i = NORM[name]
                if not 1 <= k <= NORMS[i][1] - 2:
                    return
                sq = lambda n: SQ[:, (SQUARES[i] + n) % SQ_SLOTS, :]
                dve.wait_ge(squared, SQUARES[i] + k + 1)
                if k == 1:
                    if i:
                        dve.wait_ge(ms_ready, i)
                    tt(ACC[:, :], sq(0), sq(1), ALU.add).then_inc(added, 1)
                else:
                    dve.wait_ge(added, ADDS[i] + k - 1)
                    tt(ACC[:, :], ACC[:, :], sq(k), ALU.add).then_inc(added, 1)

            def add_squares(name):
                for k in range(NORMS[NORM[name]][1]):
                    add_square(name, k)

            def invert(name):
                i = NORM[name]
                dve.wait_ge(std_ready, i + 1)
                dve.reciprocal(RS[:, i % 3, :], RS[:, i % 3, :]).then_inc(rstd_ready, 1)

            def spread_out(name):
                dve.wait_ge(spread, NORM[name] + 1)
                return spread_at(name)

            def rstd(name):
                invert(name)
                return spread_out(name)

            def low_hidden(k, base, src):
                dve.wait_ge(h_hi, base + k + 1)
                less(HL[:, k, :], src[:, k % src.shape[1], :], HH[:, k, :]).then_inc(h_ready, 1)

            def split_next():
                split_slab(split[0])
                split[0] += 1

            def pre_norm(name, base, c=None, at=0, between=()):
                r = rstd(name)
                for k in range(KD):
                    stt(out=HT[:, k % 4, :], in0=X[:, k, :], scalar=col(c or name, at + k), in1=r, op0=ALU.mult, op1=ALU.mult).then_inc(h32, 1)
                    if k >= 1:
                        low_hidden(k - 1, base, HT)
                    if k in between:
                        split_next()
                low_hidden(KD - 1, base, HT)

            def softplus(part, i, v, src, bias, scale, t, out, s, bank_taken=None):
                e, p, q = t[1], t[0], t[2]
                if part == 0:
                    first = ts(v, src, scale, bias, ALU.mult, ALU.add)
                    if bank_taken:
                        first.then_inc(u_taken, 1)
                        dve.wait_ge(u_taken, bank_taken)
                    else:
                        link(first)
                    stt(out=t[0], in0=v, scalar=-1.0, in1=v, op0=ALU.mult, op1=ALU.min).then_inc(sp_in, 1)
                if part == 1:
                    dve.wait_ge(sp_exp, i + 1)
                    link(ts(q, e, 2.0, None, ALU.add))
                    link(dve.reciprocal(q, q))
                    link(tt(e, e, q, ALU.mult))
                    link(tt(q, e, e, ALU.mult))
                    link(ts(p, q, 1 / 15, None, ALU.mult))
                    link(ts(v, v, 0.0, None, ALU.max))
                if part >= 2:
                    for n in ((13, 11, 9, 7), (5, 3))[part - 2]:
                        link(stt(out=p, in0=p, scalar=1 / n, in1=q, op0=ALU.add, op1=ALU.mult))
                if part == 3:
                    link(stt(out=p, in0=p, scalar=1.0, in1=e, op0=ALU.add, op1=ALU.mult))
                    stt(out=out, in0=p, scalar=2.0, in1=v, op0=ALU.mult, op1=ALU.add).then_inc(s, 1)

            add_squares("mix_pre")
            split_slab(0)
            split[0] = 1
            dve.wait_ge(consts_in, 16)
            dve.wait_ge(x_in[0], 16)
            dve.wait_ge(x_in[1], 16)
            pre_norm("mix_pre", 0, between=(0, 3, 6))

            rows = slice(0, SSM_HEADS)

            def dt_part(part):
                if part == 0:
                    dve.wait_ge(unit, unit_of("dt", 0))
                softplus(part, 0, SP[rows, 0, :], tile_bank("dt", 0)[rows, 0:T], col("dt_bias", rows=rows), 1.0,
                         [SP[rows, 1, :], SP[rows, 2, :], SP[rows, 3, :]], DT[:, :], dt_ready, 1)
                if part == 3:
                    dve.wait_ge(dt_ready, 1)
                    dve.wait_ge(nega, 1)
                    link(ts(SP[rows, 4, :], DT[:, :], NEGA[:, :], -1.0, ALU.mult, ALU.mult))
                    dve.wait_ge(tables, ALL_TABLES)
                    dve.tensor_tensor_scan(ACS[:, :], ones[rows, :], SP[rows, 4, :], 0.0, ALU.mult, ALU.add).then_inc(acs_ready, 1)

            ahead("xbc", 0)
            dt_part(0)

            started = [0]

            def taps(name, n, out, k=4):
                started[0] += 1
                dve.wait_ge(conv0, started[0])
                p = tile_bank(name, n)
                for back in range(1, k):
                    last = stt(out=out[:, back:T], in0=p[:, 0:T - back], scalar=col(name + "_w", k * n + k - 1 - back),
                               in1=out[:, back:T], op0=ALU.mult, op1=ALU.add)
                    if back < k - 1:
                        link(last)
                last.then_inc(conv, 1)

            for n in range(XBC_TILES):
                ahead("xbc", n)
                taps("xbc", n, A[:, n, :])
                if n == 8:
                    for m, (name, width) in enumerate((("gate_b", 16), ("br", 8), ("bi", 8))):
                        ts(HB[:, (0, 16, 24)[m]:(0, 16, 24)[m] + width], col_n(name, width), 0.5, None, ALU.mult).then_inc(half_bias, 1)

            def lambda_part(part):
                softplus(part, 1, LSP[:, 0, :], col_n("lam", KD), 0.0, -1.0, [LSP[:, 1, :], LSP[:, 2, :], LSP[:, 5, :]],
                         LSP[:, 0, :], lam_ready)
                if part == 3:
                    dve.wait_ge(lam_ready, 1)
                    link(ts(LSP[:, 3, :], LSP[:, 0, :], 4.0, None, ALU.mult))
                    ts(LSP[:, 4, :], LSP[:, 0, :], -4.0, None, ALU.mult).then_inc(lam_ready, 1)

            def turned_xs(b):
                for half in range(2):
                    dve.wait_ge(xst, 2 * b + half + 1)
                    hs = slice(8 * half, 8 * half + 8)
                    tt(XDT[:, b, hs, :], (N6, N7)[half][:, :].rearrange("p (h d) -> p h d", d=64),
                       COLS[:, b, 1, hs].unsqueeze(2).to_broadcast([P, 8, 64]), ALU.mult).then_inc(xdt_ready, 1)

            for n in range(KD):
                ahead("ly", n)
                if n in (0, 2):
                    dt_part(n // 2 + 1)
                if n == 3:
                    dt_part(3)
                if n == 1:
                    dve.wait_ge(cbt, 2)
                    for g in range(2):
                        tt(CBM[:, g, :], (N6, N7)[g][:, 0:S3], keep_incl[:, :], ALU.mult).then_inc(cbm_ready, 1)
                if n == 5:
                    dve.wait_ge(colt, 1)
                    dve.tensor_copy(COLS[:, :, :, :].rearrange("p b n h -> p (b n h)"), N5[:, 0:64]).then_inc(cols_ready, 1)
                    dve.wait_ge(cols_ready, 1)
                if n in (6, 7):
                    turned_xs(n - 6)

            def decay_args(h):
                dve.wait_ge(bcast, h + 1)
                ts(S[:, h % 2, 0:T], N4[:, 0:T], COLS[:, 0, 0, h:h + 1], 0.0, ALU.subtract, ALU.min)
                ts(S[:, h % 2, T:S3], N4[:, P:T], COLS[:, 1, 0, h:h + 1], 0.0, ALU.subtract, ALU.min).then_inc(seg_ready, 1)

            def decay_cb(h):
                dve.wait_ge(decay_ready, h + 1)
                if h >= 2:
                    dve.wait_ge(y_mm, h - 1)
                tt(M[:, h % 2, :], S[:, h % 2, :], CBM[:, h // 8, :], ALU.mult).then_inc(m_ready, 1)

            def skip(j):
                dve.wait_ge(y_mm, 2 * j + 2)
                stt(out=YS[:, j, :], in0=XS[:, j, :], scalar=col("skip", j), in1=(N6, N7)[j % 2][:, 0:T],
                    op0=ALU.mult, op1=ALU.add).then_inc(ys_ready, 1)

            def gate_y(j):
                dve.wait_ge(ys_ready, j + 1)
                dve.wait_ge(dve_take, taken("z", j))
                stt(out=YS[:, j, :], in0=YS[:, j, :], scalar=0.5, in1=ZS[:, j, :], op0=ALU.mult, op1=ALU.mult).then_inc(yg_ready, 1)

            for n in range(KD):
                ahead("lx", n)
                taps("lx", n, XC[:, n, :])
                decay_args(n)
                if n >= 2 and n % 2 == 0:
                    skip(n // 2 - 1)
                decay_cb(n)
            for n in range(KD):
                ahead("z", n)
                dve.wait_ge(zs_ready, n + 1)
                stt(out=ZS[:, n, :], in0=ZS[:, n, :], scalar=1.0, in1=tile_bank("z", n)[:, 0:T], op0=ALU.add, op1=ALU.mult).then_inc(dve_take, 1)
                decay_args(8 + n)
                if n % 2 == 0:
                    skip(3 + n // 2)
                if n < 7:
                    gate_y(n)
                decay_cb(8 + n)

            def recurrence_in(j):
                dve.wait_ge(rg_ready, 2 * j + 2)
                stt(out=IG[:, j, :], in0=IG[:, j, :], scalar=1.0, in1=XC[:, j, :], op0=ALU.add, op1=ALU.mult).then_inc(ix_ready, 1)

            def low_ya(k):
                dve.wait_ge(ya_hi, k + 1)
                less(FL[:, k, :], YS[:, k, :], FH[:, k, :]).then_inc(ya_ready, 1)

            for n in range(KD):
                ahead("g0", n)
                if n == 0:
                    skip(7)
                    gate_y(7)
                if n <= 3:
                    lambda_part(n)
                if n in (1, 3):
                    add_squares(("ssm0", "ssm1")[n // 2])
                if n == 4:
                    invert("ssm0")
                    invert("ssm1")
                if n == 5:
                    spread_out("ssm1")
                    for k in range(KD):
                        r = spread_at(("ssm0", "ssm1")[k // 4])
                        stt(out=YS[:, k, :], in0=YS[:, k, :], scalar=col("ssm_norm", k), in1=r, op0=ALU.mult, op1=ALU.mult).then_inc(yn_ready, 1)
                if n in (6, 7):
                    for k in range(4):
                        low_ya(4 * (n - 6) + k)
                if n >= 1:
                    recurrence_in(n - 1)
            recurrence_in(KD - 1)
            for n in range(KD):
                ahead("proj_ssm", n)
                dve.wait_ge(ag_ready, n + 1)
                link(tt(HT[:, n % 4, :], AG[:, n, :], AG[:, n, :], ALU.mult))
                dve.wait_ge(th_ready, n + 1)
                stt(out=TH[:, n, :], in0=HT[:, n % 4, :], scalar=1.0, in1=TH[:, n, :], op0=ALU.add, op1=ALU.mult).then_inc(m2_ready, 1)
                dve.wait_ge(unit, unit_of("proj_ssm", n))
                dve.wait_ge(evac, taken("g0", n))
                stt(out=MG[:, n, :], in0=G[:, n, :], scalar=1.0, in1=tile_bank("proj_ssm", n)[:, 0:T], op0=ALU.add, op1=ALU.mult).then_inc(dve_take, 1)

            def low_yb(k):
                dve.wait_ge(yb_hi, k + 1)
                less(FL[:, KD + k, :], GATE[:, k, :], FH[:, KD + k, :]).then_inc(yb_ready, 1)

            def recurrence(j):
                dve.wait_ge(bx_ready, j + 1)
                dve.tensor_tensor_scan(XC[:, j, :], AG[:, j, :], IG[:, j, :], 0.0, ALU.mult, ALU.add).then_inc(scanned, 1)

            for n in range(KD):
                ahead("g1", n)
                if n >= 1:
                    recurrence(n - 1)
                if n >= 3:
                    low_yb(n - 3)
            recurrence(KD - 1)
            for k in range(KD - 3, KD):
                low_yb(k)

            def low_merged(k):
                dve.wait_ge(mg_hi, k + 1)
                stt(out=FL[:, k, :], in0=MG[:, k, :], scalar=0.5, in1=FH[:, k, :].bitcast(fp32), op0=ALU.mult, op1=ALU.subtract).then_inc(mg_ready, 1)

            for n in range(KD):
                ahead("proj_lru", n)
                dve.wait_ge(unit, unit_of("proj_lru", n))
                dve.wait_ge(evac, taken("g1", n))
                stt(out=HT[:, n % 4, :], in0=G[:, n, :], scalar=1.0, in1=tile_bank("proj_lru", n)[:, 0:T], op0=ALU.add, op1=ALU.mult).then_inc(dve_take, 1)
                if n >= 1:
                    low_merged(n - 1)
            low_merged(KD - 1)

            def post_norm(name):
                r = rstd(name)
                for k in range(KD):
                    stt(out=Y[:, k, :], in0=Y[:, k, :], scalar=col(name, k), in1=r, op0=ALU.mult, op1=ALU.mult).then_inc(y_normed, 1)

            for n in range(KD):
                ahead("mix_out", n)
                add_square("mix_post", n)
            dve.wait_ge(y_evac, KD)
            ahead("ffn_up_a", 0)
            post_norm("mix_post")
            add_squares("ffn_pre")
            pre_norm("ffn_pre", 8)
            ahead("ffn_up_a", 0)

            first_start, first_conv = started[0], taken("ffn_up_a") - 1

            def low_inner(k, j, count):
                dve.wait_ge(f_hi, count)
                less(FL[:, dyn(k), :], CV[:, 2 * j, :], FH[:, dyn(k), :]).then_inc(f_ready, 1)

            def ffn_turn(name, p0, it, first_turn, slab0):
                turn = 0 if first_turn else it
                for j in range(2):
                    p = it * 2 + (p0 + j)
                    for half in range(2):
                        split_slab(slab0 + 2 * j + half, turn, R)
                        dve.wait_ge(conv0, p * 2 + (first_start + 1 + half))
                        b, out = tile_bank(name, 2 * j + half), CV[:, 2 * j + half, :]
                        for back in (1, 2):
                            last = stt(out=out[:, back:T], in0=b[:, 0:T - back], scalar=C[:, dyn((p * 2 + half) * 3 + (COL["ffn_w"] + 2 - back))],
                                       in1=out[:, back:T], op0=ALU.mult, op1=ALU.add)
                            if back == 1:
                                last.then_inc(tap_done, 1)
                                dve.wait_ge(tap_done, p * 2 + (half + 1))
                        last.then_inc(conv, 1)
                        if half == 0 and not (first_turn and j == 0):
                            low_inner(it * 2 + (j - 1), (j + 1) % 2, p * 1)
                    dve.wait_ge(gelu_done, p * 1 + 1)
                    dve.wait_ge(conv, p * 2 + (first_conv + 2))
                    tt(CV[:, 2 * j, :], CV[:, 2 * j, :], CV[:, 2 * j + 1, :], ALU.mult).then_inc(f32_ready, 1)

            def ffn_up(name, p0, following):
                slab0, turns = split[0], COUNT[name] // 4
                ffn_turn(name, p0, 0, True, slab0)
                with dve.Fori(1, turns) as it:
                    ffn_turn(name, p0, it, False, slab0)
                split[0] += 4 * turns
                ahead(*following)
                low_inner(2 * turns - 1, 1, p0 + 2 * turns)

            ffn_up("ffn_up_a", 0, ("ffn_down_a", 0))
            for n in range(KD):
                ahead("ffn_down_a", n)
            ffn_up("ffn_up_b", F_TILES, ("ffn_down_b", 0))
            for n in range(KD):
                ahead("ffn_down_b", n)
                dve.wait_ge(evac, taken("ffn_down_a", n))
                dve.wait_ge(unit, unit_of("ffn_down_b", n))
                tt(Y[:, n, :], Y[:, n, :], tile_bank("ffn_down_b", n)[:, 0:T], ALU.add).then_inc(y_sum, 1)
                add_square("ffn_post", n - 1)
            ahead("fa", 0)
            post_norm("ffn_post")
            add_squares("mix2_0")
            pre_norm("mix2_0", 16, "mix2")

            rows = slice(0, HEADS)
            ts(NB[:, :], col("b_forget", rows=rows), -1.0, None, ALU.mult).then_inc(cum_ready, 1)

            def forget_part(part):
                if part == 0:
                    dve.wait_ge(unit, unit_of("fa", 0))
                    dve.wait_ge(cum_ready, 1)
                softplus(part, 2, SP[rows, 0, :], tile_bank("fa", 0)[rows, 0:T], NB[:, :], -1.0,
                         [SP[rows, 1, :], SP[rows, 2, :], SP[rows, 3, :]], SP[rows, 4, :], cum_ready, 2)
                if part == 3:
                    dve.wait_ge(cum_ready, 2)
                    dve.tensor_tensor_scan(NCUM, ones[rows, :], SP[rows, 4, :], 0.0, ALU.mult, ALU.add).then_inc(cum_ready, 1)
                    dve.wait_ge(cum_ready, 3)
                    ts(CUM, NCUM, -1.0, None, ALU.mult).then_inc(cum_ready, 1)

            ahead("q_fox", 0)
            forget_part(0)

            def out_pair(pair):
                dve.wait_ge(o_hi, pair + 1)
                less(FL[:, pair % 8, :], N7[:, 0:T], FH[:, pair % 8, :]).then_inc(o_ready, 1)

            def scores_max(kind, i, n0, scale):
                n = n0 + i
                dve.wait_ge(s_mm, (n if kind != "mla" else n + HEADS) + 1)
                if kind == "chk":
                    dve.wait_ge(bias_ready, i + 1)
                if n >= 2:
                    dve.wait_ge(p_norm, n - 1)
                add = {"fox": neg_causal[:, :], "mla": neg_chunk[:, :], "chk": BIAS[:, i, :]}[kind]
                b = (N4, N5)[n % 2]
                for qb, (lo, cols) in enumerate(((0, P), (P, T))):
                    dve.tensor_tensor_reduce(out=S[:, n % 2, lo:lo + cols], in0=b[:, lo:lo + cols], in1=add[:, lo:lo + cols],
                                             scale=1.0, scalar=-3.0e38, op0=ALU.add, op1=ALU.max,
                                             accum_out=ST[:, n % 2, qb:qb + 1]).then_inc(s_max, 1)
                dve.wait_ge(s_max, 2 * (n + 1))
                ts(ST[:, n % 2, 2:4], ST[:, n % 2, 0:2], -scale, None, ALU.mult).then_inc(s_bias, 1)

            def normalised(n):
                dve.wait_ge(p_exp, 2 * (n + 1))
                if n >= 2:
                    dve.wait_ge(pt_mm, n - 1)
                link(dve.reciprocal(ST[:, n % 2, 6:8], ST[:, n % 2, 4:6]))
                ts(M[:, n % 2, 0:P], S[:, n % 2, 0:P], ST[:, n % 2, 6:7], None, ALU.mult)
                ts(M[:, n % 2, P:S3], S[:, n % 2, P:S3], ST[:, n % 2, 7:8], None, ALU.mult).then_inc(p_norm, 1)

            def softmax_step(kind, i, n0, o0, scale, norm_first):
                if norm_first and 1 <= i <= HEADS:
                    normalised(n0 + i - 1)
                if i < HEADS:
                    scores_max(kind, i, n0, scale)
                if not norm_first and 1 <= i <= HEADS:
                    normalised(n0 + i - 1)
                if i >= 4 and i % 2 == 0:
                    out_pair((o0 + i - 4) // 2)

            for name in ("q_fox", "k_fox", "v_fox"):
                for n in range(4):
                    ahead(name, n)
                    if (name, n) in (("q_fox", 2), ("q_fox", 3), ("k_fox", 0)):
                        forget_part((n + 2) % 4 + 1)
            for m, name in enumerate(("q_chk", "k_chk", "v_chk")):
                for n in range(4):
                    ahead(name, n)
                    if 4 * m + n < HEADS + 3:
                        softmax_step("fox", 4 * m + n, 0, 0, 1.0, True)
            def add_tile(name, n):
                ahead(name, n)
                dve.wait_ge(unit, unit_of(name, n))
                tt(X[:, n, :], X[:, n, :], tile_bank(name, n)[:, 0:T], ALU.add).then_inc(x_ready, 1)

            def softmax_over(name, kind, n0, o0, scale):
                for i in range(HEADS + 3):
                    softmax_step(kind, i, n0, o0, scale, False)
                    if i < COUNT[name]:
                        add_tile(name, i)

            def add_residual(name, norm=None, following=None):
                for n in range(COUNT[name]):
                    if norm:
                        dve.wait_ge(x_ready, taken(name, n) - KD)
                    if n == COUNT[name] - 1 and following:
                        ahead(following, 0)
                    add_tile(name, n)
                    if norm and TILES[FIRST[name]][2] > 4:
                        add_square(norm, n - 1)

            softmax_over("ab_out_a", "chk", 8, 8, 1.0)

            def mlp_up(name, f0):
                slab0 = split[0]
                with dve.Fori(0, F_TILES // 4) as it:
                    for j in range(4):
                        split_slab(slab0 + j, it, R)
                        dve.wait_ge(evac, it * 4 + (taken(name) + j))
                        dve.wait_ge(f_hi, it * 4 + (f0 + j + 1))
                        tt(RT[:, j, :], RT[:, j, :], RT[:, j, :], ALU.mult).then_inc(relu_done, 1)
                        dve.wait_ge(relu_done, it * 4 + (f0 - FFN_PAIRS + j + 1))
                        less(FL[:, dyn(it * 4 + j), :], RT[:, j, :], FH[:, dyn(it * 4 + j), :]).then_inc(f_ready, 1)
                split[0] += F_TILES

            add_residual("ab_out_b", "mlp2_0", "mlp_up0a")
            pre_norm("mlp2_0", 24, "mlp2")
            mlp_up("mlp_up0a", FFN_PAIRS)

            hi = slice(64, P)
            ang = lambda n: ANG[hi, n, :]
            ahead("mlp_down0a", 0)
            dve.wait_ge(pos_in, 16)
            link(dve.tensor_copy(ang(0), POS[hi, :]))
            link(ts(ang(1), ang(0), col("inv_freq", rows=hi), None, ALU.mult))
            link(ts(ang(2), ang(1), 1 / TWO_PI, None, ALU.mult))
            link(ts(ang(3), ang(2), ROUND, None, ALU.add))
            link(ts(ang(2), ang(3), -ROUND, None, ALU.add))
            for n, part in enumerate(TWO_PI_PARTS):
                link(stt(out=ang((3, 1, 3)[n]), in0=ang(2), scalar=-part, in1=ang((1, 3, 1)[n]), op0=ALU.mult, op1=ALU.add))
            link(ts(ang(1), ang(3), TWO_PI / 4, None, ALU.add))
            link(ts(ang(2), ang(1), PI_DOWN, -TWO_PI, ALU.is_gt, ALU.mult))
            link(tt(ang(1), ang(1), ang(2), ALU.add))
            ts(ang(4), ang(3), PI_DOWN, -PI_DOWN, ALU.min, ALU.max).then_inc(ang_ready, 1)
            ts(ang(5), ang(1), PI_DOWN, -PI_DOWN, ALU.min, ALU.max).then_inc(ang_ready, 1)

            add_residual("mlp_down0a")
            mlp_up("mlp_up0b", FFN_PAIRS + F_TILES)
            dve.wait_ge(sin_ready, 2)
            ts(SIN[hi, :], SIN[hi, :], col("rope_sign", rows=hi), None, ALU.mult).then_inc(trig_ready, 1)
            dve.memset(TQ[0:64, :], 1.0).then_inc(trig_ready, 1)
            dve.wait_ge(trig_ready, 2)
            dve.tensor_copy(TQ[64:96, :], COS[64:96, :]).then_inc(trig_ready, 1)
            dve.tensor_copy(TQ[96:P, :], SIN[96:P, :]).then_inc(trig_ready, 1)
            add_residual("mlp_down0b", "mix2_1", "c_q")
            pre_norm("mix2_1", 32, "mix2", KD)
            for n in range(Q_KT):
                ahead("c_q", n)
                add_square("q_norm", n - 1)

            def latent(name, k0, n):
                r = spread_out(name)
                for k in range(k0, k0 + n):
                    stt(out=LAT[:, k, :], in0=LAT[:, k, :], scalar=col(name, k - k0), in1=r, op0=ALU.mult, op1=ALU.mult).then_inc(h32, 1)

            for n in range(KV_KT):
                ahead("c_kv", n)
            for n in range(4):
                ahead("q_sb", n)
                if n == 1:
                    invert("q_norm")
                if n == 2:
                    latent("q_norm", 0, Q_KT)
                if n == 3:
                    invert("kv_norm")
            for name in ("k_sb", "v_sb"):
                for n in range(4):
                    ahead(name, n)
                    if name == "k_sb" and n == 0:
                        latent("kv_norm", Q_KT, KV_KT)
                    if name == "k_sb" and n == 3:
                        for k in range(Q_KT + KV_KT):
                            dve.wait_ge(h_hi, 40 + k + 1)
                            less(FL[:, KD + k, :], LAT[:, k, :], FH[:, KD + k, :]).then_inc(h_ready, 1)

            def stick_step(i):
                if i >= 4 and i % 2 == 0:
                    out_pair(8 + (i - 4) // 2)
                if 1 <= i <= HEADS:
                    h, b = i - 1, Z[(i - 1) % 3]
                    dve.wait_ge(arg_mm, h + 1)
                    if h >= 2:
                        dve.wait_ge(pv_mm, 16 + h - 1)
                    tt(M[:, h % 2, :], b[:, 0:S3], neg_strict[:, :], ALU.add).then_inc(arg_ready, 1)
                if i < HEADS:
                    h, b, s = i, Z[i % 3], S[:, i % 2, :]
                    dve.wait_ge(z_ln, h + 1)
                    stt(out=s, in0=b[:, 0:S3], scalar=0.0, in1=s, op0=ALU.max, op1=ALU.add).then_inc(lm_ready, 1)
                    dve.wait_ge(lm_ready, 2 * h + 1)
                    tt(s, s, keep_strict[:, :], ALU.mult).then_inc(lm_ready, 1)

            for n in range(2):
                ahead("k_rope", n)
                stick_step(n)
            for n in range(HEADS):
                ahead("q_mla", n)
                dve.wait_ge(unit, unit_of("q_mla", n))
                tt(Q[:, n, :], tile_bank("q_mla", n)[:, 0:T], TQ, ALU.mult).then_inc(dve_take, 1)
                stick_step(n + 2)
            stick_step(HEADS + 2)
            dve.wait_ge(evac, taken("k_rope", 1))
            dve.wait_ge(trig_ready, 4)
            link(tt(KF[hi, :], KR[hi, 0, :], COS[hi, :], ALU.mult))
            link(tt(KR[hi, 1, :], KR[hi, 1, :], SIN[hi, :], ALU.mult))
            link(tt(KF[hi, :], KF[hi, :], KR[hi, 1, :], ALU.add))
            dve.tensor_copy(K[hi, :, :], KF[hi, :].unsqueeze(1).to_broadcast([64, HEADS, T])).then_inc(kcopy, 1)
            for name in ("k_mla", "v_mla"):
                for n in range(COUNT[name]):
                    ahead(name, n)
            softmax_over("cd_out_a", "mla", 16, 24, (64 + 32) ** -0.5)
            add_residual("cd_out_b", "mlp2_1", "mlp_up1a")
            pre_norm("mlp2_1", 45, "mlp2", KD)
            mlp_up("mlp_up1a", FFN_PAIRS + 2 * F_TILES)
            add_residual("mlp_down1a")
            mlp_up("mlp_up1b", FFN_PAIRS + 3 * F_TILES)
            add_residual("mlp_down1b", "final")
            r = rstd("final")
            for k in range(KD):
                stt(out=Y[:, k, :], in0=X[:, k, :], scalar=col("final", k), in1=r, op0=ALU.mult, op1=ALU.mult).then_inc(out_ready, 1)


def features(v):
    return np.asarray(v).reshape(-1, P).T


def blocks(w):
    k, n = w.shape
    return w.reshape(k // P, P, n // P, P).transpose(2, 0, 1, 3).reshape(-1, P, P)


def value_blocks(w):
    k, n = w.shape
    return w.reshape(k // P, P, n // P, P).transpose(0, 2, 1, 3).reshape(-1, P, P)


def kernel(**given):
    import concourse.bacc as bacc
    from concourse.bass_utils import run_bass_kernel_spmd

    inp = {k: np.asarray(v) for k, v in given.items()}
    f32 = np.float32
    w_in = inp["w_in"][0]
    at = np.cumsum([0, 1024, 1536, 16, 1024, 1024, 2048])
    z, xbc, dt, ly, lx, g = (w_in[:, a:b] for a, b in zip(at[:-1], at[1:]))
    up = inp["w_ffn_up"][0].reshape(D, 2, FFN_PAIRS, P).transpose(0, 2, 1, 3).reshape(D, -1)
    w_ab, w_cd = inp["w_in_ab_2"][0], inp["w_in_cd_2"][0]
    at = np.cumsum([0, 512, 512, 512, 8, 512, 512, 512])
    qa, ka, va, fa, qb, kb, vb = (w_ab[:, a:b] for a, b in zip(at[:-1], at[1:]))
    at = np.cumsum([0, 512, 512, 512, 384, 256, 32])
    qc, kc, vc, cq, ckv, kr = (w_cd[:, a:b] for a, b in zip(at[:-1], at[1:]))
    swap = lambda w: np.concatenate([w[..., 16:32], w[..., 0:16]], axis=-1)
    none = np.zeros((D, 64), f32)
    rope = np.concatenate([none, kr, kr, none, swap(kr), swap(kr)], axis=1)
    uq = inp["w_uq_2"][0].reshape(-1, HEADS, 96)
    uq = np.concatenate([uq, swap(uq[..., 64:96])], axis=-1).reshape(-1, HEADS * P)
    ukv = inp["w_ukv_2"][0].reshape(-1, HEADS, P)
    uk = np.concatenate([ukv[..., 0:64], np.zeros_like(ukv[..., 0:64])], axis=-1).reshape(-1, HEADS * P)
    uv = ukv[..., 64:128].reshape(-1, HEADS * 64)
    ups, downs = inp["w_up_2"], inp["w_down_2"]
    widen = lambda w: np.pad(w, ((0, 0), (0, P - w.shape[1])))
    down = inp["w_ffn_down"][0]
    n_up, n_in = 2 * F_TILES * P, F_TILES * P

    halves = lambda w: (w[:D // 2], w[D // 2:])

    def mlp(l):
        return [ups[l][:, :n_in], downs[l][:n_in], ups[l][:, n_in:], downs[l][n_in:]]

    weights = [widen(dt), xbc, ly, lx, z, g[:, :D], inp["w_proj_ssm"][0], g[:, D:], inp["w_proj_lru"][0], inp["w_out"][0],
               up[:, :n_up], down[:n_in], up[:, n_up:], down[n_in:], widen(fa), qa, ka, va, qb, kb, vb,
               *halves(inp["w_out_ab_2"][0]), *mlp(0), cq, ckv, qc, kc, vc, rope, uq, uk, uv, *halves(inp["w_out_cd_2"][0]), *mlp(1)]
    for w, (name, count, depth) in zip(weights, LAYERS, strict=True):
        assert w.size == depth * P * count * P, (name, w.shape)
    stream = np.concatenate([value_blocks(w) if name in VALUES else blocks(w) for w, (name, _, _) in zip(weights, LAYERS)])
    assert len(stream) == SLABS * BLOCKS
    stream = stream.reshape(SLABS, BLOCKS, P, P).transpose(0, 2, 1, 3).reshape(SLABS, P, BLOCKS * P)

    consts = np.zeros((P, NCOL), f32)

    def put(name, v, row=0):
        consts[row:row + v.shape[0], COL[name]:COL[name] + v.shape[1]] = v

    def taps(w):
        return w.reshape(len(w), -1, P).transpose(2, 1, 0).reshape(P, -1)

    by_turns = lambda v: v.reshape(-1, 2, FFN_PAIRS, P).transpose(0, 2, 1, 3).reshape(len(v), -1)
    put("mix_pre", features(inp["mix_pre_norm"]))
    put("mix_post", features(inp["mix_post_norm"]))
    put("xbc_w", taps(inp["ssm_conv_w"][0]))
    put("xbc_b", features(inp["ssm_conv_b"]))
    put("skip", features(np.repeat(inp["ssm_d"][0], 64)))
    put("ssm_norm", features(inp["ssm_norm"]))
    put("lx_w", taps(inp["lru_conv_w"][0]))
    put("lx_b", features(inp["lru_conv_b"]))
    put("br", features(inp["lru_br"]))
    put("bi", features(inp["lru_bi"]))
    put("lam", features(inp["lru_lambda"]))
    put("gate_b", features(inp["gate_b"]))
    put("ffn_pre", features(inp["ffn_pre_norm"]))
    put("ffn_post", features(inp["ffn_post_norm"]))
    put("ffn_w", taps(by_turns(inp["ffn_conv_w"][0])))
    put("ffn_b", features(by_turns(inp["ffn_conv_b"])))
    put("mix2", features(inp["norm_mix_2"]))
    put("mlp2", features(inp["norm_mlp_2"]))
    put("final", features(inp["norm_final_2"]))
    put("q_norm", features(inp["q_norm_2"]))
    put("kv_norm", features(inp["kv_norm_2"]))
    put("dt_bias", inp["ssm_dt_bias"].T)
    put("a_log", inp["ssm_a_log"].T)
    put("b_forget", inp["b_forget_2"].T)
    half = 16
    inv_freq = (f32(10000.0) ** (-np.arange(half, dtype=f32) / f32(half))).astype(f32)
    put("inv_freq", np.tile(inv_freq, 4)[:, None], 64)
    put("rope_sign", np.tile(np.repeat(np.array([-1, 1], f32), half), 2)[:, None], 64)

    q, k = np.arange(P)[:, None], np.arange(P)[None, :]
    rel = np.concatenate([q - k, q + P - k, q - k], axis=1) + CHUNK - 1
    rel = inp["rel_bias_2"][0][:, np.clip(rel, 0, N_REL - 1)].transpose(1, 0, 2)

    diag = lambda w: w.reshape(KD, 2, 64, 64).transpose(1, 2, 0, 3)
    arrays = dict(
        x_t=inp["x"][0].T.reshape(KD, P, T).transpose(1, 0, 2), consts=consts, positions=inp["positions_2"].astype(np.int32),
        stream=stream, lru_r=diag(inp["lru_wr"][0]), lru_i=diag(inp["lru_wi"][0]), rel=rel)
    nc = bacc.Bacc("TRN2", target_bir_lowering=False, num_devices=1)
    arrays = {n: np.ascontiguousarray(v) for n, v in arrays.items()}
    aps = {n: nc.dram_tensor(f"in_{n}", v.shape, mybir.dt.from_np(v.dtype), kind="ExternalInput").ap() for n, v in arrays.items()}
    out = nc.dram_tensor("out_t", (P, KD, T), mybir.dt.float32, kind="ExternalOutput").ap()
    build(nc, out_t=out, **aps)
    r = run_bass_kernel_spmd(nc, [{f"in_{n}": v for n, v in arrays.items()}], core_ids=[0])
    got = r.results[0]["out_t"]
    return np.ascontiguousarray(got.transpose(2, 1, 0).reshape(1, T, D))
```
